# Optimizing a Trainium2 kernel written in Bass

```python
import math
import jax, jax.numpy as jnp
from jax import lax
import numpy as np

D_MODEL = 1024
BATCH = 1
SEQ = 256
DEPTH = 2

CTX_LEN = 256
GRID_W = 64
N_EVEN = (DEPTH + 1) // 2
N_ODD = DEPTH // 2

A_GROUPS = 4
A_GROUP_DIM = 128
A_WIDTH = A_GROUPS * A_GROUP_DIM
A_CHUNK = 128
B_HEADS = 4
B_HEAD_DIM = 128
B_WIDTH = B_HEADS * B_HEAD_DIM
B_CONV = 3
GDN_CHUNK = 64
AB_SPLITS = (A_WIDTH, 2 * A_WIDTH, 2 * A_WIDTH + 3 * B_WIDTH, 2 * A_WIDTH + 4 * B_WIDTH,
             2 * A_WIDTH + 4 * B_WIDTH + 2 * B_HEADS)
AB_IN = 2 * A_WIDTH + 4 * B_WIDTH + 4 * B_HEADS
AB_MIX = A_WIDTH + B_WIDTH
C_HEADS = 8
C_NOPE = 128
C_ROPE = 64
C_VDIM = 128
C_Q_LORA = 384
C_KV_LORA = 256
C_IN = C_Q_LORA + C_KV_LORA + C_ROPE
Q_BLOCK = 128
ROPE_THETA = 10000.0
D_FF = 2816
FFN_CONV = 3
EPS = 1e-6


def rms_norm(x, g):
    xf = x.astype(jnp.float32)
    y = xf * lax.rsqrt(jnp.mean(xf * xf, axis=-1, keepdims=True) + EPS)
    return (y * g.astype(jnp.float32)).astype(x.dtype)

def layer_norm(x, g, b):
    xf = x.astype(jnp.float32)
    mu = jnp.mean(xf, axis=-1, keepdims=True)
    var = jnp.mean(jnp.square(xf - mu), axis=-1, keepdims=True)
    y = (xf - mu) * lax.rsqrt(var + EPS) * g.astype(jnp.float32) + b.astype(jnp.float32)
    return y.astype(x.dtype)

def modulate(h, shift, scale):
    return h * (1 + scale) + shift

def ada_mod(cond, w, b):
    m = (jax.nn.silu(cond) @ w + b)[..., None, :]
    return jnp.split(m, 6, axis=-1)

def dwconv(x, w):
    k = w.shape[0]
    return lax.conv_general_dilated(x, w[:, None, :], (1,), [(k // 2, k // 2)],
                                    dimension_numbers=('NWC', 'WIO', 'NWC'),
                                    feature_group_count=x.shape[-1])

def axial_rope(n, rot_dim):
    rows = n // GRID_W
    row = jnp.repeat(jnp.arange(rows, dtype=jnp.float32), GRID_W)
    col = jnp.tile(jnp.arange(GRID_W, dtype=jnp.float32), rows)
    n_freq = rot_dim // 4
    inv = ROPE_THETA ** (-jnp.arange(n_freq, dtype=jnp.float32) / n_freq)
    ang = jnp.concatenate([row[:, None] * inv, col[:, None] * inv], axis=-1)
    return jnp.cos(ang), jnp.sin(ang)

def apply_rope(x, cos, sin):
    h = x.shape[-1] // 2
    x1, x2 = x[..., :h], x[..., h:]
    cos = cos.astype(x.dtype)
    sin = sin.astype(x.dtype)
    return jnp.concatenate([x1 * cos - x2 * sin, x2 * cos + x1 * sin], axis=-1)

def chunk_gmlp(u, v, ln_g, ln_b, ws, bs):
    u = jax.nn.gelu(u, approximate=False)
    v = layer_norm(jax.nn.gelu(v, approximate=False), ln_g, ln_b)
    bn, l, _ = v.shape
    vc = v.reshape(bn, l // A_CHUNK, A_CHUNK, A_GROUPS, A_GROUP_DIM)
    s = jnp.einsum('gij,bnjgd->bnigd', ws, vc) + bs.T[None, None, :, :, None]
    return u * s.reshape(bn, l, A_WIDTH)

def gdn_chunked(q, k, v, g, beta, s0):
    bn, l, h, dk = q.shape
    cs = GDN_CHUNK
    n = l // cs
    to_c = lambda t: t.reshape(bn, n, cs, h, t.shape[-1]).transpose(1, 0, 3, 2, 4)
    qc, kc, vc = to_c(q), to_c(k), to_c(v)
    gc = g.reshape(bn, n, cs, h).transpose(1, 0, 3, 2)
    bc = beta.reshape(bn, n, cs, h).transpose(1, 0, 3, 2)
    gcum = jnp.cumsum(gc, axis=-1)
    tri_incl = jnp.tril(jnp.ones((cs, cs), bool))
    tri_strict = jnp.tril(jnp.ones((cs, cs), bool), -1)
    diff = gcum[..., :, None] - gcum[..., None, :]
    decay = jnp.exp(jnp.where(tri_incl, diff, -jnp.inf))
    kb = kc * bc[..., None]
    vb = vc * bc[..., None]
    a_mat = jnp.where(tri_strict, jnp.einsum('nbhid,nbhjd->nbhij', kb, kc) * decay, 0.0)
    eye = jnp.eye(cs, dtype=jnp.float32)
    t_mat = lax.linalg.triangular_solve(eye + a_mat, jnp.broadcast_to(eye, a_mat.shape),
                                        left_side=True, lower=True, unit_diagonal=True)
    u = jnp.einsum('nbhij,nbhjd->nbhid', t_mat, vb)
    w = jnp.einsum('nbhij,nbhjd->nbhid', t_mat, kb * jnp.exp(gcum)[..., None])
    attn = jnp.einsum('nbhid,nbhjd->nbhij', qc, kc) * decay
    qg = qc * jnp.exp(gcum)[..., None]
    kdec = kc * jnp.exp(gcum[..., -1:] - gcum)[..., None]
    gend = jnp.exp(gcum[..., -1])

    def step(s, xs):
        u_i, w_i, qg_i, kd_i, at_i, ge_i = xs
        v_new = u_i - jnp.einsum('bhck,bhkv->bhcv', w_i, s)
        o_i = jnp.einsum('bhck,bhkv->bhcv', qg_i, s) + jnp.einsum('bhij,bhjv->bhiv', at_i, v_new)
        s = s * ge_i[..., None, None] + jnp.einsum('bhck,bhcv->bhkv', kd_i, v_new)
        return s, o_i

    s_fin, o = lax.scan(step, s0, (u, w, qg, kdec, attn, gend))
    o = o.transpose(1, 0, 3, 2, 4).reshape(bn, l, h, v.shape[-1])
    return o, s_fin

def gated_deltanet(qkv, gate, alpha_raw, beta_raw, conv_w, a_log, dt_bias, norm_g, s0_pair):
    bn, l, _ = qkv.shape
    hq = jax.nn.silu(dwconv(qkv, conv_w)).astype(jnp.float32)
    q, k, v = jnp.split(hq, 3, axis=-1)
    l2 = lambda t: t * lax.rsqrt(jnp.sum(t * t, axis=-1, keepdims=True) + EPS)
    q = l2(q.reshape(bn, l, B_HEADS, B_HEAD_DIM)) * (B_HEAD_DIM ** -0.5)
    k = l2(k.reshape(bn, l, B_HEADS, B_HEAD_DIM))
    v = v.reshape(bn, l, B_HEADS, B_HEAD_DIM)
    a = alpha_raw.astype(jnp.float32).reshape(bn, l, 2, B_HEADS)
    beta = jax.nn.sigmoid(beta_raw.astype(jnp.float32).reshape(bn, l, 2, B_HEADS))
    log_alpha = -jnp.exp(a_log.astype(jnp.float32)) * jax.nn.softplus(a + dt_bias.astype(jnp.float32))
    o_f, s_f = gdn_chunked(q, k, v, log_alpha[:, :, 0], beta[:, :, 0], s0_pair[0])
    flip = lambda t: jnp.flip(t, axis=1)
    o_b, s_b = gdn_chunked(flip(q), flip(k), flip(v), flip(log_alpha[:, :, 1]), flip(beta[:, :, 1]), s0_pair[1])
    o = o_f + flip(o_b)
    o = rms_norm(o, norm_g) * jax.nn.silu(gate.astype(jnp.float32).reshape(bn, l, B_HEADS, B_HEAD_DIM))
    return o.reshape(bn, l, B_WIDTH).astype(qkv.dtype), (s_f, s_b)

def ab_mixer(h_ctx, h_lat, w_in, a_ln_g, a_ln_b, a_ws, a_bs, conv_w, a_log, dt_bias, norm_g, w_out,
             need_ctx_out):
    def run(h, state0, want_out):
        a_u, a_v, qkv, gate, alpha_raw, beta_raw = jnp.split(h @ w_in, AB_SPLITS, axis=-1)
        y_b, state = gated_deltanet(qkv, gate, alpha_raw, beta_raw, conv_w, a_log, dt_bias, norm_g, state0)
        if not want_out:
            return None, state
        y_a = chunk_gmlp(a_u, a_v, a_ln_g, a_ln_b, a_ws, a_bs)
        return jnp.concatenate([y_a, y_b], axis=-1) @ w_out, state

    zero = jnp.zeros((h_ctx.shape[0], B_HEADS, B_HEAD_DIM, B_HEAD_DIM), jnp.float32)
    y_ctx, ctx_state = run(h_ctx, (zero, zero), need_ctx_out)
    y_lat, _ = run(h_lat, ctx_state, True)
    return y_ctx, y_lat

def block_attention(qn, qr, kn, kr, v):
    bn, l, h, _ = qn.shape
    nb = l // Q_BLOCK
    scale = (C_NOPE + C_ROPE) ** -0.5
    blocks = lambda t: t.reshape(bn, nb, Q_BLOCK, h, t.shape[-1]).transpose(1, 0, 2, 3, 4)

    def one(blk):
        qn_b, qr_b = blk
        s = jnp.einsum('bqhd,bkhd->bhqk', qn_b, kn) + jnp.einsum('bqhd,bkd->bhqk', qr_b, kr)
        p = jax.nn.softmax(s.astype(jnp.float32) * scale, axis=-1).astype(v.dtype)
        return jnp.einsum('bhqk,bkhd->bqhd', p, v)

    o = lax.map(one, (blocks(qn), blocks(qr)))
    return o.transpose(1, 0, 2, 3, 4).reshape(bn, l, h * v.shape[-1])

def mla_mixer(h_ctx, h_lat, w_in, q_norm_g, kv_norm_g, w_uq, w_ukv, w_out, need_ctx_out):
    n_lat = h_lat.shape[1]
    cos, sin = axial_rope(n_lat, C_ROPE)
    rot_q = lambda t: apply_rope(t, cos[:, None, :], sin[:, None, :])
    rot_k = lambda t: apply_rope(t, cos, sin)
    no_rot = lambda t: t

    def queries(cq, rot):
        bn, l, _ = cq.shape
        q = (rms_norm(cq, q_norm_g) @ w_uq).reshape(bn, l, C_HEADS, C_NOPE + C_ROPE)
        return q[..., :C_NOPE], rot(q[..., C_NOPE:])

    def keys(kv_part, rot):
        bn, l, _ = kv_part.shape
        ckv, kr = jnp.split(kv_part, [C_KV_LORA], axis=-1)
        kv = (rms_norm(ckv, kv_norm_g) @ w_ukv).reshape(bn, l, C_HEADS, C_NOPE + C_VDIM)
        return kv[..., :C_NOPE], rot(kr), kv[..., C_NOPE:]

    z_lat = h_lat @ w_in
    kn_l, kr_l, v_l = keys(z_lat[..., C_Q_LORA:], rot_k)
    qn_l, qr_l = queries(z_lat[..., :C_Q_LORA], rot_q)
    if need_ctx_out:
        z_ctx = h_ctx @ w_in
        kv_ctx = z_ctx[..., C_Q_LORA:]
    else:
        kv_ctx = h_ctx @ w_in[:, C_Q_LORA:]
    kn_c, kr_c, v_c = keys(kv_ctx, no_rot)
    kn = jnp.concatenate([kn_c, kn_l], axis=1)
    kr = jnp.concatenate([kr_c, kr_l], axis=1)
    v = jnp.concatenate([v_c, v_l], axis=1)
    y_lat = block_attention(qn_l, qr_l, kn, kr, v) @ w_out
    y_ctx = None
    if need_ctx_out:
        qn_c, qr_c = queries(z_ctx[..., :C_Q_LORA], no_rot)
        y_ctx = block_attention(qn_c, qr_c, kn_c, kr_c, v_c) @ w_out
    return y_ctx, y_lat

def conv_ffn(h, w_up, conv_w, w_down):
    g, u = jnp.split(dwconv(h @ w_up, conv_w), 2, axis=-1)
    return (jax.nn.silu(g) * u) @ w_down

def first_inputs(seed: int = 0) -> dict:
    key = jax.random.key(seed)
    ks = iter(jax.random.split(key, 32))
    nrm = lambda shape, s: jax.random.normal(next(ks), shape, jnp.float32) * s
    gain = lambda shape: 1.0 + nrm(shape, 0.02)
    d = D_MODEL
    a_log = jnp.log(jax.random.uniform(next(ks), (N_EVEN, 2, B_HEADS), jnp.float32, 1.0, 16.0))
    dt = jnp.exp(jax.random.uniform(next(ks), (N_EVEN, 2, B_HEADS), jnp.float32,
                                    math.log(1e-3), math.log(1e-1)))
    dt_bias = dt + jnp.log(-jnp.expm1(-dt))
    return {
        'x': nrm((BATCH, SEQ, d), 1.0),
        'c': nrm((BATCH, d), 1.0),
        'ctx': nrm((BATCH, CTX_LEN, d), 1.0),
        'c_ctx': nrm((d,), 1.0),
        'ada_w': nrm((DEPTH, d, 6 * d), d ** -0.5),
        'ada_b': nrm((DEPTH, 6 * d), 0.01),
        'norm1_g': gain((DEPTH, d)),
        'norm2_g': gain((DEPTH, d)),
        'ab_w_in': nrm((N_EVEN, d, AB_IN), d ** -0.5),
        'a_ln_g': gain((N_EVEN, A_WIDTH)),
        'a_ln_b': nrm((N_EVEN, A_WIDTH), 0.01),
        'a_ws': nrm((N_EVEN, A_GROUPS, A_CHUNK, A_CHUNK), 0.5 * A_CHUNK ** -0.5),
        'a_bs': 1.0 + nrm((N_EVEN, A_GROUPS, A_CHUNK), 0.1),
        'b_conv_w': nrm((N_EVEN, B_CONV, 3 * B_WIDTH), B_CONV ** -0.5),
        'b_a_log': a_log,
        'b_dt_bias': dt_bias,
        'b_norm_g': gain((N_EVEN, B_HEAD_DIM)),
        'ab_w_out': nrm((N_EVEN, AB_MIX, d), AB_MIX ** -0.5),
        'mla_w_in': nrm((N_ODD, d, C_IN), d ** -0.5),
        'mla_q_norm_g': gain((N_ODD, C_Q_LORA)),
        'mla_kv_norm_g': gain((N_ODD, C_KV_LORA)),
        'mla_w_uq': nrm((N_ODD, C_Q_LORA, C_HEADS * (C_NOPE + C_ROPE)), C_Q_LORA ** -0.5),
        'mla_w_ukv': nrm((N_ODD, C_KV_LORA, C_HEADS * (C_NOPE + C_VDIM)), C_KV_LORA ** -0.5),
        'mla_w_out': nrm((N_ODD, C_HEADS * C_VDIM, d), (C_HEADS * C_VDIM) ** -0.5),
        'ffn_w_up': nrm((DEPTH, d, 2 * D_FF), d ** -0.5),
        'ffn_conv_w': nrm((DEPTH, FFN_CONV, 2 * D_FF), FFN_CONV ** -0.5),
        'ffn_w_down': nrm((DEPTH, D_FF, d), D_FF ** -0.5),
        'final_g': gain((d,)),
    }

def first_block(x, c, ctx, c_ctx, ada_w, ada_b, norm1_g, norm2_g, ab_w_in, a_ln_g, a_ln_b, a_ws, a_bs,
              b_conv_w, b_a_log, b_dt_bias, b_norm_g, ab_w_out, mla_w_in, mla_q_norm_g, mla_kv_norm_g,
              mla_w_uq, mla_w_ukv, mla_w_out, ffn_w_up, ffn_conv_w, ffn_w_down, final_g):
    lat, cx = x, ctx
    for i in range(DEPTH):
        last = i == DEPTH - 1
        j = i // 2
        sh1, sc1, g1, sh2, sc2, g2 = ada_mod(c, ada_w[i], ada_b[i])
        csh1, csc1, cg1, csh2, csc2, cg2 = ada_mod(c_ctx, ada_w[i], ada_b[i])
        h_lat = modulate(rms_norm(lat, norm1_g[i]), sh1, sc1)
        h_ctx = modulate(rms_norm(cx, norm1_g[i]), csh1, csc1)
        if i % 2 == 0:
            y_ctx, y_lat = ab_mixer(h_ctx, h_lat, ab_w_in[j], a_ln_g[j], a_ln_b[j], a_ws[j], a_bs[j],
                                    b_conv_w[j], b_a_log[j], b_dt_bias[j], b_norm_g[j], ab_w_out[j],
                                    not last)
        else:
            y_ctx, y_lat = mla_mixer(h_ctx, h_lat, mla_w_in[j], mla_q_norm_g[j], mla_kv_norm_g[j],
                                     mla_w_uq[j], mla_w_ukv[j], mla_w_out[j], not last)
        lat = lat + g1 * y_lat
        lat = lat + g2 * conv_ffn(modulate(rms_norm(lat, norm2_g[i]), sh2, sc2),
                                  ffn_w_up[i], ffn_conv_w[i], ffn_w_down[i])
        if not last:
            cx = cx + cg1 * y_ctx
            cx = cx + cg2 * conv_ffn(modulate(rms_norm(cx, norm2_g[i]), csh2, csc2),
                                     ffn_w_up[i], ffn_conv_w[i], ffn_w_down[i])
    return rms_norm(lat, final_g)


DEPTH_2 = 1

HEAD_DIM = 64
MIX_WIDTH = D_MODEL
N_HEADS_A = (MIX_WIDTH // 2) // HEAD_DIM
N_HEADS_B = (MIX_WIDTH // 2) // HEAD_DIM
D_NOPE = HEAD_DIM
D_ROPE = HEAD_DIM // 2
KV_RANK = 2 * HEAD_DIM
V_DIM = HEAD_DIM
IDX_HEADS = 8
IDX_DIM = HEAD_DIM
TOPK_MAX = 256
DILATED_PATTERNS = ((128, 1), (512, 4), (2048, 16))
CROSS_HEADS = 4
CROSS_HEAD_DIM = D_MODEL // CROSS_HEADS
MEM_TOKENS = 256
D_FF_2 = 4 * D_MODEL
NORM_EPS = 1e-6

IN_SIZES = (N_HEADS_A * D_NOPE,
            N_HEADS_A * D_ROPE,
            KV_RANK,
            D_ROPE,
            IDX_HEADS * IDX_DIM,
            IDX_DIM,
            IDX_HEADS,
            3 * N_HEADS_B * HEAD_DIM)
IN_COLS = 512 + 256 + 128 + 32 + 512 + 64 + 8 + 1536 if D_MODEL == 1024 else int(np.sum(IN_SIZES))


def rmsnorm(x, g):
    xf = x.astype(jnp.float32)
    y = xf * lax.rsqrt(jnp.mean(xf * xf, axis=-1, keepdims=True) + NORM_EPS)
    return (y * g.astype(jnp.float32)).astype(x.dtype)

def rope(x):
    S, d = x.shape[1], x.shape[-1]
    inv = ROPE_THETA ** (-jnp.arange(0, d, 2, dtype=jnp.float32) / d)
    ang = jnp.arange(S, dtype=jnp.float32)[:, None] * inv[None, :]
    cos = jnp.cos(ang)[None, :, None, :].astype(x.dtype)
    sin = jnp.sin(ang)[None, :, None, :].astype(x.dtype)
    x1, x2 = jnp.split(x, 2, axis=-1)
    return jnp.concatenate([x1 * cos - x2 * sin, x2 * cos + x1 * sin], axis=-1)

def dsa_sparse_attention(q_nope, q_rope, c_kv, k_rope, q_idx, k_idx, w_idx, w_uk, w_uv):
    B, S = q_nope.shape[0], q_nope.shape[1]
    topk = min(TOPK_MAX, S // 4)
    nb = S // Q_BLOCK
    scale = (D_NOPE + D_ROPE) ** -0.5
    q_lat = jnp.einsum('bshn,hnc->bshc', q_nope, w_uk)
    w_eff = w_idx.astype(jnp.float32) * (IDX_HEADS ** -0.5) * (IDX_DIM ** -0.5)
    key_pos = jnp.arange(S)
    gather = jax.vmap(lambda table, ix: table[ix])

    def to_blocks(a):
        return jnp.moveaxis(a.reshape((B, nb, Q_BLOCK) + a.shape[2:]), 1, 0)

    def block(args):
        ql, qr, qi, wi, blk = args
        q_pos = blk * Q_BLOCK + jnp.arange(Q_BLOCK)
        causal = key_pos[None, :] <= q_pos[:, None]
        logits = jnp.einsum('bqhd,bsd->bhqs', qi, k_idx).astype(jnp.float32)
        index = jnp.einsum('bhqs,bqh->bqs', jax.nn.relu(logits), wi)
        index = jnp.where(causal[None], index, -jnp.inf)
        _, sel = lax.top_k(index, topk)
        valid = sel <= q_pos[None, :, None]
        c_sel = gather(c_kv, sel)
        r_sel = gather(k_rope, sel)
        s = (jnp.einsum('bqhc,bqkc->bhqk', ql, c_sel)
             + jnp.einsum('bqhr,bqkr->bhqk', qr, r_sel)).astype(jnp.float32) * scale
        s = jnp.where(valid[:, None], s, -jnp.inf)
        p = jax.nn.softmax(s, axis=-1).astype(c_sel.dtype)
        return jnp.einsum('bhqk,bqkc->bqhc', p, c_sel)

    o_lat = lax.map(block, (to_blocks(q_lat), to_blocks(q_rope), to_blocks(q_idx),
                            to_blocks(w_eff), jnp.arange(nb)))
    o_lat = jnp.moveaxis(o_lat, 0, 1).reshape(B, S, N_HEADS_A, KV_RANK)
    return jnp.einsum('bshc,hcv->bshv', o_lat, w_uv)

def dilated_pattern(q, k, v, window, dilation):
    B, H, S, d = q.shape
    n = S // dilation
    w_sub = window // dilation
    nb = -(-n // Q_BLOCK)
    pad = nb * Q_BLOCK - n

    def split(a):
        a = a.reshape(B, H, n, dilation, d).transpose(0, 1, 3, 2, 4)
        a = jnp.pad(a, ((0, 0), (0, 0), (0, 0), (0, pad), (0, 0)))
        return a.reshape(B, H, dilation, nb, Q_BLOCK, d)

    def with_prev(a):
        prev = jnp.concatenate([jnp.zeros_like(a[:, :, :, :1]), a[:, :, :, :-1]], axis=3)
        return jnp.concatenate([prev, a], axis=4)

    qb = split(q)
    kk = with_prev(split(k))
    vv = with_prev(split(v))
    s = jnp.einsum('bhrnqd,bhrnkd->bhrnqk', qb, kk).astype(jnp.float32) * (d ** -0.5)
    rel = (jnp.arange(Q_BLOCK)[:, None] + Q_BLOCK) - jnp.arange(2 * Q_BLOCK)[None, :]
    band = (rel >= 0) & (rel <= w_sub)
    has_prev = (jnp.arange(nb)[:, None, None] > 0) | (jnp.arange(2 * Q_BLOCK)[None, None, :] >= Q_BLOCK)
    mask = band[None] & has_prev
    s = jnp.where(mask, s, -jnp.inf)
    lse = jax.nn.logsumexp(s, axis=-1)
    p = jnp.exp(s - lse[..., None]).astype(v.dtype)
    o = jnp.einsum('bhrnqk,bhrnkd->bhrnqd', p, vv)

    def merge(a, tail):
        a = a.reshape((B, H, dilation, nb * Q_BLOCK) + tail)[:, :, :, :n]
        return jnp.swapaxes(a, 2, 3).reshape((B, H, S) + tail)

    return merge(o, (d,)), merge(lse, ())

def dilated_attention(q, k, v):
    outs, lses = [], []
    for window, dilation in DILATED_PATTERNS:
        o, l = dilated_pattern(q, k, v, window, dilation)
        outs.append(o)
        lses.append(l)
    alpha = jax.nn.softmax(jnp.stack(lses, axis=0), axis=0).astype(q.dtype)
    return jnp.sum(alpha[..., None] * jnp.stack(outs, axis=0), axis=0)

def second_inputs(seed: int = 0) -> dict:
    key = jax.random.key(seed)
    ks = jax.random.split(key, 20)
    f32 = jnp.float32

    def w(k, shape, fan_in):
        return jax.random.normal(k, shape, f32) * (fan_in ** -0.5)

    def gain(k, shape):
        return 1.0 + 0.02 * jax.random.normal(k, shape, f32)

    L = DEPTH_2
    return {
        "x": jax.random.normal(ks[0], (BATCH, SEQ, D_MODEL), f32),
        "mem": jax.random.normal(ks[1], (BATCH, MEM_TOKENS, D_MODEL), f32),
        "norm_mix_g": gain(ks[2], (L, D_MODEL)),
        "w_in": w(ks[3], (L, D_MODEL, IN_COLS), D_MODEL),
        "kv_norm_g": gain(ks[4], (L, KV_RANK)),
        "w_uk": w(ks[5], (L, N_HEADS_A, D_NOPE, KV_RANK), D_NOPE),
        "w_uv": w(ks[6], (L, N_HEADS_A, KV_RANK, V_DIM), KV_RANK),
        "w_out": w(ks[7], (L, N_HEADS_A * V_DIM + N_HEADS_B * HEAD_DIM, D_MODEL), MIX_WIDTH),
        "norm_cross_g": gain(ks[8], (L, D_MODEL)),
        "norm_mem_g": gain(ks[9], (L, D_MODEL)),
        "w_q_cross": w(ks[10], (L, D_MODEL, CROSS_HEADS * CROSS_HEAD_DIM), D_MODEL),
        "w_kv_cross": w(ks[11], (L, D_MODEL, 2 * CROSS_HEADS * CROSS_HEAD_DIM), D_MODEL),
        "w_o_cross": w(ks[12], (L, CROSS_HEADS * CROSS_HEAD_DIM, D_MODEL), CROSS_HEADS * CROSS_HEAD_DIM),
        "norm_mlp_g": gain(ks[13], (L, D_MODEL)),
        "w_up": w(ks[14], (L, D_MODEL, D_FF_2), D_MODEL),
        "w_down": w(ks[15], (L, D_FF_2, D_MODEL), D_FF_2),
        "norm_final_g": gain(ks[16], (D_MODEL,)),
    }

def second_block(x, mem, norm_mix_g, w_in, kv_norm_g, w_uk, w_uv, w_out, norm_cross_g, norm_mem_g,
              w_q_cross, w_kv_cross, w_o_cross, norm_mlp_g, w_up, w_down, norm_final_g):
    B, S, _ = x.shape
    M = mem.shape[1]
    split_at = [int(c) for c in np.cumsum(IN_SIZES)[:-1]]
    for l in range(DEPTH_2):
        h = rmsnorm(x, norm_mix_g[l])
        proj = h @ w_in[l]
        p_qn, p_qr, p_ckv, p_kr, p_qi, p_ki, p_wi, p_qkv = jnp.split(proj, split_at, axis=-1)
        q_nope = p_qn.reshape(B, S, N_HEADS_A, D_NOPE)
        q_rope = rope(p_qr.reshape(B, S, N_HEADS_A, D_ROPE))
        c_kv = rmsnorm(p_ckv, kv_norm_g[l])
        k_rope = rope(p_kr[:, :, None, :])[:, :, 0]
        q_idx = rope(p_qi.reshape(B, S, IDX_HEADS, IDX_DIM))
        k_idx = rope(p_ki[:, :, None, :])[:, :, 0]
        o_a = dsa_sparse_attention(q_nope, q_rope, c_kv, k_rope, q_idx, k_idx, p_wi, w_uk[l], w_uv[l])
        qkv = p_qkv.reshape(B, S, 3, N_HEADS_B, HEAD_DIM)
        q_b = rope(qkv[:, :, 0]).transpose(0, 2, 1, 3)
        k_b = rope(qkv[:, :, 1]).transpose(0, 2, 1, 3)
        v_b = qkv[:, :, 2].transpose(0, 2, 1, 3)
        o_b = dilated_attention(q_b, k_b, v_b).transpose(0, 2, 1, 3)
        heads = jnp.concatenate([o_a.reshape(B, S, N_HEADS_A * V_DIM),
                                 o_b.reshape(B, S, N_HEADS_B * HEAD_DIM)], axis=-1)
        x = x + heads @ w_out[l]
        hc = rmsnorm(x, norm_cross_g[l])
        m = rmsnorm(mem, norm_mem_g[l])
        qc = (hc @ w_q_cross[l]).reshape(B, S, CROSS_HEADS, CROSS_HEAD_DIM)
        kvc = (m @ w_kv_cross[l]).reshape(B, M, 2, CROSS_HEADS, CROSS_HEAD_DIM)
        sc = jnp.einsum('bshd,bmhd->bhsm', qc, kvc[:, :, 0]).astype(jnp.float32) * (CROSS_HEAD_DIM ** -0.5)
        pc = jax.nn.softmax(sc, axis=-1).astype(x.dtype)
        oc = jnp.einsum('bhsm,bmhd->bshd', pc, kvc[:, :, 1]).reshape(B, S, CROSS_HEADS * CROSS_HEAD_DIM)
        x = x + oc @ w_o_cross[l]
        hm = rmsnorm(x, norm_mlp_g[l])
        x = x + jnp.square(jax.nn.relu(hm @ w_up[l])) @ w_down[l]
    return rmsnorm(x, norm_final_g)


def setup_inputs(seed=0):
    out = dict(first_inputs(seed))
    for name, value in second_inputs(seed + 1).items():
        if name != "x":
            out[name + "_2"] = value
    return out


def reference(
    x, c, ctx, c_ctx, ada_w, ada_b, norm1_g, norm2_g, ab_w_in, a_ln_g, a_ln_b, a_ws, a_bs,
    b_conv_w, b_a_log, b_dt_bias, b_norm_g, ab_w_out, mla_w_in, mla_q_norm_g, mla_kv_norm_g,
    mla_w_uq, mla_w_ukv, mla_w_out, ffn_w_up, ffn_conv_w, ffn_w_down, final_g, mem_2,
    norm_mix_g_2, w_in_2, kv_norm_g_2, w_uk_2, w_uv_2, w_out_2, norm_cross_g_2, norm_mem_g_2,
    w_q_cross_2, w_kv_cross_2, w_o_cross_2, norm_mlp_g_2, w_up_2, w_down_2, norm_final_g_2,
):
    x = first_block(
        x, c, ctx, c_ctx, ada_w, ada_b, norm1_g, norm2_g, ab_w_in, a_ln_g, a_ln_b, a_ws, a_bs,
        b_conv_w, b_a_log, b_dt_bias, b_norm_g, ab_w_out, mla_w_in, mla_q_norm_g, mla_kv_norm_g,
        mla_w_uq, mla_w_ukv, mla_w_out, ffn_w_up, ffn_conv_w, ffn_w_down, final_g,
    )
    return second_block(
        x, mem_2, norm_mix_g_2, w_in_2, kv_norm_g_2, w_uk_2, w_uv_2, w_out_2, norm_cross_g_2,
        norm_mem_g_2, w_q_cross_2, w_kv_cross_2, w_o_cross_2, norm_mlp_g_2, w_up_2, w_down_2,
        norm_final_g_2,
    )


_drawn_inputs = setup_inputs


def setup_inputs(seed=0):
    import zlib

    import numpy as np

    out = dict(_drawn_inputs(seed))
    spreads = {}
    factors = {'a_ln_g': 5.429,
     'a_ln_b': 7.828,
     'b_norm_g': 3.759,
     'mla_q_norm_g': 8.0,
     'mla_kv_norm_g': 4.925,
     'kv_norm_g_2': 8.0,
     'norm_cross_g_2': 8.0,
     'norm_mem_g_2': 8.0,
     'norm_mlp_g_2': 9.67,
     'norm_final_g_2': 7.434}
    for name, (base, spread) in spreads.items():
        noise = np.random.default_rng([zlib.crc32(name.encode()), seed]).standard_normal(out[name].shape)
        drawn = base * np.exp(spread * noise) if base else spread * noise
        out[name] = __import__('jax').numpy.asarray(drawn.astype(out[name].dtype))
    for name, factor in factors.items():
        out[name] = (out[name] * factor).astype(out[name].dtype)
    return out
```

```python
from contextlib import ExitStack

import concourse.bass as bass
from concourse import mybir

P = 128
D = 1024
KC = D // P
SEQ = 256
T2 = 2 * SEQ
D_FF = 2816
FC = D_FF // P
D_FF_2 = 4096
HEADS = 4
EPS = 1e-6
NEG = -1e30
TAKEN = -3e38
BLOCK_CHUNKS = 8
BLOCK = BLOCK_CHUNKS * P

COLS = [("cond", 2 * KC), ("ada_b", 96), ("norm1", 16), ("norm2", 16), ("bconv", 36), ("dt_bias", 1), ("a_log", 1),
        ("a_ln_g", 4), ("a_ln_b", 4), ("b_norm", 1), ("mla_q", 3), ("mla_kv", 2), ("fconv", 2 * 2 * FC * 3),
        ("final1", 8), ("mix", 8), ("kv2", 1), ("cross", 8), ("mem", 8), ("mlp", 8), ("final2", 8), ("eps", 1), ("one", 1)]
COL_AT = {}
_n = 0
for _name, _w in COLS:
    COL_AT[_name] = _n
    _n += _w
NCOLS = _n

GDN_TABLES = [("cum", 2 * P), ("blk", P), ("neg", 2 * P), ("lev", 12 * P)]
LATE_TABLES = [("perm64", P), ("perm32", P), ("cm", SEQ), ("sm", SEQ), ("c64", SEQ), ("s64", SEQ), ("c32", SEQ),
               ("s32", SEQ), ("causal", 2 * SEQ), ("dneg", 2 * SEQ), ("dcnt", 2 * SEQ)]
GDN_AT, LATE_AT = {}, {}
_n = 0
for _name, _w in GDN_TABLES:
    GDN_AT[_name] = _n
    _n += _w
NGDN = _n
_n = 0
for _name, _w in LATE_TABLES:
    LATE_AT[_name] = _n
    _n += _w
NLATE = _n

STAGES = [("in0", 25, 25), ("out0", 8, 8), ("up0", 44, 44), ("dn0", 24, 8), ("in1", 6, 6), ("uq", 5, 12), ("ukv_k", 2, 8),
          ("ukv_v", 2, 8), ("out1", 8, 8), ("up1", 44, 44), ("dn1", 24, 8), ("in2", 22, 22), ("in2_v", 4, 2), ("out2", 8, 8),
          ("xq", 8, 8), ("xk", 8, 8), ("xv", 8, 4), ("xo", 8, 8), ("up2", 32, 32), ("dn2", 32, 8)]
B0, T0 = {}, {}
_b = _t = 0
for _name, _nb, _nt in STAGES:
    B0[_name], T0[_name] = _b, _t
    _b += _nb
    _t += _nt
NBLK = _b

NORMS = [("n1_0", 8, T2), ("n2_0", 8, T2), ("n1_1", 8, T2), ("cq", 3, SEQ), ("ckv", 2, T2), ("n2_1", 8, SEQ), ("final1", 8, SEQ),
         ("mix", 8, SEQ), ("kv2", 1, SEQ), ("cross", 8, SEQ), ("mem", 8, SEQ), ("mlp", 8, SEQ), ("final2", 8, SEQ)]
NORM_I = {n: i for i, (n, _, _) in enumerate(NORMS)}
SPLIT = {"n1_0", "n2_0", "n1_1", "cq", "ckv", "n2_1", "mix", "cross", "mem", "mlp"}
MODULATED = {"n1_0": (0, 0), "n2_0": (0, 3), "n1_1": (1, 0), "n2_1": (1, 3)}
NORM_C0, NORM_S0 = {}, {}
_c = _s = 0
for _name, _nc, _ in NORMS:
    NORM_C0[_name], NORM_S0[_name] = _c, _s
    _c += _nc
    _s += _nc if _name in SPLIT else 0

RES = {n: 8 * i for i, n in enumerate(["out0", "dn0", "out1", "dn1", "out2", "xo", "dn2"])}

A_FIRST = 16
A_ALL = 96


def tables():
    import numpy as np
    f = np.float32
    j, i = np.arange(P)[:, None], np.arange(P)[None, :]
    same = (j // 64) == (i // 64)
    cum = [same & (j <= i), same & (j >= i)]
    lev = []
    for d in range(2):
        for s in (1, 2, 4, 8, 16, 32):
            pair = (j // (2 * s)) == (i // (2 * s))
            lo, hi = (j // s) % 2, (i // s) % 2
            lev.append(pair & ((lo == 0) & (hi == 1) if d == 0 else (lo == 1) & (hi == 0)))
    gdn = np.concatenate([c.astype(f) for c in cum] + [same.astype(f)] + [np.where(c, 0, NEG).astype(f) for c in cum]
                         + [m.astype(f) for m in lev], axis=1)

    def perm(w):
        m = np.zeros((P, P), f)
        p = np.arange(P)
        m[(p // w) * w + (p % w + w // 2) % w, p] = 1
        return m

    def rope(ang, w):
        p = np.arange(P) % w
        c, s = np.cos(ang).astype(f), np.sin(ang).astype(f)
        return c.T[p % (w // 2)], s.T[p % (w // 2)] * np.where(p < w // 2, -1, 1).astype(f)[:, None]

    t = np.arange(SEQ, dtype=f)
    inv = (f(10000.0) ** (-np.arange(16, dtype=f) / f(16))).astype(f)
    cm, sm = rope(np.concatenate([np.floor(t / 64)[:, None] * inv, (t % 64)[:, None] * inv], axis=1), 64)
    inv64 = (f(10000.0) ** (-np.arange(0, 64, 2, dtype=f) / f(64))).astype(f)
    inv32 = (f(10000.0) ** (-np.arange(0, 32, 2, dtype=f) / f(32))).astype(f)
    c64, s64 = rope(t[:, None] * inv64, 64)
    c32, s32 = rope(t[:, None] * inv32, 32)
    q, k = np.arange(SEQ)[:, None], np.arange(SEQ)[None, :]
    back = q - k
    count = sum(((back >= 0) & (back <= w) & (back % dil == 0)).astype(f) for w, dil in ((128, 1), (512, 4), (2048, 16)))

    def rows(m):
        return m.reshape(2, P, SEQ).transpose(1, 0, 2).reshape(P, 2 * SEQ).astype(f)

    late = np.concatenate([perm(64), perm(32), cm, sm, c64, s64, c32, s32, rows(np.where(back >= 0, 0, NEG)),
                           rows(np.where(count > 0, 0, NEG)), rows(count)], axis=1).astype(f)
    return gdn, late


def lay_out(a):
    import numpy as np
    f = np.float32
    z = lambda *s: np.zeros(s, f)
    tr = lambda m: np.ascontiguousarray(m.T.reshape(KC, P, -1).transpose(1, 0, 2))

    def tiles(w, pad=0):
        k, m = w.shape
        b = w.reshape(k // P, P, m // P, P).transpose(2, 1, 0, 3)
        if pad:
            b = np.concatenate([b, z(b.shape[0], P, pad, P)], axis=2)
        return b

    def blocks(w, pad=0):
        b = tiles(w, pad)
        m, _, k, _ = b.shape
        if k >= BLOCK_CHUNKS:
            n = k // BLOCK_CHUNKS
            return b.reshape(m, P, n, BLOCK).transpose(0, 2, 1, 3).reshape(m * n, P, BLOCK)
        b = b.transpose(1, 0, 2, 3).reshape(P, m * k, P)
        n = -(-m * k // BLOCK_CHUNKS)
        b = np.concatenate([b, z(P, n * BLOCK_CHUNKS - m * k, P)], axis=1)
        return b.reshape(P, n, BLOCK).transpose(1, 0, 2)

    def moving(w):
        k, m = w.shape
        b = w.reshape(k // 256, 2, P, m // 512, 512).transpose(3, 0, 2, 1, 4)
        return b.reshape(-1, P, BLOCK)

    def wide(w):
        return np.concatenate([w, z(w.shape[0], -w.shape[1] % P)], axis=1)

    wi = a["ab_w_in"][0]
    ab = z(D, P)
    ab[:, 0:8], ab[:, 32:40] = wi[:, 3072:3080], wi[:, 3080:3088]
    pairs = np.array([[j, FC + j] for j in range(FC)]).ravel()
    ffn_cols = (pairs[:, None] * P + np.arange(P)).ravel()
    uq = a["mla_w_uq"][0].reshape(384, 8, 192)
    ukv = a["mla_w_ukv"][0].reshape(256, 8, 256)
    w2 = a["w_in_2"][0]
    mi = a["mla_w_in"][0]
    kvc = a["w_kv_cross_2"][0]
    w_in2 = np.concatenate([w2[:, 0:896], np.tile(w2[:, 896:928], (1, 4)), np.tile(w2[:, 1440:1504], (1, 2)),
                            wide(w2[:, 1504:1512]), w2[:, 928:1440], w2[:, 1512:2536]], axis=1)
    stream = [blocks(np.concatenate([wi[:, 0:3072], ab], axis=1)), blocks(a["ab_w_out"][0]),
              blocks(a["ffn_w_up"][0][:, ffn_cols]), blocks(a["ffn_w_down"][0], 2),
              blocks(np.concatenate([mi, mi[:, 640:704]], axis=1)),
              blocks(np.concatenate([uq[:, :, :128].reshape(384, -1), uq[:, :, 128:].reshape(384, -1)], axis=1)),
              blocks(np.ascontiguousarray(ukv[:, :, :128]).reshape(256, -1)), moving(np.ascontiguousarray(ukv[:, :, 128:]).reshape(256, -1)),
              blocks(a["mla_w_out"][0]), blocks(a["ffn_w_up"][1][:, ffn_cols]), blocks(a["ffn_w_down"][1], 2),
              blocks(w_in2), moving(w2[:, 2536:3048]), blocks(a["w_out_2"][0]), blocks(a["w_q_cross_2"][0]),
              blocks(kvc[:, :1024]), moving(kvc[:, 1024:]), blocks(a["w_o_cross_2"][0]), blocks(a["w_up_2"][0]), blocks(a["w_down_2"][0])]
    assert [len(s) for s in stream] == [n for _, n, _ in STAGES]
    vec = lambda v: v.reshape(-1, P).T
    dt_bias, a_log = z(P, 1), z(P, 1)
    dt_bias[:8, 0], a_log[:8, 0] = a["b_dt_bias"][0].ravel(), a["b_a_log"][0].ravel()
    cols = [np.stack([vec(a["c_ctx"]), vec(a["c"][0])], axis=2).reshape(P, -1),
            np.concatenate([vec(a["ada_b"][i]) for i in range(2)], axis=1),
            np.concatenate([vec(a["norm1_g"][i]) for i in range(2)], axis=1),
            np.concatenate([vec(a["norm2_g"][i]) for i in range(2)], axis=1),
            a["b_conv_w"][0].reshape(3, 12, P).transpose(2, 1, 0).reshape(P, -1), dt_bias, a_log,
            vec(a["a_ln_g"][0]), vec(a["a_ln_b"][0]), vec(a["b_norm_g"][0]), vec(a["mla_q_norm_g"][0]), vec(a["mla_kv_norm_g"][0]),
            np.concatenate([a["ffn_conv_w"][i][:, ffn_cols].reshape(3, 2 * FC, P).transpose(2, 1, 0).reshape(P, -1) for i in range(2)], axis=1),
            vec(a["final_g"]), vec(a["norm_mix_g_2"][0]), vec(a["kv_norm_g_2"][0]), vec(a["norm_cross_g_2"][0]),
            vec(a["norm_mem_g_2"][0]), vec(a["norm_mlp_g_2"][0]), vec(a["norm_final_g_2"]), np.full((P, 1), EPS, f), np.ones((P, 1), f)]
    gdn, late = tables()
    return {
        "x_in": np.concatenate([tr(a["ctx"][0]), tr(a["x"][0])], axis=2),
        "mem_in": tr(a["mem_2"][0]),
        "a_stream": np.concatenate([blocks(a["ada_w"][i]) for i in range(2)]),
        "w_stream": np.concatenate(stream),
        "cols": np.ascontiguousarray(np.concatenate(cols, axis=1)),
        "gdn_tables": gdn, "late_tables": late, "ident": np.eye(P, dtype=f),
        "ws_t": np.ascontiguousarray(a["a_ws"][0].transpose(2, 0, 1)),
        "bs_row": a["a_bs"][0].reshape(1, 512),
        "w_uk": np.ascontiguousarray(a["w_uk_2"][0].reshape(4, P, P).transpose(1, 0, 2)),
        "w_uv": np.ascontiguousarray(a["w_uv_2"][0].transpose(1, 0, 2)),
    }


DONE_BLOCK, DONE_TILE = {}, {}


def count_signals():
    n = 0
    for name, nb, nt in STAGES:
        b, t = B0[name], T0[name]
        if name in ("uq", "ukv_k"):
            per = 3 if name == "uq" else 2
            for m in range(nt):
                n += 1
                DONE_TILE[t + m] = n
                for k in range(nb):
                    if min(8 * k + 7, per * nt - 1) // per == m:
                        DONE_BLOCK[b + k] = n
        elif name == "ukv_v":
            for m in range(nt):
                n += 1
                DONE_TILE[t + m] = n
                DONE_BLOCK[b + m // 4] = n
        elif name in ("in2_v", "xv"):
            for k in range(nb):
                for tok in range(2):
                    n += 1
                    DONE_TILE[t + 2 * (k // 4) + tok] = n
                DONE_BLOCK[b + k] = n
        else:
            for k in range(nb):
                n += 1
                DONE_BLOCK[b + k] = n
                DONE_TILE[t + k * nt // nb] = n


count_signals()


def two_blocks_kernel(nc, x_in, mem_in, a_stream, w_stream, cols, gdn_tables, late_tables, ident, ws_t, bs_row, w_uk, w_uv, out):
    F32, F32R = mybir.dt.float32, mybir.dt.float32r
    ALU, ACT, AX = mybir.AluOpType, mybir.ActivationFunctionType, mybir.AxisListType
    ds = bass.ds
    ctx = ExitStack()
    with ctx:
        base = -(-nc.sbuf_base // 64) * 64
        end = nc.sbuf_usable_end // 32 * 32
        cursor = [base]

        def place(name, shape, dt=F32):
            size = 4
            for s in shape[1:]:
                size *= s
            size = -(-size // 32) * 32
            t = nc.alloc_sbuf_tensor_at(name, shape, dt, offset=cursor[0])
            cursor[0] += size
            assert cursor[0] <= end, (name, cursor[0] - end)
            return t

        RAW = place("w_raw", [P, 4, BLOCK])
        WH = place("w_high", [P, 2, BLOCK], F32R)
        WL = place("w_low", [P, 2, BLOCK], F32R)
        a_ring_at = cursor[0]
        AR = place("a_ring", [P, 2, BLOCK])
        X = place("x", [P, KC, T2])
        C = place("cols_sb", [P, NCOLS])
        MOD = place("mod", [P, 2, 6, KC, 2])
        GM = place("gains", [P, 2, 2, KC, 2])
        ID = place("ident_sb", [P, P])
        ONES = place("ones", [P, P])
        STD = place("std", [P, T2])
        SM = place("small", [P, 64])
        XP = place("conv_in", [P, 2, 2, SEQ + 2])
        tmp_at = cursor[0]
        TMP = place("tmp", [P, KC, T2])
        after_tmp = cursor[0]
        HH = place("h_high", [P, KC, T2], F32R)
        HL = place("h_low", [P, KC, T2], F32R)
        zone = cursor[0]
        cursor[0] = after_tmp
        A16 = place("a_first", [P, A_FIRST, BLOCK])
        MR = place("mod_rows", [2, 4, 512])
        cursor[0] = tmp_at
        C1 = place("conv_mid", [P, 2, T2])
        SG = place("silu_g", [P, T2])
        A32 = place("act", [P, T2])
        TY = place("res", [P, 2, T2])
        cursor[0] = after_tmp
        SQN = place("squares_n1_1", [P, KC, T2])
        cursor[0] = tmp_at
        GA = place("gate_a", [40, T2])
        GB = place("gate_b", [40, T2])
        GT = place("gate_t", [40, T2])
        SQ2 = place("sq2", [P, 2, T2])
        ST2 = place("st2", [P, 2, T2])
        cursor[0] = tmp_at
        CT = place("lev_ct", [P, 2, HEADS, P])
        M1 = place("lev_m1", [P, 2, HEADS, P])
        DT = place("decay", [P, HEADS, P])
        ER = place("exp_cum", [P, HEADS, P])
        VN = place("v_new", [P, 2, HEADS, P])
        cursor[0] = tmp_at
        SQ4 = place("sq4", [P, 4, T2])
        VTOK = place("v_tok", [P, 4, HEADS, P])
        cursor[0] = zone
        QKV = place("qkv", [P, 12, T2])
        UV = place("uv", [P, 8, T2])
        GATE = place("gate", [P, 4, T2])
        GTAB = place("gdn_tab", [P, NGDN])
        GTOK = place("g_tok", [P, 4, 40])
        GC = place("g_cum", [P, 4, 2, 8])
        EG = place("e_cum", [P, 4, 2, HEADS])
        EK = place("e_rest", [P, 4, 2, HEADS])
        BE = place("beta_e", [P, 4, 2, HEADS])
        GEND = place("g_end", [P, 2, 4, HEADS])
        TT = place("inv_t", [P, 4, HEADS, P])
        TU = place("inv_u", [P, 4, HEADS, P])
        ATT = place("attn_t", [P, 4, HEADS, P])
        QG0 = place("qg0", [P, 2, HEADS, P])
        S = place("state", [P, 2, HEADS, P])
        cursor[0] = after_tmp
        VB = place("v_beta", [P, 4, HEADS, P])
        KBG = place("k_beta_g", [P, 4, HEADS, P])
        KD = place("k_decay", [P, 4, HEADS, P])
        AT = place("a_t", [P, 4, HEADS, P])
        UU, WT = AT, TT
        cursor[0] = zone + 4 * (20 * T2 + 4 * T2 + NGDN) + 4096
        WS = place("ws_sb", [P, 4, P])
        BS = place("bs_sb", [1, 512])
        cursor[0] = zone
        TYO = place("res_out0", [P, 2, T2])
        cursor[0] = zone
        AH0 = place("act_high0", [P, FC, T2], F32R)
        AL0 = place("act_low0", [P, FC, T2], F32R)
        cursor[0] = zone
        LTAB = place("late_tab", [P, NLATE])
        late = cursor[0]
        CQ = place("cq", [P, 3, SEQ])
        CKV = place("ckv", [P, 2, T2])
        KR = place("kr", [P, T2])
        MQ = place("mla_q", [P, 12, SEQ])
        KN = place("mla_k", [P, 8, T2])
        VT = place("mla_v", [P, 4, 1024])
        CQH = place("cq_high", [P, 3, SEQ], F32R)
        CQL = place("cq_low", [P, 3, SEQ], F32R)
        CKH = place("ckv_high", [P, 2, T2], F32R)
        CKL = place("ckv_low", [P, 2, T2], F32R)
        cursor[0] = late
        AH1 = place("act_high1", [P, FC, SEQ], F32R)
        AL1 = place("act_low1", [P, FC, SEQ], F32R)
        cursor[0] = late
        PJ = place("proj", [P, 22, SEQ])
        VBK = place("dil_v", [P, 2, 512])
        CTK = place("c_tok", [P, 2, P])
        QL = place("q_lat", [P, 8, SEQ])
        OL = place("o_lat", [P, 2, SEQ])
        IX = place("index", [P, 2, SEQ])
        RL = place("relu", [P, 2, SEQ])
        AM = place("top_mask", [P, 2, SEQ])
        WE = place("w_eff", [P, 2, 8])
        M8 = place("max8", [P, 2, 8])
        WUK = place("w_uk_sb", [P, 4, P])
        WUV = place("w_uv_sb", [P, 8, 64])
        cursor[0] = late
        QC = place("cross_q", [P, 8, SEQ])
        KCR = place("cross_k", [P, 8, SEQ])
        VC = place("cross_v", [P, 2, 1024])
        cursor[0] = late
        AH2 = place("act_high2", [P, 32, SEQ], F32R)
        AL2 = place("act_low2", [P, 32, SEQ], F32R)
        late_end = end - 2 * BLOCK * 4
        cursor[0] = a_ring_at
        WH2 = place("w_high2", [P, 2, BLOCK], F32R)
        cursor[0] = late_end
        WL2 = place("w_low2", [P, 2, BLOCK], F32R)
        cursor[0] = tmp_at
        PB = place("probs", [P, 3, T2])
        PT = place("probs_t", [P, 2, 4, P])
        SX = place("scores", [P, 2, SEQ])
        RT = place("rot", [P, 2, SEQ])

        def slot(n):
            late_block = n - B0["in1"]
            return n % 2 if late_block < 0 else (B0["in1"] % 2, 1 - B0["in1"] % 2, 2, 3)[late_block % 4]

        def slot_before(n):
            late_block = n - B0["in1"]
            return n - 2 if late_block < 2 else B0["in1"] - 1 if late_block < 4 else n - 4

        def lead(name):
            return 2 if B0[name] < B0["in1"] else 3

        def wh(n):
            return WH[:, slot(n), :] if slot(n) < 2 else WH2[:, slot(n) - 2, :]

        def wl(n):
            return WL[:, slot(n), :] if slot(n) < 2 else WL2[:, slot(n) - 2, :]

        PL = [ctx.enter_context(nc.psum_tensor(f"proj{i}", [P, 512], F32)) for i in range(2)]
        BK = [ctx.enter_context(nc.psum_tensor(f"bank{i}", [P, 512], F32)) for i in range(6)]

        MROWS = [BK[1], BK[5], PL[0], PL[1]]
        SUMS = [BK[i] for i in (0, 2, 3, 4)]

        def bank(i, a, b):
            return BK[i][:, 0:a * b].rearrange("p (a b) -> p a b", a=a)

        def col(name, j=0):
            return C[:, COL_AT[name] + j:COL_AT[name] + j + 1]

        def gtab(name, j=0):
            return GTAB[:, GDN_AT[name] + j * P:GDN_AT[name] + (j + 1) * P]

        def ltab(name, j=0, w=SEQ):
            return LTAB[:, LATE_AT[name] + j * w:LATE_AT[name] + (j + 1) * w]

        def sem(name):
            return ctx.enter_context(nc.semaphore(name))

        cols_in, x_ready, gdn_in, ws_in, late_in, uk_in, mem_ready, out_done = map(
            sem, ("cols_in", "x_ready", "gdn_in", "ws_in", "late_in", "uk_in", "mem_ready", "out_done"))
        a_first = [sem(f"a_first{i}") for i in range(4)]
        w_landed = [sem(f"w_landed{i}") for i in range(4)]
        a_landed = [sem(f"a_landed{i}") for i in range(2)]
        w_high, w_low, pe_done, tile_out, a_used = map(sem, ("w_high_ready", "w_low_ready", "pe_done", "tile_out", "a_used"))
        cond_ready, mod_ready, init, m_sum, m_rows = map(sem, ("cond_ready", "mod_ready", "init", "m_sum", "m_rows"))
        n_sq, n_ss, n_root, n_std, n_bc, n_xn, n_hi, n_lo = map(sem, ("n_sq", "n_ss", "n_root", "n_std", "n_bc", "n_xn", "n_hi", "n_lo"))
        x_res = sem("x_res")
        conv_mid, conv_done, silu_done, act_done, act_hi, act_lo = map(sem, ("conv_mid", "conv_done", "silu_done", "act_done", "act_hi", "act_lo"))
        dve_step, act_step = sem("dve_step"), sem("act_step")
        names = ("l2_sq l2_ss l2_std l2_done g_rows g_in g_soft g_tr g_tok g_cs g_cum g_exp g_be gb_r gb_d gb_e gb_at gv_t gv_vb gv_k "
                 "lv_ct lv_m lv_m1 lv_x lv_tu uw_ready u_out w_out sc_o_read s_init on_sq on_ss on_std on_y on_hi y_b "
                 "ln_s ln_mean ln_x ln_sq ln_ss ln_std ln_n ln_v vt_t vt_out sp_s sp_y sp_hi y_a").split()
        G = {n: sem(n) for n in names}
        sc_w, sc_v, sc_s, sc_state = ([sem(f"{n}{d}") for d in range(2)] for n in ("scan_w", "scan_v", "scan_s", "scan_state"))
        names = ("rp_m rp_d at_s at_m at_p at_n at_t at_pt at_o at_hi at_y ol_out ol_o ix_l ix_r ix_a am_ready we_t we_ready ct_t ct_out "
                 "ql_m ql_out").split()
        A = {n: sem(n) for n in names}

        class Layer:
            def __init__(self, name, heads, key_tiles, per_group, a0, e0, masked, scale):
                self.name, self.heads, self.kt, self.per, self.a0, self.e0 = name, heads, key_tiles, per_group, a0, e0
                self.n, self.masked, self.scale = 2 * heads, masked, scale
                self.groups = self.n // per_group
                self.banks = BK[0:2] if masked else [BK[0], BK[1], PL[0]]
                self.lag = per_group + (5 if name == "dsa" else 3)
                self.steps = self.n - per_group + self.lag + 1

        MLA = Layer("mla", 8, 4, 2, 0, 0, False, 192 ** -0.5)
        DSA = Layer("dsa", 8, 2, 4, 16, 8, True, 96 ** -0.5)
        DIL = Layer("dil", 8, 2, 4, 32, 12, True, 64 ** -0.5)
        CRS = Layer("cross", 4, 2, 2, 48, 16, False, 256 ** -0.5)
        LAT = slice(SEQ, T2)
        CTX = slice(0, SEQ)
        ROPE1 = [(MQ[:, 8 + i, :], T0["uq"] + 8 + i, "m") for i in range(4)] + [(KR[:, LAT], T0["in1"] + 5, "m")]
        ROPE2 = [(PJ[:, i, :], T0["in2"] + i, "32" if i < 8 else "64") for i in (4, 5, 7, 8, 10, 11, 12, 13)] + [
            (PJ[:, i, :], T0["in2"] + i, "64") for i in range(14, 22)]

        def chunk_place(st, k, d):
            c = k if d == 0 else 3 - k
            return c, (c // 2) * 2 + d, 64 * (c % 2)

        def q_decayed(st, q):
            tl, d = q // 2, q % 2
            at = st * SEQ + tl * P
            return QG0[:, tl, :, :] if d == 0 else QKV[:, 0:HEADS, at:at + P]

        def squares(name, k):
            width = NORMS[NORM_I[name]][2]
            if name == "n1_1":
                return SQN[:, k, :]
            return TMP[:, k, :] if width == T2 else TMP[:, k, SEQ:T2]

        LEVELS = [(lev, q) for lev in range(6) for q in range(4)]
        block = ctx.enter_context(nc.Block())

        @block.tensor
        def _(pe):
            mm = nc.tensor.matmul

            def mm3(out_, wh, wl, xh, xl, first, last):
                mm(out_, wh, xh, start=first, stop=False)
                mm(out_, wh, xl, start=False, stop=False)
                return mm(out_, wl, xh, start=False, stop=last)

            def weights(n, off=0):
                pe.wait_ge(w_low, n + 1 + off)

            def free_bank(t, off=0):
                pe.wait_ge(tile_out, t + 1 + off)

            def tile(n, t, x, width, off=0, ready=None):
                weights(n, off)
                free_bank(t, off)
                for k in range(KC):
                    if ready:
                        pe.wait_ge(*ready(k))
                    w = slice(k * P, (k + 1) * P)
                    last = mm3(PL[t % 2][:, 0:width], wh(n)[:, w], wl(n)[:, w], HH[:, k, x], HL[:, k, x], k == 0, k == KC - 1)
                last.then_inc(pe_done, 1)

            def h_ready(name):
                return lambda k: (n_lo, NORM_S0[name] + k + 1)

            def mod_tile(w, out_, inc=True):
                for k in range(KC):
                    last = mm(out_, w[:, k * P:(k + 1) * P], C[:, COL_AT["cond"] + 2 * k:COL_AT["cond"] + 2 * k + 2], start=(k == 0), stop=(k == KC - 1))
                last.then_inc(a_used, 1)

            def ring_mod_tile(m, b, at, it=0, per=0):
                pe.wait_ge(a_landed[m % 2], 16 * ((m - A_FIRST) // 2 + 1) + 8 * per * it)
                mod_tile(AR[:, m % 2, :], BK[b][:, ds(2 * (m - at) + 2 * per * it, 2)])

            def norm_sum(name):
                _, nch, width = NORMS[NORM_I[name]]
                for k in range(nch):
                    pe.wait_ge(n_sq, NORM_C0[name] + k + 1)
                    for t in range(width // P):
                        last = mm(SUMS[t][:, 0:1], squares(name, k)[:, t * P:(t + 1) * P], ONES[:, 0:1], start=(k == 0), stop=(k == nch - 1))
                last.then_inc(n_ss, 1)

            def norm_spread(name):
                pe.wait_ge(n_std, NORM_I[name] + 1)
                for t in range(NORMS[NORM_I[name]][2] // P):
                    last = mm(BK[0][:, t * P:(t + 1) * P], STD[:, 8 + t:9 + t].to_broadcast([P, P]), ID[:], start=True, stop=True)
                last.then_inc(n_bc, 1)

            def norm(name):
                norm_sum(name)
                norm_spread(name)

            pe.wait_ge(init, 1)
            norm_sum("n1_0")
            pe.wait_ge(cond_ready, 1)
            for g in range(4):
                pe.wait_ge(a_first[g], 16)
                for k in range(KC):
                    at = COL_AT["cond"] + 2 * k
                    last = mm(MROWS[g][0:2, :].rearrange("p (m n) -> p m n", m=4), C[:, at:at + 2], A16[:, 4 * g:4 * g + 4, k * P:(k + 1) * P], start=(k == 0), stop=(k == KC - 1))
                last.then_inc(m_sum, 1)
            pe.wait_ge(cols_in, 32)
            for m in range(A_FIRST):
                pe.wait_ge(m_rows, m // 4 + 1)
                nc.tensor.transpose(BK[1][:, 2 * m:2 * m + 2], MR[0:2, m // 4, m % 4 * P:(m % 4 + 1) * P], ID[0:2, 0:2]).then_inc(a_used, 1)
            norm_spread("n1_0")

            with pe.Fori(0, 6) as i:
                for s in range(4):
                    tile(s, s, slice(0, T2), T2, 4 * i, h_ready("n1_0") if s == 0 else None)
                    ring_mod_tile(16 + s, 5, 16, i, 4)
            tile(24, 24, slice(0, T2), T2)

            for j in range(8):
                pe.wait_ge(G["l2_sq"], j + 1)
                if j >= 2:
                    pe.wait_ge(G["l2_std"], j - 1)
                mm(BK[j % 2][:], ONES[:], SQ2[:, j % 2, :], start=True, stop=True).then_inc(G["l2_ss"], 1)
            pe.wait_ge(G["g_soft"], 1)
            for t in range(4):
                last = nc.tensor.transpose(BK[4][:, 40 * t:40 * t + 40], GT[0:40, t * P:(t + 1) * P], ID[0:40, 0:40])
            last.then_inc(G["g_tr"], 1)
            pe.wait_ge(G["g_tok"], 1)
            pe.wait_ge(gdn_in, 16)
            pe.wait_ge(mod_ready, 2)
            for t in range(4):
                for d in range(2):
                    o = BK[5][:, (2 * t + d) * 8:(2 * t + d) * 8 + 8]
                    mm(o[:, 0:4], gtab("cum", d), GTOK[:, t, 4 * d:4 * d + 4], start=True, stop=True)
                    last = mm(o[:, 4:8], gtab("blk"), GTOK[:, t, 4 * d:4 * d + 4], start=True, stop=True)
            last.then_inc(G["g_cs"], 1)
            pe.wait_ge(G["l2_done"], 8)

            for st in range(2):
                if st:
                    for d in range(2):
                        pe.wait_ge(sc_state[d], 4)
                for q in range(4):
                    tl, d, z = q // 2, q % 2, 4 * st + q
                    tok = slice(st * SEQ + tl * P, st * SEQ + (tl + 1) * P)
                    tt = 2 * st + tl
                    if z:
                        pe.wait_ge(G["gb_at"], z)
                    else:
                        pe.wait_ge(G["g_cum"], 1)
                    for h in range(HEADS):
                        mm(bank(0, 4, P)[:, h, :], GTOK[:, tt, 4 * d + h:4 * d + h + 1].to_broadcast([P, P]), gtab("cum", d), start=True, stop=True)
                        last = mm(bank(1, 4, P)[:, h, :], GTOK[:, tt, 32 + 4 * d + h:33 + 4 * d + h].to_broadcast([P, P]), ID[:], start=True, stop=True)
                    if d == 0:
                        for h in range(HEADS):
                            mm(bank(2, 4, P)[:, h, :], QKV[:, 4 + h, tok], QKV[:, 4 + h, tok], start=True, stop=True)
                            last = mm(bank(3, 4, P)[:, h, :], QKV[:, 4 + h, tok], QKV[:, h, tok], start=True, stop=True)
                    last.then_inc(G["gb_r"], 1)
                pe.wait_ge(G["gb_at"], 4 * st + 4)
                for tl in range(2):
                    tok = slice(st * SEQ + tl * P, st * SEQ + (tl + 1) * P)
                    y = 2 * st + tl
                    if y:
                        pe.wait_ge(G["gv_vb"], y)
                        pe.wait_ge(G["gv_k"], y)
                    for h in range(HEADS):
                        nc.tensor.transpose(bank(4, 4, P)[:, h, :], QKV[:, 8 + h, tok], ID[:])
                    for h in range(HEADS):
                        last = nc.tensor.transpose(bank(5, 4, P)[:, h, :], QKV[:, 4 + h, tok], ID[:])
                    last.then_inc(G["gv_t"], 1)

                def first_product(k):
                    lev, q = LEVELS[k]
                    b, at = k % 2, 24 * st
                    pe.wait_ge(G["lv_ct"], at + k + 1)
                    if lev == 0:
                        if k >= 2:
                            pe.wait_ge(G["lv_tu"], at + k - 1)
                        for h in range(HEADS):
                            last = nc.tensor.transpose(bank(b, 4, P)[:, h, :], CT[:, b, h, :], ID[:])
                    else:
                        pe.wait_ge(G["lv_tu"], at + (k - 1 if k < 6 else k - 3))
                        for h in range(HEADS):
                            last = mm(bank(b, 4, P)[:, h, :], CT[:, b, h, :], TT[:, q, h, :], start=True, stop=True)
                    last.then_inc(G["lv_m"], 1)

                def second_product(k):
                    lev, q = LEVELS[k]
                    b, at = k % 2, 24 * st
                    pe.wait_ge(G["lv_m1"], 20 * st + k - 3)
                    if k >= 6:
                        pe.wait_ge(G["lv_tu"], at + k - 1)
                    else:
                        pe.wait_ge(G["gv_vb"], 2 * st + 2)
                        pe.wait_ge(G["gv_k"], 2 * st + 2)
                    if lev < 5:
                        for h in range(HEADS):
                            mm(bank(2 + 2 * b, 4, P)[:, h, :], TU[:, q, h, :], M1[:, b, h, :], start=True, stop=True)
                    for h in range(HEADS):
                        last = mm(bank(3 + 2 * b, 4, P)[:, h, :], M1[:, b, h, :], TU[:, q, h, :], start=True, stop=True)
                    last.then_inc(G["lv_x"], 1)

                for k in range(25):
                    if k < 24:
                        first_product(k)
                    if k >= 5:
                        second_product(k - 1)
                pe.wait_ge(G["lv_tu"], 24 * st + 24)
                for q in range(4):
                    b = q % 2
                    if q >= 2:
                        pe.wait_ge(G["u_out"], 4 * st + q - 1)
                        pe.wait_ge(G["w_out"], 4 * st + q - 1)
                    for h in range(HEADS):
                        mm(bank(2 + 2 * b, 4, P)[:, h, :], TU[:, q, h, :], VB[:, q, h, :], start=True, stop=True)
                        last = mm(bank(3 + 2 * b, 4, P)[:, h, :], KBG[:, q, h, :], TU[:, q, h, :], start=True, stop=True)
                    last.then_inc(G["uw_ready"], 1)
                pe.wait_ge(G["u_out"], 4 * st + 4)
                pe.wait_ge(G["w_out"], 4 * st + 4)
                pe.wait_ge(G["s_init"], 1)
                for k in range(4):
                    n = 4 * st + k
                    for d in range(2):
                        _, q, _ = chunk_place(st, k, d)
                        if n:
                            pe.wait_ge(sc_state[d], n)
                        for h in range(HEADS):
                            last = mm(bank(d, 4, P)[:, h, :], WT[:, q, h, :], S[:, d, h, :], start=True, stop=True)
                        last.then_inc(sc_w[d], 1)
                    for d in range(2):
                        _, q, po = chunk_place(st, k, d)
                        half = slice(po, po + 64)
                        pe.wait_ge(sc_v[d], n + 1)
                        o = BK[4 + d][:, 0:256].rearrange("p (h t) -> p h t", h=HEADS)
                        for h in range(HEADS):
                            mm(o[:, h, :], S[:, d, h, :], q_decayed(st, q)[:, h, half], start=True, stop=False)
                            mm(o[:, h, :], VN[half, d, h, :], ATT[half, q, h, half], start=False, stop=True)
                        for h in range(HEADS):
                            last = mm(bank(2 + d, 4, P)[:, h, :], KD[half, q, h, :], VN[half, d, h, :], start=True, stop=True)
                        last.then_inc(sc_s[d], 1)
            for d in range(2):
                pe.wait_ge(sc_state[d], 8)
            for h in range(HEADS):
                pe.wait_ge(G["on_sq"], h + 1)
                if h >= 2:
                    pe.wait_ge(G["on_std"], h - 1)
                mm(BK[h % 2][:], ONES[:], SQ2[:, h % 2, :], start=True, stop=True).then_inc(G["on_ss"], 1)
            for g in range(4):
                last = mm(BK[2][:], ONES[:], UV[:, 4 + g, :], start=(g == 0), stop=(g == 3))
            last.then_inc(G["ln_s"], 1)
            for g in range(4):
                pe.wait_ge(G["ln_sq"], g + 1)
                last = mm(BK[3][:], ONES[:], SQ4[:, g, :], start=(g == 0), stop=(g == 3))
            last.then_inc(G["ln_ss"], 1)
            pe.wait_ge(G["ln_v"], 4)
            for t in range(4):
                if t >= 2:
                    pe.wait_ge(G["vt_out"], t - 1)
                for g in range(4):
                    last = nc.tensor.transpose(bank(4 + t % 2, 4, P)[:, g, :], UV[:, 4 + g, t * P:(t + 1) * P], ID[:])
                last.then_inc(G["vt_t"], 1)
            pe.wait_ge(ws_in, 32)
            for t in range(4):
                pe.wait_ge(G["vt_out"], t + 1)
                if t >= 2:
                    pe.wait_ge(G["sp_y"], t - 1)
                for g in range(4):
                    o = bank(2 + t % 2, 4, P)[:, g, :]
                    mm(o, ONES[0:1, :], BS[0:1, g * P:(g + 1) * P], start=True, stop=False)
                    last = mm(o, VTOK[:, t, g, :], WS[:, g, :], start=False, stop=True)
                last.then_inc(G["sp_s"], 1)

            pe.wait_ge(G["y_b"], 4)
            pe.wait_ge(G["y_a"], 4)
            with pe.Fori(0, 2) as i:
                for s in range(4):
                    tile(B0["out0"] + s, T0["out0"] + s, slice(0, T2), T2, 4 * i)
                    for j in ((0, 1), (2,), (3, 4), (5,))[s]:
                        ring_mod_tile(40 + j, 1, 40, i, 6)

            def up(layer, x, width):
                name = f"up{layer}"
                with pe.Fori(0, FC // 2) as i:
                    for s in range(4):
                        tile(B0[name] + s, T0[name] + s, x, width, 4 * i, h_ready(f"n2_{layer}") if s == 0 else None)
                        if layer == 0:
                            ring_mod_tile(52 + s, 5, 52, i, 4)

            def down(layer, ah, al, width):
                name = f"dn{layer}"
                with pe.Fori(0, 2) as i:
                    for m in range(4):
                        t = T0[name] + m
                        free_bank(t, 4 * i)
                        for k in range(FC):
                            n, w = B0[name] + 3 * m + k // 8, slice(k % 8 * P, (k % 8 + 1) * P)
                            if k % 8 == 0:
                                weights(n, 12 * i)
                            if m == 0:
                                pe.wait_ge(act_lo, FC * layer + k + 1)
                            last = mm3(PL[t % 2][:, 0:width], wh(n)[:, w], wl(n)[:, w], ah[:, k, :], al[:, k, :], k == 0, k == FC - 1)
                            if k % 8 == 7 or k == FC - 1:
                                last.then_inc(pe_done, 1)

            def project(name, x, width, ready=None, loops=2):
                with pe.Fori(0, loops) as i:
                    for s in range(4):
                        tile(B0[name] + s, T0[name] + s, x, width, 4 * i, ready if s == 0 else None)

            norm("n2_0")
            up(0, slice(0, T2), T2)
            down(0, AH0, AL0, T2)

            norm("n1_1")
            for m in range(6):
                x = LAT if m < 3 else slice(0, T2)
                tile(B0["in1"] + m, T0["in1"] + m, x, SEQ if m < 3 else T2, 0, h_ready("n1_1") if m in (0, 3) else None)
            norm("cq")
            norm("ckv")

            def chunks(name, per, xh, xl, ready):
                done = -1
                for m in range(dict((s, n) for s, _, n in STAGES)[name]):
                    t = T0[name] + m
                    free_bank(t)
                    for k in range(per):
                        n, w = B0[name] + (m * per + k) // 8, slice((m * per + k) % 8 * P, ((m * per + k) % 8 + 1) * P)
                        if n != done:
                            weights(n)
                            done = n
                        if m == 0:
                            pe.wait_ge(n_lo, NORM_S0[ready] + k + 1)
                        last = mm3(PL[t % 2][:, 0:xh.shape[2]], wh(n)[:, w], wl(n)[:, w], xh[:, k, :], xl[:, k, :], k == 0, k == per - 1)
                    last.then_inc(pe_done, 1)

            def moving(name, xh, xl, x0, nblocks, toks, per_tile):
                for b in range(nblocks):
                    n = B0[name] + b
                    weights(n)
                    first, final = b % per_tile == 0, b % per_tile == per_tile - 1
                    for tok in range(toks):
                        t = T0[name] + (b // per_tile) * toks + tok
                        if first:
                            free_bank(t)
                        for kk in range(2):
                            k = 2 * (b % per_tile) + kk
                            x = slice(x0 + tok * P, x0 + (tok + 1) * P)
                            w = slice(kk * 512, (kk + 1) * 512)
                            o = PL[t % 2][:]
                            mm(o, xh[:, k, x], wh(n)[:, w], start=(first and kk == 0), stop=False)
                            mm(o, xh[:, k, x], wl(n)[:, w], start=False, stop=False)
                            last = mm(o, xl[:, k, x], wh(n)[:, w], start=False, stop=(final and kk == 1))
                        last.then_inc(pe_done, 1)

            chunks("uq", 3, CQH, CQL, "cq")
            chunks("ukv_k", 2, CKH, CKL, "ckv")
            moving("ukv_v", CKH, CKL, 0, 2, 4, 1)

            def rotate(tiles, r0):
                for i, (x, t, which) in enumerate(tiles):
                    pe.wait_ge(tile_out, t + 3)
                    if i >= 2:
                        pe.wait_ge(A["rp_d"], r0 + i - 1)
                    mm(BK[2 + i % 2][:, 0:SEQ], ltab("perm32" if which == "32" else "perm64", 0, P), x, start=True, stop=True).then_inc(A["rp_m"], 1)

            pe.wait_ge(late_in, 16)
            rotate(ROPE1, 0)
            pe.wait_ge(A["rp_d"], len(ROPE1))
            pe.wait_ge(tile_out, T0["out1"] + 2)

            def attend(ly, scores, values, extra=None):
                nb = len(ly.banks)
                for a in range(ly.n + 3):
                    if a < ly.n:
                        if ly.a0 or a >= nb:
                            pe.wait_ge(A["at_m" if ly.masked else "at_p"], ly.a0 + max(0, a - nb + 1))
                        scores(a // 2, a % 2, ly.banks[a % nb]).then_inc(A["at_s"], 1)
                    if 2 <= a < ly.n + 2:
                        p = a - 2
                        pe.wait_ge(A["at_n"], ly.a0 + p + 1)
                        for k in range(ly.kt):
                            last = nc.tensor.transpose(BK[2 + p % 2][:, k * P:(k + 1) * P], PB[:, p % 3, k * P:(k + 1) * P], ID[:])
                        last.then_inc(A["at_t"], 1)
                    if a >= 3:
                        p = a - 3
                        pe.wait_ge(A["at_pt"], ly.a0 + p + 1)
                        e = p // ly.per
                        if ly is not DSA and p % ly.per == 0 and ly.e0 + e >= 2:
                            pe.wait_ge(A["at_y"], ly.e0 + e - 1)
                        values(p // 2, p % 2, PT[:, p % 2, :, :]).then_inc(A["at_o"], 1)
                        if extra:
                            extra(p)

            def mla_scores(h, qt, o):
                q, po = slice(qt * P, (qt + 1) * P), 64 * (h % 2)
                mm(o[:], MQ[:, h, q], KN[:, h, :], start=True, stop=False)
                return mm(o[:], MQ[po:po + 64, 8 + h // 2, q], KR[po:po + 64, :], start=False, stop=True)

            def mla_values(h, qt, pt):
                for k in range(4):
                    last = mm(BK[4 + h % 2][:, qt * P:(qt + 1) * P], VT[:, k, h * P:(h + 1) * P], pt[:, k, :], start=(k == 0), stop=(k == 3))
                return last

            attend(MLA, mla_scores, mla_values)
            project("out1", LAT, SEQ, lambda k: (A["at_y"], 8))
            norm("n2_1")
            up(1, LAT, SEQ)
            down(1, AH1, AL1, SEQ)
            norm("final1")

            norm("mix")
            project("in2", LAT, SEQ, h_ready("mix"), 5)
            for m in (20, 21):
                tile(B0["in2"] + m, T0["in2"] + m, LAT, SEQ)
            moving("in2_v", HH, HL, SEQ, 4, 2, 4)
            norm("kv2")
            rotate(ROPE2, len(ROPE1))
            pe.wait_ge(A["rp_d"], len(ROPE1) + len(ROPE2))
            pe.wait_ge(tile_out, T0["out2"] + 2)
            for qt in range(2):
                last = nc.tensor.transpose(BK[4][:, 8 * qt:8 * qt + 8], PJ[0:8, 9, qt * P:(qt + 1) * P], ID[0:8, 0:8])
            last.then_inc(A["we_t"], 1)
            pe.wait_ge(n_xn, NORM_C0["kv2"] + 1)
            for qt in range(2):
                last = nc.tensor.transpose(BK[5][:, qt * P:(qt + 1) * P], PJ[:, 6, qt * P:(qt + 1) * P], ID[:])
            last.then_inc(A["ct_t"], 1)
            pe.wait_ge(uk_in, 32)
            for h in range(8):
                po = 64 * (h % 2)
                if h >= 2:
                    pe.wait_ge(A["ql_out"], h - 1)
                mm(BK[2 + h % 2][:, 0:SEQ], WUK[po:po + 64, h // 2, :], PJ[po:po + 64, h // 2, :], start=True, stop=True).then_inc(A["ql_m"], 1)
            for j in range(16):
                qt, h = j // 8, j % 8
                po = 64 * (h % 2)
                if j >= 2:
                    pe.wait_ge(A["ix_r"], j - 1)
                mm(BK[j % 2][:, 0:SEQ], PJ[po:po + 64, 10 + h // 2, qt * P:(qt + 1) * P], PJ[po:po + 64, 8, :], start=True, stop=True).then_inc(A["ix_l"], 1)
            pe.wait_ge(A["ix_r"], 16)
            pe.wait_ge(A["ql_out"], 8)
            pe.wait_ge(A["ct_out"], 1)
            pe.wait_ge(A["we_ready"], 1)

            def dsa_scores(h, qt, o):
                q, po = slice(qt * P, (qt + 1) * P), 32 * (h % 4)
                mm(o[:, 0:SEQ], QL[:, h, q], PJ[:, 6, :], start=True, stop=False)
                return mm(o[:, 0:SEQ], PJ[po:po + 32, 4 + h // 4, q], PJ[po:po + 32, 7, :], start=False, stop=True)

            def dsa_values(h, qt, pt):
                if qt == 0 and h >= 2:
                    pe.wait_ge(A["ol_out"], h - 1)
                for k in range(2):
                    last = mm(BK[4 + h % 2][:, qt * P:(qt + 1) * P], CTK[:, k, :], pt[:, k, :], start=(k == 0), stop=(k == 1))
                return last

            def dsa_out(h):
                pair, po = h // 2, 64 * (h % 2)
                pe.wait_ge(A["ol_out"], h + 1)
                if h % 2 == 0 and pair >= 2:
                    pe.wait_ge(A["at_y"], DSA.e0 + pair - 1)
                mm(PL[pair % 2][po:po + 64, 0:SEQ], WUV[:, h, :], OL[:, h % 2, :], start=True, stop=True).then_inc(A["ol_o"], 1)

            attend(DSA, dsa_scores, dsa_values, lambda p: dsa_out((p - 3) // 2) if p % 2 and p >= 3 else None)
            dsa_out(7)

            def dil_scores(h, qt, o):
                q, po = slice(qt * P, (qt + 1) * P), 64 * (h % 2)
                return mm(o[:, 0:SEQ], PJ[po:po + 64, 14 + h // 2, q], PJ[po:po + 64, 18 + h // 2, :], start=True, stop=True)

            def dil_values(h, qt, pt):
                po = 64 * (h % 2)
                for k in range(2):
                    last = mm(BK[4 + h // 2 % 2][po:po + 64, qt * P:(qt + 1) * P], VBK[:, k, h * 64:(h + 1) * 64], pt[:, k, :], start=(k == 0), stop=(k == 1))
                return last

            attend(DIL, dil_scores, dil_values)
            project("out2", LAT, SEQ, lambda k: (A["at_y"], 16))

            norm("cross")
            norm("mem")
            project("xq", LAT, SEQ, h_ready("cross"))
            project("xk", CTX, SEQ, h_ready("mem"))
            moving("xv", HH, HL, 0, 8, 2, 4)
            pe.wait_ge(tile_out, T0["xo"] + 2)

            def cross_scores(h, qt, o):
                q = slice(qt * P, (qt + 1) * P)
                mm(o[:, 0:SEQ], QC[:, 2 * h, q], KCR[:, 2 * h, :], start=True, stop=False)
                return mm(o[:, 0:SEQ], QC[:, 2 * h + 1, q], KCR[:, 2 * h + 1, :], start=False, stop=True)

            def cross_values(h, qt, pt):
                o = BK[4 + h % 2][:, 0:512].rearrange("p (c q) -> p c q", c=2)
                for c in range(2):
                    for k in range(2):
                        last = mm(o[:, c, qt * P:(qt + 1) * P], VC[:, k, h * 256 + c * P:h * 256 + (c + 1) * P], pt[:, k, :], start=(k == 0), stop=(k == 1))
                return last

            attend(CRS, cross_scores, cross_values)
            project("xo", LAT, SEQ, lambda k: (A["at_y"], 20))

            norm("mlp")
            project("up2", LAT, SEQ, h_ready("mlp"), 8)

            def down2(i):
                for m in range(2):
                    t = T0["dn2"] + m
                    free_bank(t, 2 * i)
                    for k in range(32):
                        n, w = B0["dn2"] + 4 * m + k // 8, slice(k % 8 * P, (k % 8 + 1) * P)
                        if k % 8 == 0:
                            weights(n, 8 * i)
                        if m == 0:
                            pe.wait_ge(act_lo, 2 * FC + k + 1)
                        last = mm3(PL[t % 2][:, 0:SEQ], wh(n)[:, w], wl(n)[:, w], AH2[:, k, :], AL2[:, k, :], k == 0, k == 31)
                        if k % 8 == 7:
                            last.then_inc(pe_done, 1)

            with pe.Fori(0, 4) as i:
                down2(i)
            norm("final2")

        @block.sync
        def _(sp):
            def load_w(n, off=0):
                sp.dma_start(RAW[:, n % 4, :], w_stream[n + off]).then_inc(w_landed[n % 4], 16)

            def next_w(s, off=0):
                sp.wait_ge(w_low, s + 1 + off)
                load_w(s + 4, off)

            def load_a(m, off=0):
                sp.wait_ge(a_used, m - 1 + off)
                sp.dma_start(AR[:, m % 2, :], a_stream[m + off]).then_inc(a_landed[m % 2], 16)

            sp.dma_start(X[:], x_in).then_inc(x_ready, 16)
            for g in range(4):
                m = slice(4 * g, 4 * g + 4)
                sp.dma_start(A16[:, m, :], a_stream[m].rearrange("m p n -> p m n")).then_inc(a_first[g], 16)
            for n in range(4):
                load_w(n)
            with sp.Fori(0, 6) as i:
                for s in range(4):
                    next_w(s, 4 * i)
                    load_a(16 + s, 4 * i)
            next_w(24)
            with sp.Fori(0, 2) as i:
                for s in range(4):
                    next_w(B0["out0"] + s, 4 * i)
                    for j in ((0, 1), (2,), (3, 4), (5,))[s]:
                        load_a(40 + j, 6 * i)
            with sp.Fori(0, FC // 2) as i:
                for s in range(4):
                    next_w(B0["up0"] + s, 4 * i)
                    load_a(52 + s, 4 * i)
            left = NBLK - 4 - B0["dn0"]
            with sp.Fori(0, left // 4) as i:
                for s in range(4):
                    next_w(B0["dn0"] + s, 4 * i)
            for s in range(left // 4 * 4, left):
                next_w(B0["dn0"] + s)
            for k in range(0, KC, 4):
                sp.wait_ge(n_xn, NORM_C0["final2"] + k + 4)
                sp.dma_start(out[:, k:k + 4, :], X[:, k:k + 4, LAT]).then_inc(out_done, 16)
            sp.wait_ge(out_done, 32)

        @block.gpsimd
        def _(pool):
            nc.gpsimd.memset(ONES[:], 1.0).then_inc(init, 1)
            for k in range(2):
                nc.gpsimd.memset(XP[:, k, :, 0:1], 0.0)
                nc.gpsimd.memset(XP[:, k, :, SEQ + 1:SEQ + 2], 0.0).then_inc(conv_done, 1)
            nc.gpsimd.memset(S[:], 0.0).then_inc(G["s_init"], 1)
            pool.wait_ge(mod_ready, 1)
            pool.dma_start(GTAB[:], gdn_tables).then_inc(gdn_in, 16)
            pool.wait_ge(gdn_in, 16)
            for st in range(2):
                for k, (lev, q) in enumerate(LEVELS):
                    n, b = 24 * st + k, k % 2
                    if lev == 0:
                        pool.wait_ge(G["gb_at"], 4 * st + q + 1)
                    if n >= 2:
                        pool.wait_ge(G["lv_m"], n - 1)
                    if 2 <= k < 6:
                        pool.wait_ge(G["lv_tu"], n - 1)
                    mask = gtab("lev", 6 * (q % 2) + lev).unsqueeze(1).to_broadcast([P, HEADS, P])
                    nc.gpsimd.tensor_tensor(CT[:, b, :, :], AT[:, q, :, :], mask, ALU.mult).then_inc(G["lv_ct"], 1)
            for d in range(2):
                pool.wait_ge(sc_state[d], 8)
            pool.dma_start(WS[:], ws_t).then_inc(ws_in, 16)
            pool.dma_start(BS[:], bs_row).then_inc(ws_in, 16)
            pool.wait_ge(x_res, 2 + RES["dn0"] + 8)
            pool.dma_start(LTAB[:], late_tables).then_inc(late_in, 16)
            pool.wait_ge(n_xn, NORM_C0["n1_1"] + 8)
            pool.dma_start(X[:, :, CTX], mem_in).then_inc(mem_ready, 16)
            pool.wait_ge(x_res, 2 + RES["dn1"] + 8)
            pool.dma_start(WUK[:], w_uk).then_inc(uk_in, 16)
            pool.dma_start(WUV[:], w_uv).then_inc(uk_in, 16)

        UVF = UV[:].rearrange("p a b -> p (a b)")
        PJF = PJ[:].rearrange("p a b -> p (a b)")
        QCF, KCF = QC[:].rearrange("p a b -> p (a b)"), KCR[:].rearrange("p a b -> p (a b)")
        QKVF = QKV[:].rearrange("p a b -> p (a b)")
        XF = X[:].rearrange("p a b -> p (a b)")
        MODF = MOD[:].rearrange("p a b c d -> p (a b c d)")
        NORM_OUT = {"cq": (CQH, CQL), "ckv": (CKH, CKL)}

        def norm_src(name, k):
            if name == "cq":
                return CQ[:, k, :]
            if name == "ckv":
                return CKV[:, k, :]
            if name == "kv2":
                return PJ[:, 6, :]
            if name == "mem":
                return X[:, k, CTX]
            return X[:, k, :] if NORMS[NORM_I[name]][2] == T2 else X[:, k, LAT]

        def norm_dst(name, k, low):
            if name in NORM_OUT:
                return NORM_OUT[name][low][:, k, :]
            x = CTX if name == "mem" else LAT if NORMS[NORM_I[name]][2] == SEQ else slice(0, T2)
            return (HL if low else HH)[:, k, x]

        def streams(name):
            return [(CTX, 0), (LAT, 1)] if NORMS[NORM_I[name]][2] == T2 else [(CTX, 1)]

        @block.scalar
        def _(act):
            f = nc.scalar.activation
            steps = [0]

            def link(ins):
                steps[0] += 1
                ins.then_inc(act_step, 1)
                act.wait_ge(act_step, steps[0])

            def split(n, off=0):
                if n >= NBLK:
                    return
                act.wait_ge(w_landed[n % 4], 16 * (n // 4 + 1) + 4 * off)
                if n >= 2:
                    act.wait_ge(pe_done, DONE_BLOCK[slot_before(n)] + off)
                f(wh(n), RAW[:, n % 4, :], ACT.Copy).then_inc(w_high, 1)

            def done(t, off=0):
                act.wait_ge(pe_done, DONE_TILE[t] + off)

            def norm_start(name):
                i = NORM_I[name]
                f(SM[:, 32 + i:33 + i], col("one"), ACT.Sqrt)
                if NORM_S0[name]:
                    act.wait_ge(n_lo, NORM_S0[name])
                if i:
                    act.wait_ge(n_xn, NORM_C0[name])

            def square(name, k, ready):
                act.wait_ge(*ready)
                f(squares(name, k), norm_src(name, k), ACT.Square).then_inc(n_sq, 1)

            def norm_root(name):
                i = NORM_I[name]
                width = NORMS[i][2]
                features = {"cq": 384, "ckv": 256, "kv2": 128}.get(name, D)
                act.wait_ge(n_ss, i + 1)
                for t in range(width // P):
                    last = f(STD[:, t:t + 1], SUMS[t][:, 0:1], ACT.Sqrt, scale=1.0 / features, bias=col("eps"))
                last.then_inc(n_root, 1)

            def norm_high(name):
                _, nch, width = NORMS[NORM_I[name]]
                if name not in SPLIT:
                    return
                for k in range(nch):
                    act.wait_ge(n_xn, NORM_C0[name] + k + 1)
                    if name in MODULATED:
                        layer, part = MODULATED[name]
                        for x, s in streams(name):
                            last = f(norm_dst(name, k, 0)[:, x], TMP[:, k, x], ACT.Identity, bias=MOD[:, layer, part, k, s:s + 1])
                        last.then_inc(n_hi, 1)
                    else:
                        f(norm_dst(name, k, 0), TMP[:, k, 0:width], ACT.Copy).then_inc(n_hi, 1)

            def norm_end(name):
                norm_root(name)
                norm_high(name)

            def norm(name, ready):
                norm_start(name)
                for k in range(NORMS[NORM_I[name]][1]):
                    square(name, k, ready(k))
                norm_end(name)

            def residual(name, m, gate, width):
                t, y = T0[name] + m, TYO if name == "out0" else TY
                done(t)
                act.wait_ge(x_res, RES[name] + m + 1)
                for x, s in ([(CTX, 0), (LAT, 1)] if width == T2 else [(CTX, 1)]):
                    if gate is None:
                        last = f(y[:, t % 2, x], PL[t % 2][:, x], ACT.Copy)
                    else:
                        last = f(y[:, t % 2, x], PL[t % 2][:, x], ACT.Identity, scale=MODF[:, (gate * KC + m) * 2 + s:(gate * KC + m) * 2 + s + 1])
                last.then_inc(tile_out, 1)

            def residuals(name, per, gate, width, then):
                norm_start(then)
                for m in range(KC):
                    for k in range(per):
                        split(B0[name] + per * m + k + lead(name))
                    residual(name, m, gate, width)
                    if m:
                        square(then, m - 1, (x_res, 2 + RES[name] + m))
                square(then, KC - 1, (x_res, 2 + RES[name] + KC))
                norm_end(then)

            def conv_in(t, k, cv, taps, width, it=0, per=0):
                act.wait_ge(pe_done, DONE_TILE[t] + per * it)
                act.wait_ge(conv_done, cv + k + 1 + per * it)
                n = width // SEQ
                f(XP[:, k % 2, 0:n, 1:SEQ + 1], PL[t % 2][:, 0:width].rearrange("p (s t) -> p s t", s=n), ACT.Copy)
                f(C1[:, k % 2, 0:width], PL[t % 2][:, 0:width], ACT.Identity, scale=C[:, ds(taps + 3 * k + 1 + 3 * per * it, 1)]).then_inc(tile_out, 1)

            act.dma_start(C[:], cols).then_inc(cols_in, 16)
            act.dma_start(ID[:], ident).then_inc(cols_in, 16)
            act.wait_ge(cols_in, 32)
            cond = C[:, COL_AT["cond"]:COL_AT["cond"] + 16]
            f(cond, cond, ACT.Silu).then_inc(cond_ready, 1)
            norm_start("n1_0")
            for k in range(KC):
                square("n1_0", k, (x_ready, 16))
            norm_root("n1_0")
            for g in range(4):
                act.wait_ge(m_sum, g + 1)
                f(MR[0:2, g, :], MROWS[g][0:2, :], ACT.Copy).then_inc(m_rows, 1)
            for j in range(2):
                f(SM[:, j:j + 1], col("one"), ACT.Copy).then_inc(tile_out, 1)
            split(0)
            norm_high("n1_0")
            split(1)

            with act.Fori(0, 2) as i:
                for s in range(4):
                    split(s + 2, 4 * i)
                    done(s, 4 * i)
                    f(UVF[:, ds(s * T2 + 4 * T2 * i, T2)], PL[s % 2][:], ACT.Gelu).then_inc(tile_out, 1)
            with act.Fori(0, 3) as i:
                for s in range(4):
                    split(8 + s + 2, 4 * i)
                    conv_in(8 + s, s, 0, COL_AT["bconv"], T2, i, 4)
                    act.wait_ge(conv_done, s + 3 + 4 * i)
                    f(QKVF[:, ds(s * T2 + 4 * T2 * i, T2)], C1[:, s % 2, :], ACT.Silu).then_inc(silu_done, 1)
            for t in range(20, 24):
                split(t + 2)
                done(t)
                f(GATE[:, t - 20, :], PL[t % 2][:], ACT.Silu).then_inc(tile_out, 1)
            split(26)
            done(24)
            act.wait_ge(G["g_rows"], 1)
            f(GA[0:8, :], PL[0][0:8, :], ACT.Identity, bias=C[0:8, COL_AT["dt_bias"]:COL_AT["dt_bias"] + 1])
            link(f(GT[32:40, :], PL[0][32:40, :], ACT.Sigmoid))
            f(SM[:, 2:3], col("one"), ACT.Copy).then_inc(tile_out, 1)
            link(f(GB[0:8, :], GA[0:8, :], ACT.Abs))
            link(f(GB[0:8, :], GB[0:8, :], ACT.Exp, scale=-1.0))
            f(SM[0:8, 4:5], C[0:8, COL_AT["a_log"]:COL_AT["a_log"] + 1], ACT.Exp)
            f(GB[0:8, :], GB[0:8, :], ACT.Ln, bias=C[0:8, COL_AT["one"]:COL_AT["one"] + 1]).then_inc(G["g_in"], 1)

            act.wait_ge(silu_done, 12)
            for j in range(9):
                if j < 8:
                    if j >= 2:
                        act.wait_ge(G["l2_ss"], j - 1)
                    f(SQ2[:, j % 2, :], QKV[:, j, :], ACT.Square).then_inc(G["l2_sq"], 1)
                if j >= 1:
                    act.wait_ge(G["l2_ss"], j)
                    if j >= 3:
                        act.wait_ge(G["l2_done"], j - 2)
                    f(ST2[:, (j - 1) % 2, :], BK[(j - 1) % 2][:], ACT.Sqrt, bias=col("eps")).then_inc(G["l2_std"], 1)
            act.wait_ge(G["g_cum"], 1)
            f(EG[:], GC[:, :, :, 0:4], ACT.Exp).then_inc(G["g_exp"], 1)
            act.wait_ge(G["g_cum"], 2)
            f(EK[:], EK[:], ACT.Exp).then_inc(G["g_exp"], 1)
            for st in range(2):
                for q in range(4):
                    z = 4 * st + q
                    act.wait_ge(G["gb_d"], z + 1)
                    f(DT[:], DT[:], ACT.Exp).then_inc(G["gb_e"], 1)
                    if z:
                        act.wait_ge(G["gb_at"], z)
                    f(ER[:], bank(0, 4, P), ACT.Exp).then_inc(G["gb_e"], 1)
                for tl in range(2):
                    y = 2 * st + tl
                    act.wait_ge(G["gv_t"], y + 1)
                    for d in range(2):
                        for h in range(HEADS):
                            last = f(VB[:, 2 * tl + d, h, :], bank(4, 4, P)[:, h, :], ACT.Identity, scale=GTOK[:, y, 32 + 4 * d + h:33 + 4 * d + h])
                    last.then_inc(G["gv_vb"], 1)
                for k in range(4, 24):
                    act.wait_ge(G["lv_m"], 24 * st + k + 1)
                    if k >= 6:
                        act.wait_ge(G["lv_x"], 20 * st + k - 5)
                    f(M1[:, k % 2, :, :], bank(k % 2, 4, P), ACT.Copy).then_inc(G["lv_m1"], 1)
                for q in range(4):
                    act.wait_ge(G["uw_ready"], 4 * st + q + 1)
                    f(UU[:, q, :, :], bank(2 + 2 * (q % 2), 4, P), ACT.Copy).then_inc(G["u_out"], 1)
            for d in range(2):
                act.wait_ge(sc_state[d], 8)
            for h in range(5):
                if h < 4:
                    if h >= 2:
                        act.wait_ge(G["on_ss"], h - 1)
                    f(SQ2[:, h % 2, :], QKV[:, 8 + h, :], ACT.Square).then_inc(G["on_sq"], 1)
                if h >= 1:
                    act.wait_ge(G["on_ss"], h)
                    if h >= 3:
                        act.wait_ge(G["on_y"], h - 2)
                    f(ST2[:, (h - 1) % 2, :], BK[(h - 1) % 2][:], ACT.Sqrt, scale=1.0 / P, bias=col("eps")).then_inc(G["on_std"], 1)
            for h in range(4):
                act.wait_ge(G["on_y"], h + 1)
                f(HH[:, 4 + h, :], QKV[:, 8 + h, :], ACT.Copy).then_inc(G["on_hi"], 1)
            act.wait_ge(G["ln_s"], 1)
            f(STD[:], BK[2][:], ACT.Copy, scale=1.0 / 512).then_inc(G["ln_mean"], 1)
            act.wait_ge(G["ln_x"], 1)
            for g in range(4):
                f(SQ4[:, g, :], UV[:, 4 + g, :], ACT.Square).then_inc(G["ln_sq"], 1)
            act.wait_ge(G["ln_ss"], 1)
            f(STD[:], BK[3][:], ACT.Sqrt, scale=1.0 / 512, bias=col("eps")).then_inc(G["ln_std"], 1)
            act.wait_ge(G["ln_n"], 1)
            for g in range(4):
                f(UV[:, 4 + g, :], UV[:, 4 + g, :], ACT.Identity, scale=col("a_ln_g", g), bias=col("a_ln_b", g)).then_inc(G["ln_v"], 1)
            for t in range(4):
                act.wait_ge(G["vt_t"], t + 1)
                f(VTOK[:, t, :, :], bank(4 + t % 2, 4, P), ACT.Copy).then_inc(G["vt_out"], 1)
            for t in range(4):
                act.wait_ge(G["sp_y"], t + 1)
                f(HH[:, 0:4, t * P:(t + 1) * P], UV[:, 0:4, t * P:(t + 1) * P], ACT.Copy).then_inc(G["sp_hi"], 1)

            act.wait_ge(mod_ready, 2)
            residuals("out0", 1, 2, T2, "n2_0")

            def up(layer, ah, width):
                name = f"up{layer}"
                cv, taps = 12 + 2 * FC * layer, COL_AT["fconv"] + 2 * FC * 3 * layer
                ahf = ah[:].rearrange("p a b -> p (a b)")
                def more(s, i):
                    split(B0[name] + s + lead(name), 4 * i)

                def taps_of(s, i):
                    conv_in(T0[name] + s, s, cv, taps, width, i, 4)

                def silu(p, i):
                    act.wait_ge(conv_done, cv + 2 * p + 3 + 4 * i)
                    f(SG[:, 0:width], C1[:, 0, 0:width], ACT.Silu).then_inc(silu_done, 1)

                def high(p, i):
                    act.wait_ge(act_done, FC * layer + p + 1 + 2 * i)
                    f(ahf[:, ds(p * width + 2 * width * i, width)], A32[:, 0:width], ACT.Copy).then_inc(act_hi, 1)

                with act.Fori(0, FC // 2) as i:
                    f(SM[:, 48:49], col("one"), ACT.Silu)
                    taps_of(0, i)
                    more(0, i)
                    taps_of(1, i)
                    more(1, i)
                    silu(0, i)
                    act.wait_ge(silu_done, 12 + FC * layer + 1 + 2 * i)
                    taps_of(2, i)
                    high(0, i)
                    more(2, i)
                    taps_of(3, i)
                    silu(1, i)
                    more(3, i)
                    high(1, i)

            def project(name, evac, loops=2):
                with act.Fori(0, loops) as i:
                    for s in range(4):
                        split(B0[name] + s + lead(name), 4 * i)
                        evac(s, i)

            def copy_to(name, flat, width):
                def evac(s, i):
                    done(T0[name] + s, 4 * i)
                    f(flat[:, ds(s * width + 4 * width * i, width)], PL[(T0[name] + s) % 2][:, 0:width], ACT.Copy).then_inc(tile_out, 1)
                return evac

            up(0, AH0, T2)
            act.wait_ge(mod_ready, 4)
            residuals("dn0", 3, 5, T2, "n1_1")

            split(B0["in1"] + 2)
            for m, o in enumerate([CQ[:, 0, :], CQ[:, 1, :], CQ[:, 2, :], CKV[:, 0, :], CKV[:, 1, :], KR[:]]):
                split(B0["in1"] + m + lead("in1"))
                done(T0["in1"] + m)
                f(o, PL[(T0["in1"] + m) % 2][:, 0:o.shape[1]], ACT.Copy).then_inc(tile_out, 1)
            norm("cq", lambda k: (tile_out, T0["in1"] + k + 3))
            norm("ckv", lambda k: (tile_out, T0["in1"] + k + 6))

            def walk(name, place_of):
                nb, nt = next((b, t) for s, b, t in STAGES if s == name)
                events = [(DONE_BLOCK[B0[name] + b], 0, b) for b in range(nb)] + [(DONE_TILE[T0[name] + t], 1, t) for t in range(nt)]
                for _, is_tile, j in sorted(events):
                    if is_tile:
                        o = place_of(j)
                        done(T0[name] + j)
                        f(o, PL[(T0[name] + j) % 2][:, 0:o.shape[1]], ACT.Copy).then_inc(tile_out, 1)
                    else:
                        split(B0[name] + j + lead(name))

            walk("uq", lambda m: MQ[:, m, :])
            walk("ukv_k", lambda m: KN[:, m, :])
            walk("ukv_v", lambda m: VT[:, m % 4, m // 4 * 512:(m // 4 + 1) * 512])

            def attend(ly, out_bank, out_chunks):
                for a in range(ly.steps):
                    w = ly.kt * P
                    if a < ly.n:
                        r = a % 3
                        act.wait_ge(A["at_m"], ly.a0 + a + 1)
                        if ly.a0 + a >= 3:
                            act.wait_ge(A["at_t"], ly.a0 + max(0, a - 2))
                        src = SX[:, a % 2, :] if ly.masked else ly.banks[a % 3][:, 0:w]
                        scale = 1.0 if ly.masked else ly.scale
                        if ly is DIL:
                            f(PB[:, r, 0:w], src, ACT.Exp, scale=scale, bias=SM[:, 20 + r:21 + r]).then_inc(A["at_p"], 1)
                        else:
                            f(PB[:, r, 0:w], src, ACT.Exp, scale=scale, bias=SM[:, 20 + r:21 + r], accum_out=SM[:, 24 + r:25 + r]).then_inc(A["at_p"], 1)
                    if 2 <= a < ly.n + 2:
                        p = a - 2
                        act.wait_ge(A["at_t"], ly.a0 + p + 1)
                        if ly.a0 + p >= 2:
                            act.wait_ge(A["at_o"], ly.a0 + p - 1)
                        f(PT[:, p % 2, 0:ly.kt, :], BK[2 + p % 2][:, 0:w].rearrange("p (k q) -> p k q", k=ly.kt), ACT.Copy).then_inc(A["at_pt"], 1)
                    if ly is DSA and a >= 5 and a % 2 == 1 and (a - 5) // 2 < 8:
                        h = (a - 5) // 2
                        act.wait_ge(A["at_o"], ly.a0 + 2 * h + 2)
                        if h >= 2:
                            act.wait_ge(A["ol_o"], h - 1)
                        f(OL[:, h % 2, :], BK[4 + h % 2][:, 0:SEQ], ACT.Copy).then_inc(A["ol_out"], 1)
                    if a >= ly.lag and (a - ly.lag) % ly.per == 0:
                        e = (a - ly.lag) // ly.per
                        if ly is DSA:
                            act.wait_ge(A["ol_o"], 2 * e + 2)
                        else:
                            act.wait_ge(A["at_o"], ly.a0 + ly.per * (e + 1))
                        f(out_chunks(HH, e), out_bank(e), ACT.Copy).then_inc(A["at_hi"], 1)

            attend(MLA, lambda e: BK[4 + e % 2][:, 0:SEQ], lambda h, e: h[:, e, LAT])
            residuals("out1", 1, 8, SEQ, "n2_1")
            up(1, AH1, SEQ)
            residuals("dn1", 3, 11, SEQ, "final1")

            norm("mix", lambda k: (n_xn, NORM_C0["final1"] + k + 1))
            project("in2", copy_to("in2", PJF, SEQ), 5)
            for m in (20, 21):
                split(B0["in2"] + m + lead("in2"))
                done(T0["in2"] + m)
                f(PJ[:, m, :], PL[(T0["in2"] + m) % 2][:, 0:SEQ], ACT.Copy).then_inc(tile_out, 1)
            walk("in2_v", lambda m: VBK[:, m, :])
            norm("kv2", lambda k: (tile_out, T0["in2"] + 9))
            act.wait_ge(A["ct_t"], 1)
            f(CTK[:], BK[5][:, 0:SEQ].rearrange("p (k c) -> p k c", k=2), ACT.Copy).then_inc(A["ct_out"], 1)
            for h in range(8):
                act.wait_ge(A["ql_m"], h + 1)
                f(QL[:, h, :], BK[2 + h % 2][:, 0:SEQ], ACT.Copy).then_inc(A["ql_out"], 1)
            for j in range(16):
                act.wait_ge(A["ix_l"], j + 1)
                if j >= 2:
                    act.wait_ge(A["ix_a"], j - 1)
                f(RL[:, j % 2, :], BK[j % 2][:, 0:SEQ], ACT.Relu).then_inc(A["ix_r"], 1)
            attend(DSA, lambda e: PL[e % 2][:, 0:SEQ], lambda h, e: h[:, e, LAT])
            attend(DIL, lambda e: BK[4 + e % 2][:, 0:SEQ], lambda h, e: h[:, 4 + e, LAT])
            residuals("out2", 1, None, SEQ, "cross")
            norm("mem", lambda k: (mem_ready, 16))
            project("xq", copy_to("xq", QCF, SEQ))
            project("xk", copy_to("xk", KCF, SEQ))
            walk("xv", lambda m: VC[:, m % 2, m // 2 * 512:(m // 2 + 1) * 512])
            attend(CRS, lambda e: BK[4 + e % 2][:, 0:512].rearrange("p (c q) -> p c q", c=2), lambda h, e: h[:, 2 * e:2 * e + 2, LAT])
            residuals("xo", 1, None, SEQ, "mlp")
            AHF2 = AH2[:].rearrange("p a b -> p (a b)")
            with act.Fori(0, 8) as i:
                for s in range(4):
                    split(B0["up2"] + s + lead("up2"), 4 * i)
                    t = T0["up2"] + s
                    done(t, 4 * i)
                    act.wait_ge(act_lo, 2 * FC + s - 1 + 4 * i)
                    f(C1[:, s % 2, 0:SEQ], PL[t % 2][:, 0:SEQ], ACT.Relu).then_inc(tile_out, 1)
                    act.wait_ge(tile_out, t + 3 + 4 * i)
                    f(AHF2[:, ds(s * SEQ + 4 * SEQ * i, SEQ)], C1[:, s % 2, 0:SEQ], ACT.Square).then_inc(act_hi, 1)

            residuals("dn2", 4, None, SEQ, "final2")

        @block.vector
        def _(dve):
            v = nc.vector
            steps = [0]

            def link(ins):
                steps[0] += 1
                ins.then_inc(dve_step, 1)
                dve.wait_ge(dve_step, steps[0])

            def low(n, off=0):
                if n >= NBLK:
                    return
                dve.wait_ge(w_high, n + 1 + off)
                v.tensor_tensor(wl(n), RAW[:, n % 4, :], wh(n), ALU.subtract).then_inc(w_low, 1)

            def modulation(b, first, n, at=0):
                bias = C[:, COL_AT["ada_b"] + first:COL_AT["ada_b"] + first + n].unsqueeze(2).to_broadcast([P, n, 2])
                o = MODF[:, 2 * first:2 * (first + n)].rearrange("p (m s) -> p m s", s=2)
                return v.tensor_tensor(o, BK[b][:, 2 * at:2 * (at + n)].rearrange("p (m s) -> p m s", s=2), bias, ALU.add)

            def gains(layer, which):
                at = COL_AT["norm1" if which == 0 else "norm2"] + KC * layer
                g = C[:, at:at + KC].unsqueeze(2).to_broadcast([P, KC, 2])
                return v.scalar_tensor_tensor(GM[:, layer, which, :, :], MOD[:, layer, 3 * which + 1, :, :], 1.0, g, ALU.add, ALU.mult)

            def norm_factor(name):
                i = NORM_I[name]
                nt = NORMS[i][2] // P
                dve.wait_ge(n_root, i + 1)
                v.reciprocal(STD[:, 8:8 + nt], STD[:, 0:nt]).then_inc(n_std, 1)

            def norm(name):
                i = NORM_I[name]
                _, nch, width = NORMS[i]
                if name != "n1_0":
                    norm_factor(name)
                dve.wait_ge(n_bc, i + 1)
                layer, part = MODULATED.get(name, (0, 0))

                def low_part(k):
                    dve.wait_ge(n_hi, NORM_S0[name] + k + 1)
                    if name in MODULATED:
                        for x, s in streams(name):
                            last = v.scalar_tensor_tensor(norm_dst(name, k, 1)[:, x], TMP[:, k, x], MOD[:, layer, part, k, s:s + 1], norm_dst(name, k, 0)[:, x],
                                                          ALU.add, ALU.subtract)
                    else:
                        last = v.tensor_tensor(norm_dst(name, k, 1), TMP[:, k, 0:width], norm_dst(name, k, 0), ALU.subtract)
                    last.then_inc(n_lo, 1)

                for k in range(nch):
                    src = norm_src(name, k)
                    o = TMP[:, k, 0:width] if name in SPLIT else src
                    if name in MODULATED:
                        for x, s in streams(name):
                            ins = v.scalar_tensor_tensor(o[:, x], src[:, x], GM[:, layer, part // 3, k, s:s + 1], BK[0][:, x], ALU.mult, ALU.mult)
                    else:
                        gain = {"cq": "mla_q", "ckv": "mla_kv"}.get(name, name)
                        ins = v.scalar_tensor_tensor(o, src, col(gain, k), BK[0][:, 0:width], ALU.mult, ALU.mult)
                    ins.then_inc(n_xn, 1)
                    if name in SPLIT and k:
                        low_part(k - 1)
                if name in SPLIT:
                    low_part(nch - 1)

            def conv(t, k, cv, taps, width, it=0, per=0):
                n = width // SEQ
                o = C1[:, k % 2, 0:width].rearrange("p (s t) -> p s t", s=n)
                dve.wait_ge(tile_out, t + 3 + per * it)
                v.scalar_tensor_tensor(o, XP[:, k % 2, 0:n, 0:SEQ], C[:, ds(taps + 3 * k + 3 * per * it, 1)], o, ALU.mult, ALU.add).then_inc(conv_mid, 1)
                dve.wait_ge(conv_mid, cv + k + 1 + per * it)
                v.scalar_tensor_tensor(o, XP[:, k % 2, 0:n, 2:SEQ + 2], C[:, ds(taps + 3 * k + 2 + 3 * per * it, 1)], o, ALU.mult, ALU.add).then_inc(conv_done, 1)

            def add(name, m, width, it=0, per=0):
                t = T0[name] + m
                dve.wait_ge(tile_out, t + 3 + per * it)
                x = XF[:, ds(m * T2 + (T2 - width) + per * T2 * it, width)]
                v.tensor_tensor(x, x, (TYO if name == "out0" else TY)[:, t % 2, 0:width], ALU.add).then_inc(x_res, 1)

            norm_factor("n1_0")
            dve.wait_ge(cond_ready, 1)
            dve.wait_ge(a_used, A_FIRST)
            link(modulation(1, 0, A_FIRST))
            gains(0, 0).then_inc(mod_ready, 1)
            dve.wait_ge(mod_ready, 1)
            low(0)
            norm("n1_0")
            low(1)

            with dve.Fori(0, 2) as i:
                for s in range(4):
                    low(s + 2, 4 * i)
            with dve.Fori(0, 3) as i:
                for s in range(4):
                    low(8 + s + 2, 4 * i)
                    conv(8 + s, s, 0, COL_AT["bconv"], T2, i, 4)
            for t in range(20, 25):
                low(t + 2)
            dve.wait_ge(a_used, 40)
            modulation(5, 16, 8).then_inc(x_res, 1)
            modulation(5, 24, 16, 8).then_inc(x_res, 1)
            dve.wait_ge(x_res, 2)
            gains(0, 1).then_inc(mod_ready, 1)

            v.memset(GT[:], 0.0).then_inc(G["g_rows"], 1)
            dve.wait_ge(G["g_in"], 1)
            link(v.scalar_tensor_tensor(GA[0:8, :], GA[0:8, :], 0.0, GB[0:8, :], ALU.max, ALU.add))
            v.tensor_scalar(GT[0:8, :], GA[0:8, :], SM[0:8, 4:5], -1.0, ALU.mult, ALU.mult).then_inc(G["g_soft"], 1)
            for j in range(8):
                dve.wait_ge(G["l2_std"], j + 1)
                b = j % 2
                link(v.reciprocal(ST2[:, b, :], ST2[:, b, :]))
                if j < 4:
                    ins = v.scalar_tensor_tensor(QKV[:, j, :], QKV[:, j, :], P ** -0.5, ST2[:, b, :], ALU.mult, ALU.mult)
                else:
                    ins = v.tensor_tensor(QKV[:, j, :], QKV[:, j, :], ST2[:, b, :], ALU.mult)
                ins.then_inc(G["l2_done"], 1)
            dve.wait_ge(G["g_tr"], 1)
            v.tensor_copy(GTOK[:], BK[4][:, 0:160].rearrange("p (t r) -> p t r", t=4)).then_inc(G["g_tok"], 1)
            dve.wait_ge(G["g_cs"], 1)
            v.tensor_copy(GC[:], BK[5][:, 0:64].rearrange("p (t d r) -> p t d r", t=4, d=2)).then_inc(G["g_cum"], 1)
            dve.wait_ge(G["g_cum"], 1)
            v.tensor_tensor(EK[:], GC[:, :, :, 4:8], GC[:, :, :, 0:4], ALU.subtract).then_inc(G["g_cum"], 1)
            dve.wait_ge(G["g_exp"], 1)
            link(v.tensor_tensor(BE[:], EG[:], GTOK[:, :, 32:40].rearrange("p t (d h) -> p t d h", d=2), ALU.mult))
            dve.wait_ge(G["g_exp"], 2)
            dve.wait_ge(gdn_in, 16)
            for st in range(2):
                for q in range(4):
                    tl, d, z, tt = q // 2, q % 2, 4 * st + q, 2 * st + q // 2
                    tok = slice(st * SEQ + tl * P, st * SEQ + (tl + 1) * P)
                    dve.wait_ge(G["gb_r"], z + 1)
                    for h in range(HEADS):
                        last = v.scalar_tensor_tensor(DT[:, h, :], bank(0, 4, P)[:, h, :], GC[:, tt, d, h:h + 1], gtab("neg", d), ALU.subtract, ALU.add)
                    last.then_inc(G["gb_d"], 1)
                    dve.wait_ge(G["gb_e"], 2 * z + 1)
                    v.tensor_tensor(ATT[:, q, :, :], bank(3, 4, P), DT[:], ALU.mult)
                    link(v.tensor_tensor(DT[:], DT[:], bank(1, 4, P), ALU.mult))
                    v.tensor_tensor(AT[:, q, :, :], bank(2, 4, P), DT[:], ALU.mult)
                    dve.wait_ge(G["gb_e"], 2 * z + 2)
                    for c in range(2):
                        e = 64 * c + (63 if d == 0 else 0)
                        v.tensor_copy(GEND[:, d, 2 * tl + c, :], ER[:, :, e])
                    v.tensor_tensor(q_decayed(st, q), QKV[:, 0:HEADS, tok], ER[:], ALU.mult).then_inc(G["gb_at"], 1)
                for tl in range(2):
                    y = 2 * st + tl
                    dve.wait_ge(G["gv_t"], y + 1)
                    for d in range(2):
                        for h in range(HEADS):
                            k = bank(5, 4, P)[:, h, :]
                            v.tensor_scalar(KBG[:, 2 * tl + d, h, :], k, BE[:, y, d, h:h + 1], None, ALU.mult)
                            last = v.tensor_scalar(KD[:, 2 * tl + d, h, :], k, EK[:, y, d, h:h + 1], None, ALU.mult)
                    last.then_inc(G["gv_k"], 1)
                eye = ID[:].unsqueeze(1).to_broadcast([P, HEADS, P])
                for k, (lev, q) in enumerate(LEVELS):
                    b = k % 2
                    if lev == 0:
                        dve.wait_ge(G["lv_m"], 24 * st + k + 1)
                        v.tensor_tensor(TT[:, q, :, :], eye, bank(b, 4, P), ALU.subtract)
                        v.tensor_tensor(TU[:, q, :, :], eye, CT[:, b, :, :], ALU.subtract).then_inc(G["lv_tu"], 1)
                    else:
                        dve.wait_ge(G["lv_x"], 20 * st + k - 3)
                        if lev < 5:
                            v.tensor_tensor(TT[:, q, :, :], TT[:, q, :, :], bank(2 + 2 * b, 4, P), ALU.subtract)
                        v.tensor_tensor(TU[:, q, :, :], TU[:, q, :, :], bank(3 + 2 * b, 4, P), ALU.subtract).then_inc(G["lv_tu"], 1)
                for q in range(4):
                    dve.wait_ge(G["uw_ready"], 4 * st + q + 1)
                    v.tensor_copy(WT[:, q, :, :], bank(3 + 2 * (q % 2), 4, P)).then_inc(G["w_out"], 1)
                dve.wait_ge(G["u_out"], 4 * st + 4)
                dve.wait_ge(G["s_init"], 1)
                for k in range(4):
                    n = 4 * st + k
                    for d in range(2):
                        _, q, po = chunk_place(st, k, d)
                        half = slice(po, po + 64)
                        dve.wait_ge(sc_w[d], n + 1)
                        v.tensor_tensor(VN[half, d, :, :], UU[half, q, :, :], bank(d, 4, P)[half], ALU.subtract).then_inc(sc_v[d], 1)
                    for d in range(2):
                        c, _, _ = chunk_place(st, k, d)
                        dve.wait_ge(sc_s[d], n + 1)
                        o = QKV[:, 8:12, st * SEQ + c * 64:st * SEQ + (c + 1) * 64]
                        new = BK[4 + d][:, 0:256].rearrange("p (h t) -> p h t", h=HEADS)
                        if k < 2:
                            v.tensor_copy(o, new)
                        else:
                            v.tensor_tensor(o, o, new, ALU.add)
                        for h in range(HEADS):
                            last = v.scalar_tensor_tensor(S[:, d, h, :], S[:, d, h, :], GEND[:, d, c, h:h + 1], bank(2 + d, 4, P)[:, h, :], ALU.mult, ALU.add)
                        last.then_inc(sc_state[d], 1)
            for h in range(4):
                dve.wait_ge(G["on_std"], h + 1)
                b = h % 2
                link(v.reciprocal(ST2[:, b, :], ST2[:, b, :]))
                link(v.scalar_tensor_tensor(QKV[:, 8 + h, :], QKV[:, 8 + h, :], col("b_norm"), ST2[:, b, :], ALU.mult, ALU.mult))
                v.tensor_tensor(QKV[:, 8 + h, :], QKV[:, 8 + h, :], GATE[:, h, :], ALU.mult).then_inc(G["on_y"], 1)
            for h in range(4):
                dve.wait_ge(G["on_hi"], h + 1)
                v.tensor_tensor(HL[:, 4 + h, :], QKV[:, 8 + h, :], HH[:, 4 + h, :], ALU.subtract).then_inc(G["y_b"], 1)
            wide = STD[:].unsqueeze(1).to_broadcast([P, 4, T2])
            dve.wait_ge(G["ln_mean"], 1)
            v.tensor_tensor(UV[:, 4:8, :], UV[:, 4:8, :], wide, ALU.subtract).then_inc(G["ln_x"], 1)
            dve.wait_ge(G["ln_std"], 1)
            link(v.reciprocal(STD[:], STD[:]))
            v.tensor_tensor(UV[:, 4:8, :], UV[:, 4:8, :], wide, ALU.mult).then_inc(G["ln_n"], 1)
            for t in range(4):
                tok = slice(t * P, (t + 1) * P)
                dve.wait_ge(G["sp_s"], t + 1)
                v.tensor_tensor(UV[:, 0:4, tok], UV[:, 0:4, tok], bank(2 + t % 2, 4, P), ALU.mult).then_inc(G["sp_y"], 1)
            for t in range(4):
                tok = slice(t * P, (t + 1) * P)
                dve.wait_ge(G["sp_hi"], t + 1)
                v.tensor_tensor(HL[:, 0:4, tok], UV[:, 0:4, tok], HH[:, 0:4, tok], ALU.subtract).then_inc(G["y_a"], 1)

            def project(name, width=None, loops=2):
                with dve.Fori(0, loops) as i:
                    for s in range(4):
                        low(B0[name] + s + lead(name), 4 * i)
                        if width:
                            add(name, s, width, i, 4)

            def up(layer, ah, al, width):
                name = f"up{layer}"
                cv, taps = 12 + 2 * FC * layer, COL_AT["fconv"] + 2 * FC * 3 * layer
                ahf, alf = ah[:].rearrange("p a b -> p (a b)"), al[:].rearrange("p a b -> p (a b)")
                def more(s, i):
                    low(B0[name] + s + lead(name), 4 * i)

                def outer_taps(s, i):
                    conv(T0[name] + s, s, cv, taps, width, i, 4)

                def gated(p, i):
                    dve.wait_ge(silu_done, 12 + FC * layer + p + 1 + 2 * i)
                    dve.wait_ge(conv_done, cv + 2 * p + 4 + 4 * i)
                    v.tensor_tensor(A32[:, 0:width], SG[:, 0:width], C1[:, 1, 0:width], ALU.mult).then_inc(act_done, 1)

                def low_part(p, i):
                    dve.wait_ge(act_hi, FC * layer + p + 1 + 2 * i)
                    o = ds(p * width + 2 * width * i, width)
                    v.tensor_tensor(alf[:, o], A32[:, 0:width], ahf[:, o], ALU.subtract).then_inc(act_lo, 1)

                with dve.Fori(0, FC // 2) as i:
                    outer_taps(0, i)
                    more(0, i)
                    outer_taps(1, i)
                    more(1, i)
                    gated(0, i)
                    outer_taps(2, i)
                    low_part(0, i)
                    more(2, i)
                    outer_taps(3, i)
                    gated(1, i)
                    more(3, i)
                    low_part(1, i)

            def down(layer, width):
                name = f"dn{layer}"
                with dve.Fori(0, 2) as i:
                    for m in range(4):
                        for k in range(3):
                            low(B0[name] + 3 * m + k + lead(name), 12 * i)
                        add(name, m, width, i, 4)

            def rest(name):
                for b in range(next(n for s, n, _ in STAGES if s == name)):
                    low(B0[name] + b + lead(name))

            project("out0", T2)
            dve.wait_ge(a_used, 52)
            modulation(1, 40, 12).then_inc(mod_ready, 1)
            dve.wait_ge(mod_ready, 3)
            norm("n2_0")
            up(0, AH0, AL0, T2)
            dve.wait_ge(a_used, A_ALL)
            link(modulation(5, 52, 44))
            gains(1, 0)
            gains(1, 1).then_inc(mod_ready, 1)
            dve.wait_ge(mod_ready, 4)
            down(0, T2)

            norm("n1_1")
            low(B0["in1"] + 2)
            rest("in1")
            norm("cq")
            norm("ckv")
            rest("uq")
            rest("ukv_k")
            rest("ukv_v")

            def rotate(tiles, r0):
                for i, (x, _, which) in enumerate(tiles):
                    cos, sin = ("cm", "sm") if which == "m" else ("c" + which, "s" + which)
                    dve.wait_ge(A["rp_m"], r0 + i + 1)
                    v.tensor_tensor(RT[:, i % 2, :], BK[2 + i % 2][:, 0:SEQ], ltab(sin), ALU.mult)
                    link(v.tensor_tensor(x, x, ltab(cos), ALU.mult))
                    v.tensor_tensor(x, x, RT[:, i % 2, :], ALU.add).then_inc(A["rp_d"], 1)

            dve.wait_ge(late_in, 16)
            rotate(ROPE1, 0)

            def attend(ly, out_bank, out_chunks, mask=None):
                for a in range(ly.steps):
                    w = ly.kt * P
                    if a < ly.n:
                        r = a % 3
                        src = ly.banks[a % len(ly.banks)][:, 0:w]
                        dve.wait_ge(A["at_s"], ly.a0 + a + 1)
                        if ly.masked:
                            link(v.scalar_tensor_tensor(SX[:, a % 2, :], src, ly.scale, mask(a % 2), ALU.mult, ALU.add))
                            src = SX[:, a % 2, :]
                        link(v.tensor_reduce(SM[:, 16 + r:17 + r], src, AX.X, ALU.max))
                        v.tensor_scalar(SM[:, 20 + r:21 + r], SM[:, 16 + r:17 + r], -1.0 if ly.masked else -ly.scale, None, ALU.mult).then_inc(A["at_m"], 1)
                    if 1 <= a <= ly.n:
                        p = a - 1
                        r = p % 3
                        dve.wait_ge(A["at_p"], ly.a0 + p + 1)
                        if ly is DIL:
                            link(v.scalar_tensor_tensor(PB[:, r, 0:w], PB[:, r, 0:w], 1.0, ltab("dcnt", p % 2), ALU.mult, ALU.mult, accum_out=SM[:, 24 + r:25 + r]))
                        link(v.reciprocal(SM[:, 28 + r:29 + r], SM[:, 24 + r:25 + r]))
                        v.tensor_scalar(PB[:, r, 0:w], PB[:, r, 0:w], SM[:, 28 + r:29 + r], None, ALU.mult).then_inc(A["at_n"], 1)
                    if a >= ly.lag and (a - ly.lag) % ly.per == 0:
                        e = (a - ly.lag) // ly.per
                        dve.wait_ge(A["at_hi"], ly.e0 + e + 1)
                        v.tensor_tensor(out_chunks(HL, e), out_bank(e), out_chunks(HH, e), ALU.subtract).then_inc(A["at_y"], 1)

            attend(MLA, lambda e: BK[4 + e % 2][:, 0:SEQ], lambda h, e: h[:, e, LAT])
            project("out1", SEQ)
            norm("n2_1")
            up(1, AH1, AL1, SEQ)
            down(1, SEQ)
            norm("final1")

            norm("mix")
            project("in2", None, 5)
            low(B0["in2"] + 20 + lead("in2"))
            low(B0["in2"] + 21 + lead("in2"))
            rest("in2_v")
            norm("kv2")
            rotate(ROPE2, len(ROPE1))
            dve.wait_ge(A["we_t"], 1)
            v.tensor_scalar(WE[:], BK[4][:, 0:16].rearrange("p (t h) -> p t h", t=2), 8 ** -0.5 * 64 ** -0.5, None, ALU.mult).then_inc(A["we_ready"], 1)
            dve.wait_ge(A["we_ready"], 1)
            for j in range(16):
                qt, h = j // 8, j % 8
                dve.wait_ge(A["ix_r"], j + 1)
                if j:
                    dve.wait_ge(A["ix_a"], j)
                if h == 0:
                    ins = v.tensor_scalar(IX[:, qt, :], RL[:, j % 2, :], WE[:, qt, h:h + 1], None, ALU.mult)
                else:
                    ins = v.scalar_tensor_tensor(IX[:, qt, :], RL[:, j % 2, :], WE[:, qt, h:h + 1], IX[:, qt, :], ALU.mult, ALU.add)
                ins.then_inc(A["ix_a"], 1)
            dve.wait_ge(A["ix_a"], 16)
            causal = LTAB[:, LATE_AT["causal"]:LATE_AT["causal"] + 2 * SEQ].rearrange("p (t k) -> p t k", t=2)
            link(v.tensor_tensor(IX[:], IX[:], causal, ALU.add))
            for r in range(8):
                v.max(M8[:, 0, :], IX[:, 0, :])
                link(v.max(M8[:, 1, :], IX[:, 1, :]))
                v.match_replace(IX[:, 0, :], M8[:, 0, :], IX[:, 0, :], TAKEN)
                link(v.match_replace(IX[:, 1, :], M8[:, 1, :], IX[:, 1, :], TAKEN))
            link(v.tensor_scalar(AM[:], IX[:], -2e38, NEG, ALU.is_gt, ALU.mult))
            link(v.tensor_tensor(AM[:], AM[:], causal, ALU.add))
            attend(DSA, lambda e: PL[e % 2][:, 0:SEQ], lambda h, e: h[:, e, LAT], lambda qt: AM[:, qt, :])
            attend(DIL, lambda e: BK[4 + e % 2][:, 0:SEQ], lambda h, e: h[:, 4 + e, LAT], lambda qt: ltab("dneg", qt))
            project("out2", SEQ)
            norm("cross")
            norm("mem")
            project("xq")
            project("xk")
            rest("xv")
            attend(CRS, lambda e: BK[4 + e % 2][:, 0:512].rearrange("p (c q) -> p c q", c=2), lambda h, e: h[:, 2 * e:2 * e + 2, LAT])
            project("xo", SEQ)
            norm("mlp")
            ahf, alf = AH2[:].rearrange("p a b -> p (a b)"), AL2[:].rearrange("p a b -> p (a b)")
            with dve.Fori(0, 8) as i:
                for s in range(4):
                    low(B0["up2"] + s + lead("up2"), 4 * i)
                    dve.wait_ge(tile_out, T0["up2"] + s + 3 + 4 * i)
                    half = slice(s % 2 * SEQ, (s % 2 + 1) * SEQ)
                    v.tensor_tensor(A32[:, half], C1[:, s % 2, 0:SEQ], C1[:, s % 2, 0:SEQ], ALU.mult).then_inc(act_done, 1)
                    dve.wait_ge(act_done, 2 * FC + s + 1 + 4 * i)
                    dve.wait_ge(act_hi, 2 * FC + s + 1 + 4 * i)
                    o = ds(s * SEQ + 4 * SEQ * i, SEQ)
                    v.tensor_tensor(alf[:, o], A32[:, half], ahf[:, o], ALU.subtract).then_inc(act_lo, 1)

            with dve.Fori(0, 3) as i:
                for m in range(2):
                    for k in range(4):
                        low(B0["dn2"] + 4 * m + k + lead("dn2"), 8 * i)
                    add("dn2", m, SEQ, i, 2)
            for m in (6, 7):
                for k in range(4):
                    low(B0["dn2"] + 4 * m + k + lead("dn2"))
                add("dn2", m, SEQ)
            norm("final2")


def kernel(**inputs):
    import numpy as np
    import concourse.bacc as bacc
    from concourse.bass_utils import run_bass_kernel_spmd

    arrays = {k: np.ascontiguousarray(v) for k, v in lay_out({k: np.asarray(v) for k, v in inputs.items()}).items()}
    nc = bacc.Bacc("TRN2", target_bir_lowering=False, num_devices=1)
    args = [nc.dram_tensor(k, v.shape, mybir.dt.float32, kind="ExternalInput").ap() for k, v in arrays.items()]
    out = nc.dram_tensor("out", (P, KC, SEQ), mybir.dt.float32, kind="ExternalOutput").ap()
    two_blocks_kernel(nc, *args, out)
    r = run_bass_kernel_spmd(nc, [arrays], core_ids=[0])
    y = r.results[0]["out"]
    return np.ascontiguousarray(y.transpose(2, 1, 0).reshape(1, SEQ, D))
```

```python
from contextlib import ExitStack

import concourse.bass as bass
from concourse import mybir

P = 128
D = 1024
KC = D // P
SEQ = 256
T2 = 2 * SEQ
D_FF = 2816
FC = D_FF // P
D_FF_2 = 4096
HEADS = 4
EPS = 1e-6
NEG = -1e30
TAKEN = -3e38
BLOCK_CHUNKS = 8
BLOCK = BLOCK_CHUNKS * P

COLS = [("cond", 2 * KC), ("ada_b", 96), ("norm1", 16), ("norm2", 16), ("bconv", 36), ("dt_bias", 1), ("a_log", 1),
        ("a_ln_g", 4), ("a_ln_b", 4), ("b_norm", 1), ("mla_q", 3), ("mla_kv", 2), ("fconv", 2 * 2 * FC * 3),
        ("final1", 8), ("mix", 8), ("kv2", 1), ("cross", 8), ("mem", 8), ("mlp", 8), ("final2", 8), ("eps", 1), ("one", 1)]
COL_AT = {}
_n = 0
for _name, _w in COLS:
    COL_AT[_name] = _n
    _n += _w
NCOLS = _n

GDN_TABLES = [("cum", 2 * P), ("blk", P), ("neg", 2 * P), ("lev", 12 * P)]
LATE_TABLES = [("perm64", P), ("perm32", P), ("cm", SEQ), ("sm", SEQ), ("c64", SEQ), ("s64", SEQ), ("c32", SEQ),
               ("s32", SEQ), ("causal", 2 * SEQ), ("dneg", 2 * SEQ), ("dcnt", 2 * SEQ)]
GDN_AT, LATE_AT = {}, {}
_n = 0
for _name, _w in GDN_TABLES:
    GDN_AT[_name] = _n
    _n += _w
NGDN = _n
_n = 0
for _name, _w in LATE_TABLES:
    LATE_AT[_name] = _n
    _n += _w
NLATE = _n

STAGES = [("in0", 25, 25), ("out0", 8, 8), ("up0", 44, 44), ("dn0", 24, 8), ("in1", 6, 6), ("uq", 5, 12), ("ukv_k", 2, 8),
          ("ukv_v", 2, 8), ("out1", 8, 8), ("up1", 44, 44), ("dn1", 24, 8), ("in2", 22, 22), ("in2_v", 4, 2), ("xk", 8, 8),
          ("xv", 8, 4), ("out2", 8, 8), ("xq", 8, 8), ("xo", 8, 8), ("up2", 32, 32), ("dn2", 32, 8)]
B0, T0 = {}, {}
_b = _t = 0
for _name, _nb, _nt in STAGES:
    B0[_name], T0[_name] = _b, _t
    _b += _nb
    _t += _nt
NBLK = _b

NORMS = [("n1_0", 8, T2), ("n2_0", 8, T2), ("n1_1", 8, T2), ("cq", 3, SEQ), ("ckv", 2, T2), ("mem", 8, SEQ), ("n2_1", 8, SEQ), ("final1", 8, SEQ),
         ("mix", 8, SEQ), ("kv2", 1, SEQ), ("cross", 8, SEQ), ("mlp", 8, SEQ), ("final2", 8, SEQ)]
NORM_I = {n: i for i, (n, _, _) in enumerate(NORMS)}
SPLIT = {"n1_0", "n2_0", "n1_1", "cq", "ckv", "n2_1", "mix", "cross", "mem", "mlp"}
MODULATED = {"n1_0": (0, 0), "n2_0": (0, 3), "n1_1": (1, 0), "n2_1": (1, 3)}
NORM_C0, NORM_S0 = {}, {}
_c = _s = 0
for _name, _nc, _ in NORMS:
    NORM_C0[_name], NORM_S0[_name] = _c, _s
    _c += _nc
    _s += _nc if _name in SPLIT else 0

RES = {n: 8 * i for i, n in enumerate(["out0", "dn0", "out1", "dn1", "out2", "xo", "dn2"])}

A_FIRST = 16
A_ALL = 96


def tables():
    import numpy as np
    f = np.float32
    j, i = np.arange(P)[:, None], np.arange(P)[None, :]
    same = (j // 64) == (i // 64)
    cum = [same & (j <= i), same & (j >= i)]
    lev = []
    for d in range(2):
        for s in (1, 2, 4, 8, 16, 32):
            pair = (j // (2 * s)) == (i // (2 * s))
            lo, hi = (j // s) % 2, (i // s) % 2
            lev.append(pair & ((lo == 0) & (hi == 1) if d == 0 else (lo == 1) & (hi == 0)))
    gdn = np.concatenate([c.astype(f) for c in cum] + [same.astype(f)] + [np.where(c, 0, NEG).astype(f) for c in cum]
                         + [m.astype(f) for m in lev], axis=1)

    def perm(w):
        m = np.zeros((P, P), f)
        p = np.arange(P)
        m[(p // w) * w + (p % w + w // 2) % w, p] = 1
        return m

    def rope(ang, w):
        p = np.arange(P) % w
        c, s = np.cos(ang).astype(f), np.sin(ang).astype(f)
        return c.T[p % (w // 2)], s.T[p % (w // 2)] * np.where(p < w // 2, -1, 1).astype(f)[:, None]

    t = np.arange(SEQ, dtype=f)
    inv = (f(10000.0) ** (-np.arange(16, dtype=f) / f(16))).astype(f)
    cm, sm = rope(np.concatenate([np.floor(t / 64)[:, None] * inv, (t % 64)[:, None] * inv], axis=1), 64)
    inv64 = (f(10000.0) ** (-np.arange(0, 64, 2, dtype=f) / f(64))).astype(f)
    inv32 = (f(10000.0) ** (-np.arange(0, 32, 2, dtype=f) / f(32))).astype(f)
    c64, s64 = rope(t[:, None] * inv64, 64)
    c32, s32 = rope(t[:, None] * inv32, 32)
    q, k = np.arange(SEQ)[:, None], np.arange(SEQ)[None, :]
    back = q - k
    count = sum(((back >= 0) & (back <= w) & (back % dil == 0)).astype(f) for w, dil in ((128, 1), (512, 4), (2048, 16)))

    def rows(m):
        return m.reshape(2, P, SEQ).transpose(1, 0, 2).reshape(P, 2 * SEQ).astype(f)

    late = np.concatenate([perm(64), perm(32), cm, sm, c64, s64, c32, s32, rows(np.where(back >= 0, 0, NEG)),
                           rows(np.where(count > 0, 0, NEG)), rows(count)], axis=1).astype(f)
    return gdn, late


def lay_out(a):
    import numpy as np
    f = np.float32
    z = lambda *s: np.zeros(s, f)
    tr = lambda m: np.ascontiguousarray(m.T.reshape(KC, P, -1).transpose(1, 0, 2))

    def tiles(w, pad=0):
        k, m = w.shape
        b = w.reshape(k // P, P, m // P, P).transpose(2, 1, 0, 3)
        if pad:
            b = np.concatenate([b, z(b.shape[0], P, pad, P)], axis=2)
        return b

    def blocks(w, pad=0):
        b = tiles(w, pad)
        m, _, k, _ = b.shape
        if k >= BLOCK_CHUNKS:
            n = k // BLOCK_CHUNKS
            return b.reshape(m, P, n, BLOCK).transpose(0, 2, 1, 3).reshape(m * n, P, BLOCK)
        b = b.transpose(1, 0, 2, 3).reshape(P, m * k, P)
        n = -(-m * k // BLOCK_CHUNKS)
        b = np.concatenate([b, z(P, n * BLOCK_CHUNKS - m * k, P)], axis=1)
        return b.reshape(P, n, BLOCK).transpose(1, 0, 2)

    def moving(w):
        k, m = w.shape
        b = w.reshape(k // 256, 2, P, m // 512, 512).transpose(3, 0, 2, 1, 4)
        return b.reshape(-1, P, BLOCK)

    def wide(w):
        return np.concatenate([w, z(w.shape[0], -w.shape[1] % P)], axis=1)

    wi = a["ab_w_in"][0]
    ab = z(D, P)
    ab[:, 0:8], ab[:, 32:40] = wi[:, 3072:3080], wi[:, 3080:3088]
    pairs = np.array([[j, FC + j] for j in range(FC)]).ravel()
    ffn_cols = (pairs[:, None] * P + np.arange(P)).ravel()
    uq = a["mla_w_uq"][0].reshape(384, 8, 192)
    ukv = a["mla_w_ukv"][0].reshape(256, 8, 256)
    w2 = a["w_in_2"][0]
    mi = a["mla_w_in"][0]
    kvc = a["w_kv_cross_2"][0]
    w_in2 = np.concatenate([w2[:, 0:896], np.tile(w2[:, 896:928], (1, 4)), np.tile(w2[:, 1440:1504], (1, 2)),
                            wide(w2[:, 1504:1512]), w2[:, 928:1440], w2[:, 1512:2536]], axis=1)
    stream = [blocks(np.concatenate([wi[:, 0:3072], ab], axis=1)), blocks(a["ab_w_out"][0]),
              blocks(a["ffn_w_up"][0][:, ffn_cols]), blocks(a["ffn_w_down"][0], 2),
              blocks(np.concatenate([mi, mi[:, 640:704]], axis=1)),
              blocks(np.concatenate([uq[:, :, :128].reshape(384, -1), uq[:, :, 128:].reshape(384, -1)], axis=1)),
              blocks(np.ascontiguousarray(ukv[:, :, :128]).reshape(256, -1)), moving(np.ascontiguousarray(ukv[:, :, 128:]).reshape(256, -1)),
              blocks(a["mla_w_out"][0]), blocks(a["ffn_w_up"][1][:, ffn_cols]), blocks(a["ffn_w_down"][1], 2),
              blocks(w_in2), moving(w2[:, 2536:3048]), blocks(kvc[:, :1024]), moving(kvc[:, 1024:]),
              blocks(a["w_out_2"][0]), blocks(a["w_q_cross_2"][0]), blocks(a["w_o_cross_2"][0]), blocks(a["w_up_2"][0]), blocks(a["w_down_2"][0])]
    assert [len(s) for s in stream] == [n for _, n, _ in STAGES]
    vec = lambda v: v.reshape(-1, P).T
    dt_bias, a_log = z(P, 1), z(P, 1)
    dt_bias[:8, 0], a_log[:8, 0] = a["b_dt_bias"][0].ravel(), a["b_a_log"][0].ravel()
    cols = [np.stack([vec(a["c_ctx"]), vec(a["c"][0])], axis=2).reshape(P, -1),
            np.concatenate([vec(a["ada_b"][i]) for i in range(2)], axis=1),
            np.concatenate([vec(a["norm1_g"][i]) for i in range(2)], axis=1),
            np.concatenate([vec(a["norm2_g"][i]) for i in range(2)], axis=1),
            a["b_conv_w"][0].reshape(3, 12, P).transpose(2, 1, 0).reshape(P, -1), dt_bias, a_log,
            vec(a["a_ln_g"][0]), vec(a["a_ln_b"][0]), vec(a["b_norm_g"][0]), vec(a["mla_q_norm_g"][0]), vec(a["mla_kv_norm_g"][0]),
            np.concatenate([a["ffn_conv_w"][i][:, ffn_cols].reshape(3, 2 * FC, P).transpose(2, 1, 0).reshape(P, -1) for i in range(2)], axis=1),
            vec(a["final_g"]), vec(a["norm_mix_g_2"][0]), vec(a["kv_norm_g_2"][0]), vec(a["norm_cross_g_2"][0]),
            vec(a["norm_mem_g_2"][0]), vec(a["norm_mlp_g_2"][0]), vec(a["norm_final_g_2"]), np.full((P, 1), EPS, f), np.ones((P, 1), f)]
    gdn, late = tables()
    return {
        "x_in": np.concatenate([tr(a["ctx"][0]), tr(a["x"][0])], axis=2),
        "mem_in": tr(a["mem_2"][0]),
        "a_stream": np.concatenate([blocks(a["ada_w"][i]) for i in range(2)]),
        "w_stream": np.concatenate(stream),
        "cols": np.ascontiguousarray(np.concatenate(cols, axis=1)),
        "gdn_tables": gdn, "late_tables": late, "ident": np.eye(P, dtype=f),
        "ws_t": np.ascontiguousarray(a["a_ws"][0].transpose(2, 0, 1)),
        "bs_row": a["a_bs"][0].reshape(1, 512),
        "ln_rows": np.tile(np.concatenate([a["a_ln_g"][0], a["a_ln_b"][0]]), (P, 1)),
        "w_uk": np.ascontiguousarray(a["w_uk_2"][0].reshape(4, P, P).transpose(1, 0, 2)),
        "w_uv": np.ascontiguousarray(a["w_uv_2"][0].transpose(1, 0, 2)),
    }


DONE_BLOCK, DONE_TILE = {}, {}


def count_signals():
    n = 0
    for name, nb, nt in STAGES:
        b, t = B0[name], T0[name]
        if name in ("uq", "ukv_k"):
            per = 3 if name == "uq" else 2
            for m in range(nt):
                n += 1
                DONE_TILE[t + m] = n
                for k in range(nb):
                    if min(8 * k + 7, per * nt - 1) // per == m:
                        DONE_BLOCK[b + k] = n
        elif name == "ukv_v":
            for m in range(nt):
                n += 1
                DONE_TILE[t + m] = n
                DONE_BLOCK[b + m // 4] = n
        elif name in ("in2_v", "xv"):
            for k in range(nb):
                for tok in range(2):
                    n += 1
                    DONE_TILE[t + 2 * (k // 4) + tok] = n
                DONE_BLOCK[b + k] = n
        else:
            for k in range(nb):
                n += 1
                DONE_BLOCK[b + k] = n
                DONE_TILE[t + k * nt // nb] = n


count_signals()


def two_blocks_kernel(nc, x_in, mem_in, a_stream, w_stream, cols, gdn_tables, late_tables, ident, ws_t, bs_row, ln_rows, w_uk, w_uv, out):
    F32, F32R = mybir.dt.float32, mybir.dt.float32r
    ALU, ACT, AX = mybir.AluOpType, mybir.ActivationFunctionType, mybir.AxisListType
    ds = bass.ds
    ctx = ExitStack()
    with ctx:
        base = -(-nc.sbuf_base // 64) * 64
        end = nc.sbuf_usable_end // 32 * 32
        cursor = [base]

        def place(name, shape, dt=F32):
            size = 4
            for s in shape[1:]:
                size *= s
            size = -(-size // 32) * 32
            t = nc.alloc_sbuf_tensor_at(name, shape, dt, offset=cursor[0])
            cursor[0] += size
            assert cursor[0] <= end, (name, cursor[0] - end)
            return t

        RAW = place("w_raw", [P, 4, BLOCK])
        WH = place("w_high", [P, 2, BLOCK], F32R)
        WL = place("w_low", [P, 2, BLOCK], F32R)
        a_ring_at = cursor[0]
        AR = place("a_ring", [P, 2, BLOCK])
        X = place("x", [P, KC, T2])
        C = place("cols_sb", [P, NCOLS])
        MOD = place("mod", [P, 2, 6, KC, 2])
        GM = place("gains", [P, 2, 2, KC, 2])
        ID = place("ident_sb", [P, P])
        ONES = place("ones", [P, P])
        STD = place("std", [P, T2])
        SM = place("small", [P, 72])
        XP = place("conv_in", [P, 2, 2, SEQ + 2])
        tmp_at = cursor[0]
        TMP = place("tmp", [P, KC, T2])
        after_tmp = cursor[0]
        HH = place("h_high", [P, KC, T2], F32R)
        HL = place("h_low", [P, KC, T2], F32R)
        zone = cursor[0]
        cursor[0] = after_tmp
        A16 = place("a_first", [P, A_FIRST, BLOCK])
        MR = place("mod_rows", [2, 4, 512])
        cursor[0] = tmp_at
        C1 = place("conv_mid", [P, 2, T2])
        SG = place("silu_g", [P, T2])
        A32 = place("act", [P, T2])
        TY = place("res", [P, 2, T2])
        cursor[0] = after_tmp
        SQN = place("squares_n1_1", [P, KC, T2])
        cursor[0] = tmp_at
        GA = place("gate_a", [40, T2])
        GB = place("gate_b", [40, T2])
        GT = place("gate_t", [40, T2])
        SQL = place("qk_squares", [P, 4, T2])
        L2 = place("qk_lengths", [P, 2, 32])
        cursor[0] = tmp_at
        CT = place("lev_ct", [P, 2, HEADS, P])
        M1 = place("lev_m1", [P, 2, HEADS, P])
        decay_at = cursor[0]
        DT = place("decay", [P, 2, HEADS, P])
        ER = place("exp_cum", [P, 2, HEADS, P])
        cursor[0] = decay_at
        VN = place("v_new", [P, 2, HEADS, P])
        cursor[0] = decay_at
        ONQ = place("out_squares", [P, HEADS, SEQ])
        cursor[0] = decay_at
        LNR = place("ln_rows_sb", [P, 2, 4, P])
        WS = place("ws_sb", [P, 4, P])
        BS = place("bs_sb", [1, 512])
        cursor[0] = zone
        QKV = place("qkv", [P, 12, T2])
        UV = place("uv", [P, 8, T2])
        GATE = place("gate", [P, 4, T2])
        GTAB = place("gdn_tab", [P, NGDN])
        GTOK = place("g_tok", [P, 4, 40])
        GC = place("g_cum", [P, 4, 2, 8])
        EG = place("e_cum", [P, 4, 2, HEADS])
        EK = place("e_rest", [P, 4, 2, HEADS])
        BE = place("beta_e", [P, 4, 2, HEADS])
        GEND = place("g_end", [P, 2, 4, HEADS])
        TT = place("inv_t", [P, 4, HEADS, P])
        TU = place("inv_u", [P, 4, HEADS, P])
        ATT = place("attn_t", [P, 4, HEADS, P])
        QG0 = place("qg0", [P, 2, HEADS, P])
        S = place("state", [P, 2, HEADS, P])
        cursor[0] = after_tmp
        VB = place("v_beta", [P, 4, HEADS, P])
        KBG = place("k_beta_g", [P, 4, HEADS, P])
        KD = place("k_decay", [P, 4, HEADS, P])
        AT = place("a_t", [P, 4, HEADS, P])
        UU, WT = AT, TT
        cursor[0] = zone
        TYO = place("res_out0", [P, 2, T2])
        cursor[0] = zone
        AH0 = place("act_high0", [P, FC, T2], F32R)
        AL0 = place("act_low0", [P, FC, T2], F32R)
        cursor[0] = zone
        LTAB = place("late_tab", [P, NLATE])
        late = cursor[0]
        CQ = place("cq", [P, 3, SEQ])
        CKV = place("ckv", [P, 2, T2])
        KR = place("kr", [P, T2])
        MQ = place("mla_q", [P, 12, SEQ])
        KN = place("mla_k", [P, 8, T2])
        VT = place("mla_v", [P, 4, 1024])
        CQH = place("cq_high", [P, 3, SEQ], F32R)
        CQL = place("cq_low", [P, 3, SEQ], F32R)
        CKH = place("ckv_high", [P, 2, T2], F32R)
        CKL = place("ckv_low", [P, 2, T2], F32R)
        cursor[0] = late
        AH1 = place("act_high1", [P, FC, SEQ], F32R)
        AL1 = place("act_low1", [P, FC, SEQ], F32R)
        cursor[0] = late
        PJ = place("proj", [P, 22, SEQ])
        VBK = place("dil_v", [P, 2, 512])
        CTK = place("c_tok", [P, 2, P])
        QL = place("q_lat", [P, 8, SEQ])
        OL = place("o_lat", [P, 2, SEQ])
        IX = place("index", [P, 2, SEQ])
        RL = place("relu", [P, 2, SEQ])
        AM = place("top_mask", [P, 2, SEQ])
        WE = place("w_eff", [P, 2, 8])
        M8 = place("max8", [P, 2, 8])
        WUK = place("w_uk_sb", [P, 4, P])
        WUV = place("w_uv_sb", [P, 8, 64])
        KCR = place("cross_k", [P, 8, SEQ])
        VC = place("cross_v", [P, 2, 1024])
        cursor[0] = late
        QC = place("cross_q", [P, 8, SEQ])
        cursor[0] = late
        AH2 = place("act_high2", [P, 32, SEQ], F32R)
        AL2 = place("act_low2", [P, 32, SEQ], F32R)
        late_end = end - 2 * BLOCK * 4
        cursor[0] = a_ring_at
        WH2 = place("w_high2", [P, 2, BLOCK], F32R)
        cursor[0] = late_end
        WL2 = place("w_low2", [P, 2, BLOCK], F32R)
        cursor[0] = tmp_at
        PB = place("probs", [P, 3, T2])
        PT = place("probs_t", [P, 2, 4, P])
        SX = place("scores", [P, 2, SEQ])
        RT = place("rot", [P, 2, SEQ])

        def slot(n):
            late_block = n - B0["in1"]
            return n % 2 if late_block < 0 else (B0["in1"] % 2, 1 - B0["in1"] % 2, 2, 3)[late_block % 4]

        def slot_before(n):
            late_block = n - B0["in1"]
            return n - 2 if late_block < 2 else B0["in1"] - 1 if late_block < 4 else n - 4

        def lead(name):
            return 2 if B0[name] < B0["in1"] else 3

        def wh(n):
            return WH[:, slot(n), :] if slot(n) < 2 else WH2[:, slot(n) - 2, :]

        def wl(n):
            return WL[:, slot(n), :] if slot(n) < 2 else WL2[:, slot(n) - 2, :]

        PL = [ctx.enter_context(nc.psum_tensor(f"proj{i}", [P, 512], F32)) for i in range(2)]
        BK = [ctx.enter_context(nc.psum_tensor(f"bank{i}", [P, 512], F32)) for i in range(6)]

        MROWS = [BK[1], BK[5], PL[0], PL[1]]
        ROWS = [(BK[0], BK[1]), (PL[0], PL[1])]
        SUMS = [BK[i] for i in (0, 2, 3, 4)]

        def bank(i, a, b):
            return BK[i][:, 0:a * b].rearrange("p (a b) -> p a b", a=a)

        def col(name, j=0):
            return C[:, COL_AT[name] + j:COL_AT[name] + j + 1]

        def gtab(name, j=0):
            return GTAB[:, GDN_AT[name] + j * P:GDN_AT[name] + (j + 1) * P]

        def ltab(name, j=0, w=SEQ):
            return LTAB[:, LATE_AT[name] + j * w:LATE_AT[name] + (j + 1) * w]

        def sem(name):
            return ctx.enter_context(nc.semaphore(name))

        cols_in, x_ready, gdn_in, ws_in, late_in, uk_in, mem_ready, out_done = map(
            sem, ("cols_in", "x_ready", "gdn_in", "ws_in", "late_in", "uk_in", "mem_ready", "out_done"))
        a_first = [sem(f"a_first{i}") for i in range(4)]
        w_landed = [sem(f"w_landed{i}") for i in range(4)]
        a_landed = [sem(f"a_landed{i}") for i in range(2)]
        w_high, w_low, pe_done, tile_out, a_used = map(sem, ("w_high_ready", "w_low_ready", "pe_done", "tile_out", "a_used"))
        cond_ready, mod_ready, init, m_sum, m_rows = map(sem, ("cond_ready", "mod_ready", "init", "m_sum", "m_rows"))
        n_sq, n_ss, n_root, n_std, n_bc, n_xn, n_hi, n_lo = map(sem, ("n_sq", "n_ss", "n_root", "n_std", "n_bc", "n_xn", "n_hi", "n_lo"))
        x_res = sem("x_res")
        conv_mid, conv_done, silu_done, act_done, act_hi, act_lo = map(sem, ("conv_mid", "conv_done", "silu_done", "act_done", "act_hi", "act_lo"))
        dve_step, act_step = sem("dve_step"), sem("act_step")
        names = ("l2_sq l2_ss l2_root l2_std l2_bc l2_done g_rows g_in g_soft g_tr g_tok g_cs g_cum g_exp g_be gb_r gb_d gb_e gb_at gb_q gb_k "
                 "gv_t gv_vb gv_k lv_ct lv_m lv_m1 lv_x lv_tu uw_ready u_out w_out s_init on_sq on_ss on_root on_std on_bc on_n on_y on_hi y_b "
                 "vt_t vt_out ln_mean ln_sq ln_std ln_r ln_n ln_g ln_v sp_s sp_y sp_hi y_a").split()
        G = {n: sem(n) for n in names}
        sc_w, sc_v, sc_s, sc_state = ([sem(f"{n}{d}") for d in range(2)] for n in ("scan_w", "scan_v", "scan_s", "scan_state"))
        names = ("rp_m rp_d at_s at_m at_p at_n at_t at_pt at_o at_hi at_y ol_out ol_o ix_l ix_r ix_a am_ready we_t we_ready ct_t ct_out "
                 "ql_m ql_out").split()
        A = {n: sem(n) for n in names}

        class Layer:
            def __init__(self, name, heads, key_tiles, per_group, a0, e0, masked, scale):
                self.name, self.heads, self.kt, self.per, self.a0, self.e0 = name, heads, key_tiles, per_group, a0, e0
                self.n, self.masked, self.scale = 2 * heads, masked, scale
                self.groups = self.n // per_group
                self.banks = BK[0:2] if masked else [BK[0], BK[1], PL[0]]
                self.lag = per_group + (5 if name == "dsa" else 3)
                self.steps = self.n - per_group + self.lag + 1

        MLA = Layer("mla", 8, 4, 2, 0, 0, False, 192 ** -0.5)
        DSA = Layer("dsa", 8, 2, 4, 16, 8, True, 96 ** -0.5)
        DIL = Layer("dil", 8, 2, 4, 32, 12, True, 64 ** -0.5)
        CRS = Layer("cross", 4, 2, 2, 48, 16, False, 256 ** -0.5)
        LAT = slice(SEQ, T2)
        CTX = slice(0, SEQ)
        ROPE1 = [(MQ[:, 8 + i, :], T0["uq"] + 8 + i, "m") for i in range(4)] + [(KR[:, LAT], T0["in1"] + 5, "m")]
        ROPE2 = [(PJ[:, i, :], T0["in2"] + i, "32" if i in (4, 5, 7) else "64") for i in (10, 11, 12, 13, 8, 4, 5, 7, *range(14, 22))]
        SIDE = 16
        ROTATE_AT = {j: [r for r in (2 * j, 2 * j + 1) if r < len(ROPE2)] for j in range(SIDE)}
        INDEX_AT, TOP_AT, LATENT_AT = range(4, 8), range(8, 16), range(10, 14)

        def chunk_place(st, k, d):
            c = k if d == 0 else 3 - k
            return c, (c // 2) * 2 + d, 64 * (c % 2)

        def q_decayed(st, q):
            tl, d = q // 2, q % 2
            at = st * SEQ + tl * P
            return QG0[:, tl, :, :] if d == 0 else QKV[:, 0:HEADS, at:at + P]

        def squares(name, k):
            width = NORMS[NORM_I[name]][2]
            if name == "n1_1":
                return SQN[:, k, :]
            return TMP[:, k, :] if width == T2 else TMP[:, k, SEQ:T2]

        TURNS = [(3, 6), (13, 16)]
        LEVELS = [(lev, q) for lev in range(6) for q in range(4)]
        block = ctx.enter_context(nc.Block())

        @block.tensor
        def _(pe):
            mm = nc.tensor.matmul

            def mm3(out_, wh, wl, xh, xl, first, last):
                mm(out_, wh, xh, start=first, stop=False)
                mm(out_, wh, xl, start=False, stop=False)
                return mm(out_, wl, xh, start=False, stop=last)

            def weights(n, off=0):
                pe.wait_ge(w_low, n + 1 + off)

            def free_bank(t, off=0):
                pe.wait_ge(tile_out, t + 1 + off)

            def tile(n, t, x, width, off=0, ready=None):
                weights(n, off)
                free_bank(t, off)
                for k in range(KC):
                    if ready:
                        pe.wait_ge(*ready(k))
                    w = slice(k * P, (k + 1) * P)
                    last = mm3(PL[t % 2][:, 0:width], wh(n)[:, w], wl(n)[:, w], HH[:, k, x], HL[:, k, x], k == 0, k == KC - 1)
                last.then_inc(pe_done, 1)

            def h_ready(name):
                return lambda k: (n_lo, NORM_S0[name] + k + 1)

            def mod_tile(w, out_, inc=True):
                for k in range(KC):
                    last = mm(out_, w[:, k * P:(k + 1) * P], C[:, COL_AT["cond"] + 2 * k:COL_AT["cond"] + 2 * k + 2], start=(k == 0), stop=(k == KC - 1))
                last.then_inc(a_used, 1)

            def ring_mod_tile(m, b, at, it=0, per=0):
                pe.wait_ge(a_landed[m % 2], 16 * ((m - A_FIRST) // 2 + 1) + 8 * per * it)
                mod_tile(AR[:, m % 2, :], BK[b][:, ds(2 * (m - at) + 2 * per * it, 2)])

            def norm_sum(name):
                _, nch, width = NORMS[NORM_I[name]]
                for k in range(nch):
                    pe.wait_ge(n_sq, NORM_C0[name] + k + 1)
                    for t in range(width // P):
                        last = mm(SUMS[t][:, 0:1], squares(name, k)[:, t * P:(t + 1) * P], ONES[:, 0:1], start=(k == 0), stop=(k == nch - 1))
                last.then_inc(n_ss, 1)

            def norm_spread(name):
                pe.wait_ge(n_std, NORM_I[name] + 1)
                for t in range(NORMS[NORM_I[name]][2] // P):
                    last = mm(BK[0][:, t * P:(t + 1) * P], STD[:, 8 + t:9 + t].to_broadcast([P, P]), ID[:], start=True, stop=True)
                last.then_inc(n_bc, 1)

            def norm(name):
                norm_sum(name)
                norm_spread(name)

            pe.wait_ge(init, 1)
            norm_sum("n1_0")
            pe.wait_ge(cond_ready, 1)
            for g in range(4):
                pe.wait_ge(a_first[g], 16)
                for k in range(KC):
                    at = COL_AT["cond"] + 2 * k
                    last = mm(MROWS[g][0:2, :].rearrange("p (m n) -> p m n", m=4), C[:, at:at + 2], A16[:, 4 * g:4 * g + 4, k * P:(k + 1) * P], start=(k == 0), stop=(k == KC - 1))
                last.then_inc(m_sum, 1)
            pe.wait_ge(cols_in, 32)
            for m in range(A_FIRST):
                pe.wait_ge(m_rows, m // 4 + 1)
                nc.tensor.transpose(BK[1][:, 2 * m:2 * m + 2], MR[0:2, m // 4, m % 4 * P:(m % 4 + 1) * P], ID[0:2, 0:2]).then_inc(a_used, 1)
            norm_spread("n1_0")

            with pe.Fori(0, 5) as i:
                for s in range(4):
                    tile(s, s, slice(0, T2), T2, 4 * i, h_ready("n1_0") if s == 0 else None)
                    ring_mod_tile(16 + s, 5, 16, i, 4)

            def lengths(j):
                pe.wait_ge(G["l2_sq"], j + 1)
                for t in range(4):
                    last = mm(BK[0][:, 8 * t + j:8 * t + j + 1], SQL[:, j % 4, t * P:(t + 1) * P], ONES[:, 0:1], start=True, stop=True)
                last.then_inc(G["l2_ss"], 1)

            for t in range(20, 24):
                tile(t, t, slice(0, T2), T2)
                ring_mod_tile(16 + t, 5, 16)
                if t in (20, 22):
                    for j in range(2 * (t - 20), 2 * (t - 20) + 4):
                        lengths(j)
            tile(24, 24, slice(0, T2), T2)

            pe.wait_ge(G["l2_std"], 1)
            for j in range(8):
                if j >= 4:
                    pe.wait_ge(G["l2_done"], j - 3)
                for t in range(4):
                    last = mm(BK[1 + j % 4][:, t * P:(t + 1) * P], L2[:, 1, 8 * t + j:8 * t + j + 1].to_broadcast([P, P]), ID[:], start=True, stop=True)
                last.then_inc(G["l2_bc"], 1)
            pe.wait_ge(G["g_soft"], 1)
            for t in range(4):
                last = nc.tensor.transpose(BK[0][:, 40 * t:40 * t + 40], GT[0:40, t * P:(t + 1) * P], ID[0:40, 0:40])
            last.then_inc(G["g_tr"], 1)
            pe.wait_ge(G["g_tok"], 1)
            pe.wait_ge(gdn_in, 16)
            pe.wait_ge(mod_ready, 2)
            for t in range(4):
                for d in range(2):
                    o = BK[5][:, (2 * t + d) * 8:(2 * t + d) * 8 + 8]
                    mm(o[:, 0:4], gtab("cum", d), GTOK[:, t, 4 * d:4 * d + 4], start=True, stop=True)
                    last = mm(o[:, 4:8], gtab("blk"), GTOK[:, t, 4 * d:4 * d + 4], start=True, stop=True)
            last.then_inc(G["g_cs"], 1)
            pe.wait_ge(G["l2_done"], 8)
            pe.wait_ge(tile_out, 27)

            def values_keys(st, k):
                if k in TURNS[st]:
                    tl = TURNS[st].index(k)
                    tok = slice(st * SEQ + tl * P, st * SEQ + (tl + 1) * P)
                    if tl:
                        pe.wait_ge(G["gv_vb"], 2 * (2 * st + tl))
                        pe.wait_ge(G["gv_k"], 2 * (2 * st + tl))
                    elif st:
                        pe.wait_ge(G["on_n"], 2)
                    for h in range(HEADS):
                        nc.tensor.transpose(PL[0][:, h * P:(h + 1) * P], QKV[:, 8 + h, tok], ID[:])
                    for h in range(HEADS):
                        last = nc.tensor.transpose(PL[1][:, h * P:(h + 1) * P], QKV[:, 4 + h, tok], ID[:])
                    last.then_inc(G["gv_t"], 1)

            def spatial_gate(k):
                if k in (9, 11):
                    for t in (k - 9, k - 8):
                        if t >= 2:
                            pe.wait_ge(G["vt_out"], t - 1)
                        else:
                            pe.wait_ge(G["gv_vb"], 4)
                            pe.wait_ge(G["gv_k"], 4)
                        for g in range(4):
                            last = nc.tensor.transpose(PL[t % 2][:, g * P:(g + 1) * P], UV[:, 4 + g, t * P:(t + 1) * P], ID[:])
                        last.then_inc(G["vt_t"], 1)
                if k >= 24:
                    t = k - 24
                    pe.wait_ge(ws_in, 48)
                    pe.wait_ge(G["ln_v"], t + 1)
                    if t >= 2:
                        pe.wait_ge(G["sp_y"], t - 1)
                    for g in range(4):
                        o = PL[t % 2][:, g * P:(g + 1) * P]
                        mm(o, ONES[0:1, :], BS[0:1, g * P:(g + 1) * P], start=True, stop=False)
                        last = mm(o, UV[:, 4 + g, t * P:(t + 1) * P], WS[:, g, :], start=False, stop=True)
                    last.then_inc(G["sp_s"], 1)

            def out_sums(st):
                pe.wait_ge(G["on_sq"], st + 1)
                for h in range(HEADS):
                    for t in range(2):
                        last = mm(PL[0][:, 2 * h + t:2 * h + t + 1], ONQ[:, h, t * P:(t + 1) * P], ONES[:, 0:1], start=True, stop=True)
                last.then_inc(G["on_ss"], 1)

            def out_spread(st):
                pe.wait_ge(G["on_std"], st + 1)
                for h in range(HEADS):
                    for t in range(2):
                        last = mm(PL[h // 2][:, h % 2 * SEQ + t * P:h % 2 * SEQ + (t + 1) * P], SM[:, 64 + 2 * h + t:65 + 2 * h + t].to_broadcast([P, P]), ID[:], start=True, stop=True)
                last.then_inc(G["on_bc"], 1)

            def first_outputs(k):
                if k == 6:
                    out_sums(0)
                if k == 9:
                    out_spread(0)

            for st in range(2):
                if st:
                    for d in range(2):
                        pe.wait_ge(sc_state[d], 4)
                    pe.wait_ge(G["sp_y"], 4)
                for q in range(4):
                    tl, d, z = q // 2, q % 2, 4 * st + q
                    tt = 2 * st + tl
                    if q >= 2:
                        pe.wait_ge(G["gb_at"], z - 1)
                    elif z == 0:
                        pe.wait_ge(G["g_cum"], 1)
                    sums, betas = ROWS[q % 2]
                    for h in range(HEADS):
                        mm(sums[:, h * P:(h + 1) * P], GTOK[:, tt, 4 * d + h:4 * d + h + 1].to_broadcast([P, P]), gtab("cum", d), start=True, stop=True)
                        last = mm(betas[:, h * P:(h + 1) * P], GTOK[:, tt, 32 + 4 * d + h:33 + 4 * d + h].to_broadcast([P, P]), ID[:], start=True, stop=True)
                    last.then_inc(G["gb_r"], 1)
                    if q < 2:
                        tok = slice(st * SEQ + q * P, st * SEQ + (q + 1) * P)
                        for h in range(HEADS):
                            mm(bank(2 + 2 * q, 4, P)[:, h, :], QKV[:, 4 + h, tok], QKV[:, 4 + h, tok], start=True, stop=True)
                            last = mm(bank(3 + 2 * q, 4, P)[:, h, :], QKV[:, 4 + h, tok], QKV[:, h, tok], start=True, stop=True)
                        last.then_inc(G["gb_k"], 1)
                pe.wait_ge(G["gb_at"], 4 * st + 4)

                def first_product(k):
                    lev, q = LEVELS[k]
                    b, at = k % 2, 24 * st
                    pe.wait_ge(G["lv_ct"], at + k + 1)
                    if lev == 0:
                        if k >= 2:
                            pe.wait_ge(G["lv_tu"], at + k - 1)
                        for h in range(HEADS):
                            last = nc.tensor.transpose(bank(b, 4, P)[:, h, :], CT[:, b, h, :], ID[:])
                    else:
                        pe.wait_ge(G["lv_tu"], at + (k - 1 if k < 6 else k - 3))
                        for h in range(HEADS):
                            last = mm(bank(b, 4, P)[:, h, :], CT[:, b, h, :], TT[:, q, h, :], start=True, stop=True)
                    last.then_inc(G["lv_m"], 1)

                def second_product(k):
                    lev, q = LEVELS[k]
                    b, at = k % 2, 24 * st
                    pe.wait_ge(G["lv_m1"], 20 * st + k - 3)
                    if k >= 6:
                        pe.wait_ge(G["lv_tu"], at + k - 1)
                    if lev < 5:
                        for h in range(HEADS):
                            mm(bank(2 + 2 * b, 4, P)[:, h, :], TU[:, q, h, :], M1[:, b, h, :], start=True, stop=True)
                    for h in range(HEADS):
                        last = mm(bank(3 + 2 * b, 4, P)[:, h, :], M1[:, b, h, :], TU[:, q, h, :], start=True, stop=True)
                    last.then_inc(G["lv_x"], 1)

                for k in range(25):
                    if k < 24:
                        first_product(k)
                    if k >= 5:
                        second_product(k - 1)
                    if k < 24:
                        values_keys(st, k)
                        (first_outputs if st else spatial_gate)(k)
                pe.wait_ge(G["lv_tu"], 24 * st + 24)
                for q in range(4):
                    b = q % 2
                    if q >= 2:
                        pe.wait_ge(G["u_out"], 4 * st + q - 1)
                        pe.wait_ge(G["w_out"], 4 * st + q - 1)
                    for h in range(HEADS):
                        mm(bank(2 + 2 * b, 4, P)[:, h, :], TU[:, q, h, :], VB[:, q, h, :], start=True, stop=True)
                        last = mm(bank(3 + 2 * b, 4, P)[:, h, :], KBG[:, q, h, :], TU[:, q, h, :], start=True, stop=True)
                    last.then_inc(G["uw_ready"], 1)
                pe.wait_ge(G["u_out"], 4 * st + 4)
                pe.wait_ge(G["w_out"], 4 * st + 4)
                pe.wait_ge(G["s_init"], 1)
                pe.wait_ge(G["gb_q"], 4 * st + 4)
                for k in range(4):
                    n = 4 * st + k
                    for d in range(2):
                        _, q, _ = chunk_place(st, k, d)
                        if n:
                            pe.wait_ge(sc_state[d], n)
                        for h in range(HEADS):
                            last = mm(bank(d, 4, P)[:, h, :], WT[:, q, h, :], S[:, d, h, :], start=True, stop=True)
                        last.then_inc(sc_w[d], 1)
                    for d in range(2):
                        _, q, po = chunk_place(st, k, d)
                        half = slice(po, po + 64)
                        pe.wait_ge(sc_v[d], n + 1)
                        o = BK[4 + d][:, 0:256].rearrange("p (h t) -> p h t", h=HEADS)
                        for h in range(HEADS):
                            mm(o[:, h, :], S[:, d, h, :], q_decayed(st, q)[:, h, half], start=True, stop=False)
                            mm(o[:, h, :], VN[half, d, h, :], ATT[half, q, h, half], start=False, stop=True)
                        for h in range(HEADS):
                            last = mm(bank(2 + d, 4, P)[:, h, :], KD[half, q, h, :], VN[half, d, h, :], start=True, stop=True)
                        last.then_inc(sc_s[d], 1)
                    if st == 0:
                        spatial_gate(24 + k)
            for d in range(2):
                pe.wait_ge(sc_state[d], 8)
            out_sums(1)
            out_spread(1)

            pe.wait_ge(G["y_b"], 2)
            pe.wait_ge(G["y_a"], 4)
            with pe.Fori(0, 2) as i:
                for s in range(4):
                    tile(B0["out0"] + s, T0["out0"] + s, slice(0, T2), T2, 4 * i)
                    for j in ((0, 1), (2,), (3, 4), (5,))[s]:
                        ring_mod_tile(40 + j, 1, 40, i, 6)

            def up(layer, x, width):
                name = f"up{layer}"
                with pe.Fori(0, FC // 2) as i:
                    for s in range(4):
                        tile(B0[name] + s, T0[name] + s, x, width, 4 * i, h_ready(f"n2_{layer}") if s == 0 else None)
                        if layer == 0:
                            ring_mod_tile(52 + s, 5, 52, i, 4)

            def down(layer, ah, al, width):
                name = f"dn{layer}"
                with pe.Fori(0, 2) as i:
                    for m in range(4):
                        t = T0[name] + m
                        free_bank(t, 4 * i)
                        for k in range(FC):
                            n, w = B0[name] + 3 * m + k // 8, slice(k % 8 * P, (k % 8 + 1) * P)
                            if k % 8 == 0:
                                weights(n, 12 * i)
                            if m == 0:
                                pe.wait_ge(act_lo, FC * layer + k + 1)
                            last = mm3(PL[t % 2][:, 0:width], wh(n)[:, w], wl(n)[:, w], ah[:, k, :], al[:, k, :], k == 0, k == FC - 1)
                            if k % 8 == 7 or k == FC - 1:
                                last.then_inc(pe_done, 1)

            def project(name, x, width, ready=None, loops=2):
                with pe.Fori(0, loops) as i:
                    for s in range(4):
                        tile(B0[name] + s, T0[name] + s, x, width, 4 * i, ready if s == 0 else None)

            norm("n2_0")
            up(0, slice(0, T2), T2)
            down(0, AH0, AL0, T2)

            norm("n1_1")
            for m in range(6):
                x = LAT if m < 3 else slice(0, T2)
                tile(B0["in1"] + m, T0["in1"] + m, x, SEQ if m < 3 else T2, 0, h_ready("n1_1") if m in (0, 3) else None)
            norm("cq")
            norm("ckv")

            def chunks(name, per, xh, xl, ready):
                done = -1
                for m in range(dict((s, n) for s, _, n in STAGES)[name]):
                    t = T0[name] + m
                    free_bank(t)
                    for k in range(per):
                        n, w = B0[name] + (m * per + k) // 8, slice((m * per + k) % 8 * P, ((m * per + k) % 8 + 1) * P)
                        if n != done:
                            weights(n)
                            done = n
                        if m == 0:
                            pe.wait_ge(n_lo, NORM_S0[ready] + k + 1)
                        last = mm3(PL[t % 2][:, 0:xh.shape[2]], wh(n)[:, w], wl(n)[:, w], xh[:, k, :], xl[:, k, :], k == 0, k == per - 1)
                    last.then_inc(pe_done, 1)

            def moving(name, xh, xl, x0, some, toks, per_tile):
                for b in some:
                    n = B0[name] + b
                    weights(n)
                    first, final = b % per_tile == 0, b % per_tile == per_tile - 1
                    for tok in range(toks):
                        t = T0[name] + (b // per_tile) * toks + tok
                        if first:
                            free_bank(t)
                        for kk in range(2):
                            k = 2 * (b % per_tile) + kk
                            x = slice(x0 + tok * P, x0 + (tok + 1) * P)
                            w = slice(kk * 512, (kk + 1) * 512)
                            o = PL[t % 2][:]
                            mm(o, xh[:, k, x], wh(n)[:, w], start=(first and kk == 0), stop=False)
                            mm(o, xh[:, k, x], wl(n)[:, w], start=False, stop=False)
                            last = mm(o, xl[:, k, x], wh(n)[:, w], start=False, stop=(final and kk == 1))
                        last.then_inc(pe_done, 1)

            chunks("uq", 3, CQH, CQL, "cq")
            norm("mem")
            chunks("ukv_k", 2, CKH, CKL, "ckv")

            def rotate(tiles, r0, some):
                for i in some:
                    x, t, which = tiles[i]
                    pe.wait_ge(tile_out, t + 3)
                    if i >= 2:
                        pe.wait_ge(A["rp_d"], r0 + i - 1)
                    mm(BK[2 + i % 2][:, 0:SEQ], ltab("perm32" if which == "32" else "perm64", 0, P), x, start=True, stop=True).then_inc(A["rp_m"], 1)

            pe.wait_ge(late_in, 16)
            for b in range(2):
                rotate(ROPE1, 0, (2 * b, 2 * b + 1))
                moving("ukv_v", CKH, CKL, 0, (b,), 4, 1)
            rotate(ROPE1, 0, (4,))

            pe.wait_ge(A["rp_d"], len(ROPE1))
            pe.wait_ge(tile_out, T0["out1"] + 2)

            def attend(ly, scores, values, extra=None):
                nb = len(ly.banks)
                for a in range(ly.n + 3):
                    if a < ly.n:
                        if ly.a0 or a >= nb:
                            pe.wait_ge(A["at_m" if ly.masked else "at_p"], ly.a0 + max(0, a - nb + 1))
                        scores(a // 2, a % 2, ly.banks[a % nb]).then_inc(A["at_s"], 1)
                    if 2 <= a < ly.n + 2:
                        p = a - 2
                        pe.wait_ge(A["at_n"], ly.a0 + p + 1)
                        for k in range(ly.kt):
                            last = nc.tensor.transpose(BK[2 + p % 2][:, k * P:(k + 1) * P], PB[:, p % 3, k * P:(k + 1) * P], ID[:])
                        last.then_inc(A["at_t"], 1)
                    if a >= 3:
                        p = a - 3
                        pe.wait_ge(A["at_pt"], ly.a0 + p + 1)
                        e = p // ly.per
                        if ly is not DSA and p % ly.per == 0 and ly.e0 + e >= 2:
                            pe.wait_ge(A["at_y"], ly.e0 + e - 1)
                        values(p // 2, p % 2, PT[:, p % 2, :, :]).then_inc(A["at_o"], 1)
                        if extra:
                            extra(p)

            def mla_scores(h, qt, o):
                q, po = slice(qt * P, (qt + 1) * P), 64 * (h % 2)
                mm(o[:], MQ[:, h, q], KN[:, h, :], start=True, stop=False)
                return mm(o[:], MQ[po:po + 64, 8 + h // 2, q], KR[po:po + 64, :], start=False, stop=True)

            def mla_values(h, qt, pt):
                for k in range(4):
                    last = mm(BK[4 + h % 2][:, qt * P:(qt + 1) * P], VT[:, k, h * P:(h + 1) * P], pt[:, k, :], start=(k == 0), stop=(k == 3))
                return last

            attend(MLA, mla_scores, mla_values)
            project("out1", LAT, SEQ, lambda k: (A["at_y"], 8))
            norm("n2_1")
            up(1, LAT, SEQ)
            down(1, AH1, AL1, SEQ)
            norm("final1")

            norm("mix")
            project("in2", LAT, SEQ, h_ready("mix"), 5)
            for m in (20, 21):
                tile(B0["in2"] + m, T0["in2"] + m, LAT, SEQ)
            moving("in2_v", HH, HL, SEQ, range(4), 2, 4)
            norm("kv2")
            for j in range(SIDE):
                if j < 8:
                    tile(B0["xk"] + j, T0["xk"] + j, CTX, SEQ, 0, None if j else h_ready("mem"))
                else:
                    moving("xv", HH, HL, 0, (j - 8,), 2, 4)
                rotate(ROPE2, len(ROPE1), ROTATE_AT[j])
                if j == 2:
                    for qt in range(2):
                        last = nc.tensor.transpose(BK[4][:, 8 * qt:8 * qt + 8], PJ[0:8, 9, qt * P:(qt + 1) * P], ID[0:8, 0:8])
                    last.then_inc(A["we_t"], 1)
                    pe.wait_ge(n_xn, NORM_C0["kv2"] + 1)
                    for qt in range(2):
                        last = nc.tensor.transpose(BK[5][:, qt * P:(qt + 1) * P], PJ[:, 6, qt * P:(qt + 1) * P], ID[:])
                    last.then_inc(A["ct_t"], 1)
                if j in INDEX_AT:
                    pe.wait_ge(A["rp_d"], len(ROPE1) + 5)
                    for c in range(4 * (j - INDEX_AT[0]), 4 * (j - INDEX_AT[0]) + 4):
                        qt, h = c // 8, c % 8
                        po = 64 * (h % 2)
                        if c >= 2:
                            pe.wait_ge(A["ix_r"], c - 1)
                        mm(BK[c % 2][:, 0:SEQ], PJ[po:po + 64, 10 + h // 2, qt * P:(qt + 1) * P], PJ[po:po + 64, 8, :], start=True, stop=True).then_inc(A["ix_l"], 1)
                if j in LATENT_AT:
                    pe.wait_ge(uk_in, 32)
                    pe.wait_ge(A["rp_d"], len(ROPE1) + len(ROPE2))
                    for h in (2 * (j - LATENT_AT[0]), 2 * (j - LATENT_AT[0]) + 1):
                        po = 64 * (h % 2)
                        if h >= 2:
                            pe.wait_ge(A["ql_out"], h - 1)
                        mm(BK[2 + h % 2][:, 0:SEQ], WUK[po:po + 64, h // 2, :], PJ[po:po + 64, h // 2, :], start=True, stop=True).then_inc(A["ql_m"], 1)
            pe.wait_ge(A["rp_d"], len(ROPE1) + len(ROPE2))
            pe.wait_ge(tile_out, T0["out2"] + 2)
            pe.wait_ge(A["ix_r"], 16)
            pe.wait_ge(A["ql_out"], 8)
            pe.wait_ge(A["ct_out"], 1)
            pe.wait_ge(A["we_ready"], 1)

            def dsa_scores(h, qt, o):
                q, po = slice(qt * P, (qt + 1) * P), 32 * (h % 4)
                mm(o[:, 0:SEQ], QL[:, h, q], PJ[:, 6, :], start=True, stop=False)
                return mm(o[:, 0:SEQ], PJ[po:po + 32, 4 + h // 4, q], PJ[po:po + 32, 7, :], start=False, stop=True)

            def dsa_values(h, qt, pt):
                if qt == 0 and h >= 2:
                    pe.wait_ge(A["ol_out"], h - 1)
                for k in range(2):
                    last = mm(BK[4 + h % 2][:, qt * P:(qt + 1) * P], CTK[:, k, :], pt[:, k, :], start=(k == 0), stop=(k == 1))
                return last

            def dsa_out(h):
                pair, po = h // 2, 64 * (h % 2)
                pe.wait_ge(A["ol_out"], h + 1)
                if h % 2 == 0 and pair >= 2:
                    pe.wait_ge(A["at_y"], DSA.e0 + pair - 1)
                mm(PL[pair % 2][po:po + 64, 0:SEQ], WUV[:, h, :], OL[:, h % 2, :], start=True, stop=True).then_inc(A["ol_o"], 1)

            attend(DSA, dsa_scores, dsa_values, lambda p: dsa_out((p - 3) // 2) if p % 2 and p >= 3 else None)
            dsa_out(7)

            def dil_scores(h, qt, o):
                q, po = slice(qt * P, (qt + 1) * P), 64 * (h % 2)
                return mm(o[:, 0:SEQ], PJ[po:po + 64, 14 + h // 2, q], PJ[po:po + 64, 18 + h // 2, :], start=True, stop=True)

            def dil_values(h, qt, pt):
                po = 64 * (h % 2)
                for k in range(2):
                    last = mm(BK[4 + h // 2 % 2][po:po + 64, qt * P:(qt + 1) * P], VBK[:, k, h * 64:(h + 1) * 64], pt[:, k, :], start=(k == 0), stop=(k == 1))
                return last

            attend(DIL, dil_scores, dil_values)
            project("out2", LAT, SEQ, lambda k: (A["at_y"], 16))

            norm("cross")
            project("xq", LAT, SEQ, h_ready("cross"))
            pe.wait_ge(tile_out, T0["xo"] + 2)

            def cross_scores(h, qt, o):
                q = slice(qt * P, (qt + 1) * P)
                mm(o[:, 0:SEQ], QC[:, 2 * h, q], KCR[:, 2 * h, :], start=True, stop=False)
                return mm(o[:, 0:SEQ], QC[:, 2 * h + 1, q], KCR[:, 2 * h + 1, :], start=False, stop=True)

            def cross_values(h, qt, pt):
                o = BK[4 + h % 2][:, 0:512].rearrange("p (c q) -> p c q", c=2)
                for c in range(2):
                    for k in range(2):
                        last = mm(o[:, c, qt * P:(qt + 1) * P], VC[:, k, h * 256 + c * P:h * 256 + (c + 1) * P], pt[:, k, :], start=(k == 0), stop=(k == 1))
                return last

            attend(CRS, cross_scores, cross_values)
            project("xo", LAT, SEQ, lambda k: (A["at_y"], 20))

            norm("mlp")
            project("up2", LAT, SEQ, h_ready("mlp"), 8)

            def down2(i):
                for m in range(2):
                    t = T0["dn2"] + m
                    free_bank(t, 2 * i)
                    for k in range(32):
                        n, w = B0["dn2"] + 4 * m + k // 8, slice(k % 8 * P, (k % 8 + 1) * P)
                        if k % 8 == 0:
                            weights(n, 8 * i)
                        if m == 0:
                            pe.wait_ge(act_lo, 2 * FC + k + 1)
                        last = mm3(PL[t % 2][:, 0:SEQ], wh(n)[:, w], wl(n)[:, w], AH2[:, k, :], AL2[:, k, :], k == 0, k == 31)
                        if k % 8 == 7:
                            last.then_inc(pe_done, 1)

            with pe.Fori(0, 4) as i:
                down2(i)
            norm("final2")

        @block.sync
        def _(sp):
            def load_w(n, off=0):
                sp.dma_start(RAW[:, n % 4, :], w_stream[n + off]).then_inc(w_landed[n % 4], 16)

            def next_w(s, off=0):
                sp.wait_ge(w_low, s + 1 + off)
                load_w(s + 4, off)

            def load_a(m, off=0):
                sp.wait_ge(a_used, m - 1 + off)
                sp.dma_start(AR[:, m % 2, :], a_stream[m + off]).then_inc(a_landed[m % 2], 16)

            sp.dma_start(X[:], x_in).then_inc(x_ready, 16)
            for g in range(4):
                m = slice(4 * g, 4 * g + 4)
                sp.dma_start(A16[:, m, :], a_stream[m].rearrange("m p n -> p m n")).then_inc(a_first[g], 16)
            for n in range(4):
                load_w(n)
            with sp.Fori(0, 6) as i:
                for s in range(4):
                    next_w(s, 4 * i)
                    load_a(16 + s, 4 * i)
            next_w(24)
            with sp.Fori(0, 2) as i:
                for s in range(4):
                    next_w(B0["out0"] + s, 4 * i)
                    for j in ((0, 1), (2,), (3, 4), (5,))[s]:
                        load_a(40 + j, 6 * i)
            with sp.Fori(0, FC // 2) as i:
                for s in range(4):
                    next_w(B0["up0"] + s, 4 * i)
                    load_a(52 + s, 4 * i)
            left = NBLK - 4 - B0["dn0"]
            with sp.Fori(0, left // 4) as i:
                for s in range(4):
                    next_w(B0["dn0"] + s, 4 * i)
            for s in range(left // 4 * 4, left):
                next_w(B0["dn0"] + s)
            for k in range(0, KC, 4):
                sp.wait_ge(n_xn, NORM_C0["final2"] + k + 4)
                sp.dma_start(out[:, k:k + 4, :], X[:, k:k + 4, LAT]).then_inc(out_done, 16)
            sp.wait_ge(out_done, 32)

        @block.gpsimd
        def _(pool):
            nc.gpsimd.memset(ONES[:], 1.0).then_inc(init, 1)
            for k in range(2):
                nc.gpsimd.memset(XP[:, k, :, 0:1], 0.0)
                nc.gpsimd.memset(XP[:, k, :, SEQ + 1:SEQ + 2], 0.0).then_inc(conv_done, 1)
            nc.gpsimd.memset(S[:], 0.0).then_inc(G["s_init"], 1)
            pool.wait_ge(mod_ready, 1)
            pool.dma_start(GTAB[:], gdn_tables).then_inc(gdn_in, 16)
            pool.wait_ge(gdn_in, 16)
            for st in range(2):
                for q in range(4):
                    tl, z = q // 2, 4 * st + q
                    tok = slice(st * SEQ + tl * P, st * SEQ + (tl + 1) * P)
                    pool.wait_ge(G["gb_e"], 2 * z + 1)
                    if q % 2:
                        pool.wait_ge(G["gb_q"], z)
                        pool.wait_ge(G["gb_k"], 2 * st + tl + 1)
                    nc.gpsimd.tensor_tensor(q_decayed(st, q), QKV[:, 0:HEADS, tok], ER[:, z % 2, :, :], ALU.mult).then_inc(G["gb_q"], 1)
                for k, (lev, q) in enumerate(LEVELS):
                    n, b = 24 * st + k, k % 2
                    if lev == 0:
                        pool.wait_ge(G["gb_at"], 4 * st + q + 1)
                    if n >= 2:
                        pool.wait_ge(G["lv_m"], n - 1)
                    if 2 <= k < 6:
                        pool.wait_ge(G["lv_tu"], n - 1)
                    mask = gtab("lev", 6 * (q % 2) + lev).unsqueeze(1).to_broadcast([P, HEADS, P])
                    nc.gpsimd.tensor_tensor(CT[:, b, :, :], AT[:, q, :, :], mask, ALU.mult).then_inc(G["lv_ct"], 1)
                    if st == 0 and k == 3:
                        pool.dma_start(LNR[:], ln_rows.rearrange("p (a b c) -> p a b c", a=2, b=4)).then_inc(ws_in, 16)
                        pool.dma_start(WS[:], ws_t).then_inc(ws_in, 16)
                        pool.dma_start(BS[:], bs_row).then_inc(ws_in, 16)
                    if st == 0 and k >= 20:
                        x = UV[:, 4:8, (k - 20) * P:(k - 19) * P]
                        pool.wait_ge(G["ln_g"], k - 19)
                        pool.wait_ge(ws_in, 48)
                        nc.gpsimd.tensor_tensor(x, x, LNR[:, 1, :, :], ALU.add).then_inc(G["ln_v"], 1)
            pool.wait_ge(x_res, 2 + RES["dn0"] + 8)
            pool.dma_start(LTAB[:], late_tables).then_inc(late_in, 16)
            pool.wait_ge(n_xn, NORM_C0["n1_1"] + 8)
            pool.dma_start(X[:, :, CTX], mem_in).then_inc(mem_ready, 16)
            pool.wait_ge(x_res, 2 + RES["dn1"] + 8)
            pool.dma_start(WUK[:], w_uk).then_inc(uk_in, 16)
            pool.dma_start(WUV[:], w_uv).then_inc(uk_in, 16)

        UVF = UV[:].rearrange("p a b -> p (a b)")
        PJF = PJ[:].rearrange("p a b -> p (a b)")
        QCF = QC[:].rearrange("p a b -> p (a b)")
        QKVF = QKV[:].rearrange("p a b -> p (a b)")
        XF = X[:].rearrange("p a b -> p (a b)")
        MODF = MOD[:].rearrange("p a b c d -> p (a b c d)")
        NORM_OUT = {"cq": (CQH, CQL), "ckv": (CKH, CKL)}

        def norm_src(name, k):
            if name == "cq":
                return CQ[:, k, :]
            if name == "ckv":
                return CKV[:, k, :]
            if name == "kv2":
                return PJ[:, 6, :]
            if name == "mem":
                return X[:, k, CTX]
            return X[:, k, :] if NORMS[NORM_I[name]][2] == T2 else X[:, k, LAT]

        def norm_dst(name, k, low):
            if name in NORM_OUT:
                return NORM_OUT[name][low][:, k, :]
            x = CTX if name == "mem" else LAT if NORMS[NORM_I[name]][2] == SEQ else slice(0, T2)
            return (HL if low else HH)[:, k, x]

        def streams(name):
            return [(CTX, 0), (LAT, 1)] if NORMS[NORM_I[name]][2] == T2 else [(CTX, 1)]

        @block.scalar
        def _(act):
            f = nc.scalar.activation
            steps = [0]

            def link(ins):
                steps[0] += 1
                ins.then_inc(act_step, 1)
                act.wait_ge(act_step, steps[0])

            def split(n, off=0):
                if n >= NBLK:
                    return
                act.wait_ge(w_landed[n % 4], 16 * (n // 4 + 1) + 4 * off)
                if n >= 2:
                    act.wait_ge(pe_done, DONE_BLOCK[slot_before(n)] + off)
                f(wh(n), RAW[:, n % 4, :], ACT.Copy).then_inc(w_high, 1)

            def done(t, off=0):
                act.wait_ge(pe_done, DONE_TILE[t] + off)

            def norm_start(name):
                i = NORM_I[name]
                f(SM[:, 32 + i:33 + i], col("one"), ACT.Sqrt)
                if NORM_S0[name]:
                    act.wait_ge(n_lo, NORM_S0[name])
                if i:
                    act.wait_ge(n_xn, NORM_C0[name])

            def square(name, k, ready):
                act.wait_ge(*ready)
                f(squares(name, k), norm_src(name, k), ACT.Square).then_inc(n_sq, 1)

            def norm_root(name):
                i = NORM_I[name]
                width = NORMS[i][2]
                features = {"cq": 384, "ckv": 256, "kv2": 128}.get(name, D)
                act.wait_ge(n_ss, i + 1)
                for t in range(width // P):
                    last = f(STD[:, t:t + 1], SUMS[t][:, 0:1], ACT.Sqrt, scale=1.0 / features, bias=col("eps"))
                last.then_inc(n_root, 1)

            def norm_high(name, some=None):
                _, nch, width = NORMS[NORM_I[name]]
                if name not in SPLIT:
                    return
                for k in some or range(nch):
                    act.wait_ge(n_xn, NORM_C0[name] + k + 1)
                    if name in MODULATED:
                        layer, part = MODULATED[name]
                        for x, s in streams(name):
                            last = f(norm_dst(name, k, 0)[:, x], TMP[:, k, x], ACT.Identity, bias=MOD[:, layer, part, k, s:s + 1])
                        last.then_inc(n_hi, 1)
                    else:
                        f(norm_dst(name, k, 0), TMP[:, k, 0:width], ACT.Copy).then_inc(n_hi, 1)

            def norm_end(name):
                norm_root(name)
                norm_high(name)

            def norm(name, ready):
                norm_start(name)
                for k in range(NORMS[NORM_I[name]][1]):
                    square(name, k, ready(k))
                norm_end(name)

            def residual(name, m, gate, width):
                t, y = T0[name] + m, TYO if name == "out0" else TY
                done(t)
                act.wait_ge(x_res, RES[name] + m + 1)
                for x, s in ([(CTX, 0), (LAT, 1)] if width == T2 else [(CTX, 1)]):
                    if gate is None:
                        last = f(y[:, t % 2, x], PL[t % 2][:, x], ACT.Copy)
                    else:
                        last = f(y[:, t % 2, x], PL[t % 2][:, x], ACT.Identity, scale=MODF[:, (gate * KC + m) * 2 + s:(gate * KC + m) * 2 + s + 1])
                last.then_inc(tile_out, 1)

            def residuals(name, per, gate, width, then):
                norm_start(then)
                for m in range(KC):
                    for k in range(per):
                        split(B0[name] + per * m + k + lead(name))
                    residual(name, m, gate, width)
                    if m:
                        square(then, m - 1, (x_res, 2 + RES[name] + m))
                square(then, KC - 1, (x_res, 2 + RES[name] + KC))
                norm_end(then)

            def conv_in(t, k, cv, taps, width, it=0, per=0):
                act.wait_ge(pe_done, DONE_TILE[t] + per * it)
                act.wait_ge(conv_done, cv + k + 1 + per * it)
                n = width // SEQ
                f(XP[:, k % 2, 0:n, 1:SEQ + 1], PL[t % 2][:, 0:width].rearrange("p (s t) -> p s t", s=n), ACT.Copy)
                f(C1[:, k % 2, 0:width], PL[t % 2][:, 0:width], ACT.Identity, scale=C[:, ds(taps + 3 * k + 1 + 3 * per * it, 1)]).then_inc(tile_out, 1)

            act.dma_start(C[:], cols).then_inc(cols_in, 16)
            act.dma_start(ID[:], ident).then_inc(cols_in, 16)
            act.wait_ge(cols_in, 32)
            cond = C[:, COL_AT["cond"]:COL_AT["cond"] + 16]
            f(cond, cond, ACT.Silu).then_inc(cond_ready, 1)
            norm_start("n1_0")
            for k in range(KC):
                square("n1_0", k, (x_ready, 16))
            norm_root("n1_0")
            for g in range(4):
                act.wait_ge(m_sum, g + 1)
                f(MR[0:2, g, :], MROWS[g][0:2, :], ACT.Copy).then_inc(m_rows, 1)
            for j in range(2):
                f(SM[:, j:j + 1], col("one"), ACT.Copy).then_inc(tile_out, 1)
            split(0)
            norm_high("n1_0")
            split(1)

            with act.Fori(0, 2) as i:
                for s in range(4):
                    split(s + 2, 4 * i)
                    done(s, 4 * i)
                    f(UVF[:, ds(s * T2 + 4 * T2 * i, T2)], PL[s % 2][:], ACT.Gelu).then_inc(tile_out, 1)
            with act.Fori(0, 3) as i:
                for s in range(4):
                    split(8 + s + 2, 4 * i)
                    conv_in(8 + s, s, 0, COL_AT["bconv"], T2, i, 4)
                    act.wait_ge(conv_done, s + 3 + 4 * i)
                    f(QKVF[:, ds(s * T2 + 4 * T2 * i, T2)], C1[:, s % 2, :], ACT.Silu).then_inc(silu_done, 1)
            act.wait_ge(silu_done, 12)
            for t in range(20, 24):
                split(t + 2)
                if t in (20, 22):
                    for j in range(2 * (t - 20), 2 * (t - 20) + 4):
                        if j >= 4:
                            act.wait_ge(G["l2_ss"], j - 3)
                        f(SQL[:, j % 4, :], QKV[:, j, :], ACT.Square).then_inc(G["l2_sq"], 1)
                done(t)
                f(GATE[:, t - 20, :], PL[t % 2][:], ACT.Silu).then_inc(tile_out, 1)
            act.wait_ge(G["l2_ss"], 8)
            f(L2[:, 0, :], BK[0][:, 0:32], ACT.Sqrt, bias=col("eps")).then_inc(G["l2_root"], 1)
            split(26)
            done(24)
            act.wait_ge(G["g_rows"], 1)
            f(GA[0:8, :], PL[0][0:8, :], ACT.Identity, bias=C[0:8, COL_AT["dt_bias"]:COL_AT["dt_bias"] + 1])
            link(f(GT[32:40, :], PL[0][32:40, :], ACT.Sigmoid))
            f(SM[:, 2:3], col("one"), ACT.Copy).then_inc(tile_out, 1)
            link(f(GB[0:8, :], GA[0:8, :], ACT.Abs))
            link(f(GB[0:8, :], GB[0:8, :], ACT.Exp, scale=-1.0))
            f(SM[0:8, 4:5], C[0:8, COL_AT["a_log"]:COL_AT["a_log"] + 1], ACT.Exp)
            f(GB[0:8, :], GB[0:8, :], ACT.Ln, bias=C[0:8, COL_AT["one"]:COL_AT["one"] + 1]).then_inc(G["g_in"], 1)

            def values(st, k):
                for tl, at in enumerate(TURNS[st]):
                    if k - at in (1, 2):
                        y, d = 2 * st + tl, k - at - 1
                        act.wait_ge(G["gv_t"], y + 1)
                        for h in range(HEADS):
                            last = f(VB[:, 2 * tl + d, h, :], PL[0][:, h * P:(h + 1) * P], ACT.Identity, scale=GTOK[:, y, 32 + 4 * d + h:33 + 4 * d + h])
                        last.then_inc(G["gv_vb"], 1)

            def spatial_gate(k):
                if k in (10, 12):
                    for t in (k - 10, k - 9):
                        act.wait_ge(G["vt_t"], t + 1)
                        f(UV[:, 4:8, t * P:(t + 1) * P], PL[t % 2][:].rearrange("p (a b) -> p a b", a=4), ACT.Copy, accum_out=SM[:, 50 + t:51 + t]).then_inc(G["vt_out"], 1)
                if k in (14, 15):
                    act.wait_ge(G["ln_mean"], 1)
                    for t in (2 * k - 28, 2 * k - 27):
                        if t:
                            act.wait_ge(G["ln_sq"], t)
                        f(STD[:].rearrange("p (a b) -> p a b", a=4), UV[:, 4:8, t * P:(t + 1) * P], ACT.Square, bias=SM[:, 54 + t:55 + t], accum_out=SM[:, 58 + t:59 + t]).then_inc(G["ln_sq"], 1)
                if k == 16:
                    act.wait_ge(G["ln_sq"], 4)
                    f(SM[:, 58:62], SM[:, 58:62], ACT.Sqrt, scale=1.0 / 512, bias=col("eps")).then_inc(G["ln_std"], 1)

            def out_squares(st):
                f(ONQ[:], QKV[:, 8:12, st * SEQ:(st + 1) * SEQ], ACT.Square).then_inc(G["on_sq"], 1)

            def out_root(st):
                act.wait_ge(G["on_ss"], st + 1)
                f(SM[:, 64:72], PL[0][:, 0:8], ACT.Sqrt, scale=1.0 / P, bias=col("eps")).then_inc(G["on_root"], 1)

            def first_outputs(k):
                if k == 4:
                    out_squares(0)
                if k == 7:
                    out_root(0)

            act.wait_ge(G["g_cum"], 1)
            f(EG[:], GC[:, :, :, 0:4], ACT.Exp).then_inc(G["g_exp"], 1)
            act.wait_ge(G["g_cum"], 2)
            f(EK[:], EK[:], ACT.Exp).then_inc(G["g_exp"], 1)
            for st in range(2):
                for q in range(4):
                    z = 4 * st + q
                    act.wait_ge(G["gb_r"], z + 1)
                    if z >= 2:
                        act.wait_ge(G["gb_at"], z - 1)
                        act.wait_ge(G["gb_q"], z - 1)
                    f(ER[:, z % 2, :, :], ROWS[q % 2][0][:].rearrange("p (a b) -> p a b", a=HEADS), ACT.Exp).then_inc(G["gb_e"], 1)
                    act.wait_ge(G["gb_d"], z + 1)
                    f(DT[:, z % 2, :, :], DT[:, z % 2, :, :], ACT.Exp).then_inc(G["gb_e"], 1)
                for k in range(4, 24):
                    act.wait_ge(G["lv_m"], 24 * st + k + 1)
                    if k >= 6:
                        act.wait_ge(G["lv_x"], 20 * st + k - 5)
                    f(M1[:, k % 2, :, :], bank(k % 2, 4, P), ACT.Copy).then_inc(G["lv_m1"], 1)
                    values(st, k)
                    (first_outputs if st else spatial_gate)(k)
                for q in range(4):
                    act.wait_ge(G["uw_ready"], 4 * st + q + 1)
                    f(UU[:, q, :, :], bank(2 + 2 * (q % 2), 4, P), ACT.Copy).then_inc(G["u_out"], 1)
            for t in range(4):
                f(HH[:, 0:4, t * P:(t + 1) * P], UV[:, 0:4, t * P:(t + 1) * P], ACT.Copy).then_inc(G["sp_hi"], 1)
            act.wait_ge(G["on_y"], 1)
            f(HH[:, 4:8, CTX], QKV[:, 8:12, CTX], ACT.Copy).then_inc(G["on_hi"], 1)
            for d in range(2):
                act.wait_ge(sc_state[d], 8)
            out_squares(1)
            out_root(1)
            act.wait_ge(G["on_y"], 2)
            f(HH[:, 4:8, LAT], QKV[:, 8:12, LAT], ACT.Copy).then_inc(G["on_hi"], 1)

            act.wait_ge(mod_ready, 2)
            residuals("out0", 1, 2, T2, "n2_0")

            def up(layer, ah, width):
                name = f"up{layer}"
                cv, taps = 12 + 2 * FC * layer, COL_AT["fconv"] + 2 * FC * 3 * layer
                ahf = ah[:].rearrange("p a b -> p (a b)")
                def more(s, i):
                    split(B0[name] + s + lead(name), 4 * i)

                def taps_of(s, i):
                    conv_in(T0[name] + s, s, cv, taps, width, i, 4)

                def silu(p, i):
                    act.wait_ge(conv_done, cv + 2 * p + 3 + 4 * i)
                    f(SG[:, 0:width], C1[:, 0, 0:width], ACT.Silu).then_inc(silu_done, 1)

                def high(p, i):
                    act.wait_ge(act_done, FC * layer + p + 1 + 2 * i)
                    f(ahf[:, ds(p * width + 2 * width * i, width)], A32[:, 0:width], ACT.Copy).then_inc(act_hi, 1)

                def step(i, first=False):
                    f(SM[:, 48:49], col("one"), ACT.Silu)
                    taps_of(0, i)
                    if not first:
                        high(-1, i)
                    more(0, i)
                    taps_of(1, i)
                    more(1, i)
                    silu(0, i)
                    act.wait_ge(silu_done, 12 + FC * layer + 1 + 2 * i)
                    taps_of(2, i)
                    high(0, i)
                    more(2, i)
                    more(3, i)
                    taps_of(3, i)
                    silu(1, i)
                    act.wait_ge(silu_done, 12 + FC * layer + 2 + 2 * i)

                step(0, True)
                with act.Fori(1, FC // 2) as i:
                    step(i)
                high(1, FC // 2 - 1)

            def project(name, evac, loops=2):
                with act.Fori(0, loops) as i:
                    for s in range(4):
                        split(B0[name] + s + lead(name), 4 * i)
                        evac(s, i)

            def copy_to(name, flat, width):
                def evac(s, i):
                    done(T0[name] + s, 4 * i)
                    f(flat[:, ds(s * width + 4 * width * i, width)], PL[(T0[name] + s) % 2][:, 0:width], ACT.Copy).then_inc(tile_out, 1)
                return evac

            up(0, AH0, T2)
            act.wait_ge(mod_ready, 4)
            residuals("dn0", 3, 5, T2, "n1_1")

            split(B0["in1"] + 2)
            for m, o in enumerate([CQ[:, 0, :], CQ[:, 1, :], CQ[:, 2, :], CKV[:, 0, :], CKV[:, 1, :], KR[:]]):
                split(B0["in1"] + m + lead("in1"))
                done(T0["in1"] + m)
                f(o, PL[(T0["in1"] + m) % 2][:, 0:o.shape[1]], ACT.Copy).then_inc(tile_out, 1)
            norm("cq", lambda k: (tile_out, T0["in1"] + k + 3))
            norm("ckv", lambda k: (tile_out, T0["in1"] + k + 6))

            def walk(name, place_of, beside=None):
                nb, nt = next((b, t) for s, b, t in STAGES if s == name)
                events = [(DONE_BLOCK[B0[name] + b], 0, b) for b in range(nb)] + [(DONE_TILE[T0[name] + t], 1, t) for t in range(nt)]
                for _, is_tile, j in sorted(events):
                    if is_tile:
                        o = place_of(j)
                        done(T0[name] + j)
                        f(o, PL[(T0[name] + j) % 2][:, 0:o.shape[1]], ACT.Copy).then_inc(tile_out, 1)
                        if beside:
                            beside(j)
                    else:
                        split(B0[name] + j + lead(name))

            norm_start("mem")
            for k in range(KC):
                square("mem", k, (mem_ready, 16))
            walk("uq", lambda m: MQ[:, m, :])
            norm_root("mem")
            walk("ukv_k", lambda m: KN[:, m, :], lambda m: norm_high("mem", (m,)))
            walk("ukv_v", lambda m: VT[:, m % 4, m // 4 * 512:(m // 4 + 1) * 512])

            def attend(ly, out_bank, out_chunks):
                for a in range(ly.steps):
                    w = ly.kt * P
                    if a < ly.n:
                        r = a % 3
                        act.wait_ge(A["at_m"], ly.a0 + a + 1)
                        if ly.a0 + a >= 3:
                            act.wait_ge(A["at_t"], ly.a0 + max(0, a - 2))
                        src = SX[:, a % 2, :] if ly.masked else ly.banks[a % 3][:, 0:w]
                        scale = 1.0 if ly.masked else ly.scale
                        if ly is DIL:
                            f(PB[:, r, 0:w], src, ACT.Exp, scale=scale, bias=SM[:, 20 + r:21 + r]).then_inc(A["at_p"], 1)
                        else:
                            f(PB[:, r, 0:w], src, ACT.Exp, scale=scale, bias=SM[:, 20 + r:21 + r], accum_out=SM[:, 24 + r:25 + r]).then_inc(A["at_p"], 1)
                    if 2 <= a < ly.n + 2:
                        p = a - 2
                        act.wait_ge(A["at_t"], ly.a0 + p + 1)
                        if ly.a0 + p >= 2:
                            act.wait_ge(A["at_o"], ly.a0 + p - 1)
                        f(PT[:, p % 2, 0:ly.kt, :], BK[2 + p % 2][:, 0:w].rearrange("p (k q) -> p k q", k=ly.kt), ACT.Copy).then_inc(A["at_pt"], 1)
                    if ly is DSA and a >= 5 and a % 2 == 1 and (a - 5) // 2 < 8:
                        h = (a - 5) // 2
                        act.wait_ge(A["at_o"], ly.a0 + 2 * h + 2)
                        if h >= 2:
                            act.wait_ge(A["ol_o"], h - 1)
                        f(OL[:, h % 2, :], BK[4 + h % 2][:, 0:SEQ], ACT.Copy).then_inc(A["ol_out"], 1)
                    if a >= ly.lag and (a - ly.lag) % ly.per == 0:
                        e = (a - ly.lag) // ly.per
                        if ly is DSA:
                            act.wait_ge(A["ol_o"], 2 * e + 2)
                        else:
                            act.wait_ge(A["at_o"], ly.a0 + ly.per * (e + 1))
                        f(out_chunks(HH, e), out_bank(e), ACT.Copy).then_inc(A["at_hi"], 1)

            attend(MLA, lambda e: BK[4 + e % 2][:, 0:SEQ], lambda h, e: h[:, e, LAT])
            residuals("out1", 1, 8, SEQ, "n2_1")
            up(1, AH1, SEQ)
            residuals("dn1", 3, 11, SEQ, "final1")

            norm("mix", lambda k: (n_xn, NORM_C0["final1"] + k + 1))
            project("in2", copy_to("in2", PJF, SEQ), 5)
            for m in (20, 21):
                split(B0["in2"] + m + lead("in2"))
                done(T0["in2"] + m)
                f(PJ[:, m, :], PL[(T0["in2"] + m) % 2][:, 0:SEQ], ACT.Copy).then_inc(tile_out, 1)
            walk("in2_v", lambda m: VBK[:, m, :])
            norm("kv2", lambda k: (tile_out, T0["in2"] + 9))
            for j in range(SIDE):
                if j < 8:
                    split(B0["xk"] + j + lead("xk"))
                    done(T0["xk"] + j)
                    f(KCR[:, j, :], PL[(T0["xk"] + j) % 2][:, 0:SEQ], ACT.Copy).then_inc(tile_out, 1)
                else:
                    split(B0["xv"] + j - 8 + lead("xv"))
                    if j % 4 == 3:
                        for m in (2 * (j // 12), 2 * (j // 12) + 1):
                            t = T0["xv"] + m
                            done(t)
                            f(VC[:, m % 2, m // 2 * 512:(m // 2 + 1) * 512], PL[t % 2][:], ACT.Copy).then_inc(tile_out, 1)
                if j == 2:
                    act.wait_ge(A["ct_t"], 1)
                    f(CTK[:], BK[5][:, 0:SEQ].rearrange("p (k c) -> p k c", k=2), ACT.Copy).then_inc(A["ct_out"], 1)
                if j in INDEX_AT:
                    for c in range(4 * (j - INDEX_AT[0]), 4 * (j - INDEX_AT[0]) + 4):
                        act.wait_ge(A["ix_l"], c + 1)
                        if c >= 2:
                            act.wait_ge(A["ix_a"], c - 1)
                        f(RL[:, c % 2, :], BK[c % 2][:, 0:SEQ], ACT.Relu).then_inc(A["ix_r"], 1)
                if j in LATENT_AT:
                    for h in (2 * (j - LATENT_AT[0]), 2 * (j - LATENT_AT[0]) + 1):
                        act.wait_ge(A["ql_m"], h + 1)
                        f(QL[:, h, :], BK[2 + h % 2][:, 0:SEQ], ACT.Copy).then_inc(A["ql_out"], 1)
            attend(DSA, lambda e: PL[e % 2][:, 0:SEQ], lambda h, e: h[:, e, LAT])
            attend(DIL, lambda e: BK[4 + e % 2][:, 0:SEQ], lambda h, e: h[:, 4 + e, LAT])
            residuals("out2", 1, None, SEQ, "cross")
            project("xq", copy_to("xq", QCF, SEQ))
            attend(CRS, lambda e: BK[4 + e % 2][:, 0:512].rearrange("p (c q) -> p c q", c=2), lambda h, e: h[:, 2 * e:2 * e + 2, LAT])
            residuals("xo", 1, None, SEQ, "mlp")
            AHF2 = AH2[:].rearrange("p a b -> p (a b)")
            with act.Fori(0, 8) as i:
                for s in range(4):
                    split(B0["up2"] + s + lead("up2"), 4 * i)
                    t = T0["up2"] + s
                    done(t, 4 * i)
                    act.wait_ge(act_lo, 2 * FC + s - 1 + 4 * i)
                    f(C1[:, s % 2, 0:SEQ], PL[t % 2][:, 0:SEQ], ACT.Relu).then_inc(tile_out, 1)
                    act.wait_ge(tile_out, t + 3 + 4 * i)
                    f(AHF2[:, ds(s * SEQ + 4 * SEQ * i, SEQ)], C1[:, s % 2, 0:SEQ], ACT.Square).then_inc(act_hi, 1)

            residuals("dn2", 4, None, SEQ, "final2")

        @block.vector
        def _(dve):
            v = nc.vector
            steps = [0]

            def link(ins):
                steps[0] += 1
                ins.then_inc(dve_step, 1)
                dve.wait_ge(dve_step, steps[0])

            def low(n, off=0):
                if n >= NBLK:
                    return
                dve.wait_ge(w_high, n + 1 + off)
                v.tensor_tensor(wl(n), RAW[:, n % 4, :], wh(n), ALU.subtract).then_inc(w_low, 1)

            def modulation(b, first, n, at=0):
                bias = C[:, COL_AT["ada_b"] + first:COL_AT["ada_b"] + first + n].unsqueeze(2).to_broadcast([P, n, 2])
                o = MODF[:, 2 * first:2 * (first + n)].rearrange("p (m s) -> p m s", s=2)
                return v.tensor_tensor(o, BK[b][:, 2 * at:2 * (at + n)].rearrange("p (m s) -> p m s", s=2), bias, ALU.add)

            def gains(layer, which):
                at = COL_AT["norm1" if which == 0 else "norm2"] + KC * layer
                g = C[:, at:at + KC].unsqueeze(2).to_broadcast([P, KC, 2])
                return v.scalar_tensor_tensor(GM[:, layer, which, :, :], MOD[:, layer, 3 * which + 1, :, :], 1.0, g, ALU.add, ALU.mult)

            def norm_factor(name):
                i = NORM_I[name]
                nt = NORMS[i][2] // P
                dve.wait_ge(n_root, i + 1)
                v.reciprocal(STD[:, 8:8 + nt], STD[:, 0:nt]).then_inc(n_std, 1)

            def norm(name):
                i = NORM_I[name]
                _, nch, width = NORMS[i]
                if name != "n1_0":
                    norm_factor(name)
                dve.wait_ge(n_bc, i + 1)
                layer, part = MODULATED.get(name, (0, 0))

                def low_part(k):
                    dve.wait_ge(n_hi, NORM_S0[name] + k + 1)
                    if name in MODULATED:
                        for x, s in streams(name):
                            last = v.scalar_tensor_tensor(norm_dst(name, k, 1)[:, x], TMP[:, k, x], MOD[:, layer, part, k, s:s + 1], norm_dst(name, k, 0)[:, x],
                                                          ALU.add, ALU.subtract)
                    else:
                        last = v.tensor_tensor(norm_dst(name, k, 1), TMP[:, k, 0:width], norm_dst(name, k, 0), ALU.subtract)
                    last.then_inc(n_lo, 1)

                for k in range(nch):
                    src = norm_src(name, k)
                    o = TMP[:, k, 0:width] if name in SPLIT else src
                    if name in MODULATED:
                        for x, s in streams(name):
                            ins = v.scalar_tensor_tensor(o[:, x], src[:, x], GM[:, layer, part // 3, k, s:s + 1], BK[0][:, x], ALU.mult, ALU.mult)
                    else:
                        gain = {"cq": "mla_q", "ckv": "mla_kv"}.get(name, name)
                        ins = v.scalar_tensor_tensor(o, src, col(gain, k), BK[0][:, 0:width], ALU.mult, ALU.mult)
                    ins.then_inc(n_xn, 1)
                    if name in SPLIT and k:
                        low_part(k - 1)
                if name in SPLIT:
                    low_part(nch - 1)

            def conv(t, k, cv, taps, width, it=0, per=0):
                n = width // SEQ
                o = C1[:, k % 2, 0:width].rearrange("p (s t) -> p s t", s=n)
                dve.wait_ge(tile_out, t + 3 + per * it)
                v.scalar_tensor_tensor(o, XP[:, k % 2, 0:n, 0:SEQ], C[:, ds(taps + 3 * k + 3 * per * it, 1)], o, ALU.mult, ALU.add).then_inc(conv_mid, 1)
                dve.wait_ge(conv_mid, cv + k + 1 + per * it)
                v.scalar_tensor_tensor(o, XP[:, k % 2, 0:n, 2:SEQ + 2], C[:, ds(taps + 3 * k + 2 + 3 * per * it, 1)], o, ALU.mult, ALU.add).then_inc(conv_done, 1)

            def add(name, m, width, it=0, per=0):
                t = T0[name] + m
                dve.wait_ge(tile_out, t + 3 + per * it)
                x = XF[:, ds(m * T2 + (T2 - width) + per * T2 * it, width)]
                v.tensor_tensor(x, x, (TYO if name == "out0" else TY)[:, t % 2, 0:width], ALU.add).then_inc(x_res, 1)

            norm_factor("n1_0")
            dve.wait_ge(cond_ready, 1)
            dve.wait_ge(a_used, A_FIRST)
            link(modulation(1, 0, A_FIRST))
            gains(0, 0).then_inc(mod_ready, 1)
            dve.wait_ge(mod_ready, 1)
            low(0)
            norm("n1_0")
            low(1)

            with dve.Fori(0, 2) as i:
                for s in range(4):
                    low(s + 2, 4 * i)
            with dve.Fori(0, 3) as i:
                for s in range(4):
                    low(8 + s + 2, 4 * i)
                    conv(8 + s, s, 0, COL_AT["bconv"], T2, i, 4)
            for t in range(20, 25):
                low(t + 2)
            dve.wait_ge(G["l2_root"], 1)
            v.reciprocal(L2[:, 1, :], L2[:, 0, :]).then_inc(G["l2_std"], 1)
            dve.wait_ge(a_used, 40)
            modulation(5, 16, 8).then_inc(x_res, 1)
            modulation(5, 24, 16, 8).then_inc(x_res, 1)
            dve.wait_ge(x_res, 2)
            gains(0, 1).then_inc(mod_ready, 1)

            v.memset(GT[:], 0.0).then_inc(G["g_rows"], 1)
            for j in range(8):
                dve.wait_ge(G["l2_bc"], j + 1)
                factor = BK[1 + j % 4][:]
                if j < 4:
                    ins = v.scalar_tensor_tensor(QKV[:, j, :], QKV[:, j, :], P ** -0.5, factor, ALU.mult, ALU.mult)
                else:
                    ins = v.tensor_tensor(QKV[:, j, :], QKV[:, j, :], factor, ALU.mult)
                ins.then_inc(G["l2_done"], 1)
            dve.wait_ge(G["g_in"], 1)
            link(v.scalar_tensor_tensor(GA[0:8, :], GA[0:8, :], 0.0, GB[0:8, :], ALU.max, ALU.add))
            v.tensor_scalar(GT[0:8, :], GA[0:8, :], SM[0:8, 4:5], -1.0, ALU.mult, ALU.mult).then_inc(G["g_soft"], 1)
            dve.wait_ge(G["g_tr"], 1)
            v.tensor_copy(GTOK[:], BK[0][:, 0:160].rearrange("p (t r) -> p t r", t=4)).then_inc(G["g_tok"], 1)
            dve.wait_ge(G["g_cs"], 1)
            v.tensor_copy(GC[:], BK[5][:, 0:64].rearrange("p (t d r) -> p t d r", t=4, d=2)).then_inc(G["g_cum"], 1)
            dve.wait_ge(G["g_cum"], 1)
            v.tensor_tensor(EK[:], GC[:, :, :, 4:8], GC[:, :, :, 0:4], ALU.subtract).then_inc(G["g_cum"], 1)
            dve.wait_ge(G["g_exp"], 1)
            link(v.tensor_tensor(BE[:], EG[:], GTOK[:, :, 32:40].rearrange("p t (d h) -> p t d h", d=2), ALU.mult))
            dve.wait_ge(G["g_exp"], 2)
            dve.wait_ge(gdn_in, 16)

            def keys(st, k):
                for tl, at in enumerate(TURNS[st]):
                    if k - at in (1, 2):
                        y = 2 * st + tl
                        dve.wait_ge(G["gv_t"], y + 1)
                        for d in range(2):
                            o, factor = ((KBG, BE), (KD, EK))[k - at - 1]
                            last = v.tensor_tensor(o[:, 2 * tl + d, :, :], PL[1][:].rearrange("p (a b) -> p a b", a=HEADS),
                                                   factor[:, y, d, :].unsqueeze(2).to_broadcast([P, HEADS, P]), ALU.mult)
                        last.then_inc(G["gv_k"], 1)

            def spatial_gate(k):
                if k == 13:
                    dve.wait_ge(G["vt_out"], 4)
                    v.tensor_scalar(SM[:, 54:58], SM[:, 50:54], -1.0 / 512, None, ALU.mult).then_inc(G["ln_mean"], 1)
                if k == 17:
                    dve.wait_ge(G["ln_std"], 1)
                    v.reciprocal(SM[:, 58:62], SM[:, 58:62]).then_inc(G["ln_r"], 1)
                    dve.wait_ge(G["ln_r"], 1)
                    dve.wait_ge(ws_in, 48)
                if 18 <= k < 22:
                    t = k - 18
                    x = UV[:, 4:8, t * P:(t + 1) * P]
                    v.tensor_scalar(x, x, SM[:, 54 + t:55 + t], SM[:, 58 + t:59 + t], ALU.add, ALU.mult).then_inc(G["ln_n"], 1)
                    dve.wait_ge(G["ln_n"], t + 1)
                    v.tensor_tensor(x, x, LNR[:, 0, :, :], ALU.mult).then_inc(G["ln_g"], 1)
                if k >= 24:
                    t = k - 24
                    x = UV[:, 0:4, t * P:(t + 1) * P]
                    dve.wait_ge(G["sp_s"], t + 1)
                    v.tensor_tensor(x, x, PL[t % 2][:].rearrange("p (a b) -> p a b", a=4), ALU.mult).then_inc(G["sp_y"], 1)

            def out_factor(st):
                dve.wait_ge(G["on_root"], st + 1)
                v.reciprocal(SM[:, 64:72], SM[:, 64:72]).then_inc(G["on_std"], 1)

            def out_norm(st):
                x = slice(st * SEQ, (st + 1) * SEQ)
                dve.wait_ge(G["on_bc"], st + 1)
                for p in range(2):
                    o = QKV[:, 8 + 2 * p:10 + 2 * p, x]
                    v.scalar_tensor_tensor(o, o, col("b_norm"), PL[p][:].rearrange("p (a b) -> p a b", a=2), ALU.mult, ALU.mult).then_inc(G["on_n"], 1)
                dve.wait_ge(G["on_n"], 2 * st + 2)
                v.tensor_tensor(QKV[:, 8:12, x], QKV[:, 8:12, x], GATE[:, :, x], ALU.mult).then_inc(G["on_y"], 1)

            def first_outputs(k):
                if k == 8:
                    out_factor(0)
                if k == 10:
                    out_norm(0)

            for st in range(2):
                def decays(q):
                    tl, d, z = q // 2, q % 2, 4 * st + q
                    dve.wait_ge(G["gb_e"], 2 * z + 1)
                    if z >= 2:
                        dve.wait_ge(G["gb_at"], z - 1)
                    for h in range(HEADS):
                        last = v.scalar_tensor_tensor(DT[:, z % 2, h, :], ROWS[q % 2][0][:, h * P:(h + 1) * P], GC[:, 2 * st + tl, d, h:h + 1], gtab("neg", d), ALU.subtract, ALU.add)
                    last.then_inc(G["gb_d"], 1)

                def triangles(q):
                    tl, d, z = q // 2, q % 2, 4 * st + q
                    dt = DT[:, z % 2, :, :]
                    dve.wait_ge(G["gb_e"], 2 * z + 2)
                    dve.wait_ge(G["gb_k"], 2 * st + tl + 1)
                    v.tensor_tensor(ATT[:, q, :, :], bank(3 + 2 * tl, 4, P), dt, ALU.mult)
                    for c in range(2):
                        e = 64 * c + (63 if d == 0 else 0)
                        v.tensor_copy(GEND[:, d, 2 * tl + c, :], ER[:, z % 2, :, e])
                    link(v.tensor_tensor(dt, dt, ROWS[q % 2][1][:].rearrange("p (a b) -> p a b", a=HEADS), ALU.mult))
                    v.tensor_tensor(AT[:, q, :, :], bank(2 + 2 * tl, 4, P), dt, ALU.mult).then_inc(G["gb_at"], 1)

                for q in (0, 2):
                    decays(q)
                    decays(q + 1)
                    triangles(q)
                    triangles(q + 1)
                eye = ID[:].unsqueeze(1).to_broadcast([P, HEADS, P])
                for k, (lev, q) in enumerate(LEVELS):
                    b = k % 2
                    if lev == 0:
                        dve.wait_ge(G["lv_m"], 24 * st + k + 1)
                        v.tensor_tensor(TT[:, q, :, :], eye, bank(b, 4, P), ALU.subtract)
                        v.tensor_tensor(TU[:, q, :, :], eye, CT[:, b, :, :], ALU.subtract).then_inc(G["lv_tu"], 1)
                    else:
                        dve.wait_ge(G["lv_x"], 20 * st + k - 3)
                        if lev < 5:
                            v.tensor_tensor(TT[:, q, :, :], TT[:, q, :, :], bank(2 + 2 * b, 4, P), ALU.subtract)
                        v.tensor_tensor(TU[:, q, :, :], TU[:, q, :, :], bank(3 + 2 * b, 4, P), ALU.subtract).then_inc(G["lv_tu"], 1)
                    keys(st, k)
                    (first_outputs if st else spatial_gate)(k)
                for q in range(4):
                    dve.wait_ge(G["uw_ready"], 4 * st + q + 1)
                    v.tensor_copy(WT[:, q, :, :], bank(3 + 2 * (q % 2), 4, P)).then_inc(G["w_out"], 1)
                dve.wait_ge(G["u_out"], 4 * st + 4)
                dve.wait_ge(G["s_init"], 1)
                dve.wait_ge(G["ln_v"], 4)
                for k in range(4):
                    n = 4 * st + k
                    for d in range(2):
                        _, q, po = chunk_place(st, k, d)
                        half = slice(po, po + 64)
                        dve.wait_ge(sc_w[d], n + 1)
                        v.tensor_tensor(VN[half, d, :, :], UU[half, q, :, :], bank(d, 4, P)[half], ALU.subtract).then_inc(sc_v[d], 1)
                    for d in range(2):
                        c, _, _ = chunk_place(st, k, d)
                        dve.wait_ge(sc_s[d], n + 1)
                        o = QKV[:, 8:12, st * SEQ + c * 64:st * SEQ + (c + 1) * 64]
                        new = BK[4 + d][:, 0:256].rearrange("p (h t) -> p h t", h=HEADS)
                        if k < 2:
                            v.tensor_copy(o, new)
                        else:
                            v.tensor_tensor(o, o, new, ALU.add)
                        if st == 0 and d == 0:
                            spatial_gate(24 + k - 1) if k else None
                        for h in range(HEADS):
                            last = v.scalar_tensor_tensor(S[:, d, h, :], S[:, d, h, :], GEND[:, d, c, h:h + 1], bank(2 + d, 4, P)[:, h, :], ALU.mult, ALU.add)
                        last.then_inc(sc_state[d], 1)
                if st == 0:
                    spatial_gate(27)
            out_factor(1)
            for t in range(4):
                tok = slice(t * P, (t + 1) * P)
                dve.wait_ge(G["sp_hi"], t + 1)
                v.tensor_tensor(HL[:, 0:4, tok], UV[:, 0:4, tok], HH[:, 0:4, tok], ALU.subtract).then_inc(G["y_a"], 1)
            out_norm(1)
            for st, x in enumerate((CTX, LAT)):
                dve.wait_ge(G["on_hi"], st + 1)
                v.tensor_tensor(HL[:, 4:8, x], QKV[:, 8:12, x], HH[:, 4:8, x], ALU.subtract).then_inc(G["y_b"], 1)

            def project(name, width=None, loops=2):
                with dve.Fori(0, loops) as i:
                    for s in range(4):
                        low(B0[name] + s + lead(name), 4 * i)
                        if width:
                            add(name, s, width, i, 4)

            def up(layer, ah, al, width):
                name = f"up{layer}"
                cv, taps = 12 + 2 * FC * layer, COL_AT["fconv"] + 2 * FC * 3 * layer
                ahf, alf = ah[:].rearrange("p a b -> p (a b)"), al[:].rearrange("p a b -> p (a b)")
                def more(s, i):
                    low(B0[name] + s + lead(name), 4 * i)

                def outer_taps(s, i):
                    conv(T0[name] + s, s, cv, taps, width, i, 4)

                def gated(p, i):
                    dve.wait_ge(silu_done, 12 + FC * layer + p + 1 + 2 * i)
                    dve.wait_ge(conv_done, cv + 2 * p + 4 + 4 * i)
                    v.tensor_tensor(A32[:, 0:width], SG[:, 0:width], C1[:, 1, 0:width], ALU.mult).then_inc(act_done, 1)

                def low_part(p, i):
                    dve.wait_ge(act_hi, FC * layer + p + 1 + 2 * i)
                    o = ds(p * width + 2 * width * i, width)
                    v.tensor_tensor(alf[:, o], A32[:, 0:width], ahf[:, o], ALU.subtract).then_inc(act_lo, 1)

                def step(i, first=False):
                    outer_taps(0, i)
                    if not first:
                        low_part(-1, i)
                    more(0, i)
                    outer_taps(1, i)
                    more(1, i)
                    gated(0, i)
                    outer_taps(2, i)
                    more(2, i)
                    low_part(0, i)
                    outer_taps(3, i)
                    gated(1, i)
                    more(3, i)

                step(0, True)
                with dve.Fori(1, FC // 2) as i:
                    step(i)
                low_part(1, FC // 2 - 1)

            def down(layer, width):
                name = f"dn{layer}"
                with dve.Fori(0, 2) as i:
                    for m in range(4):
                        for k in range(3):
                            low(B0[name] + 3 * m + k + lead(name), 12 * i)
                        add(name, m, width, i, 4)

            def rest(name):
                for b in range(next(n for s, n, _ in STAGES if s == name)):
                    low(B0[name] + b + lead(name))

            project("out0", T2)
            dve.wait_ge(a_used, 52)
            modulation(1, 40, 12).then_inc(mod_ready, 1)
            dve.wait_ge(mod_ready, 3)
            norm("n2_0")
            up(0, AH0, AL0, T2)
            dve.wait_ge(a_used, A_ALL)
            link(modulation(5, 52, 44))
            gains(1, 0)
            gains(1, 1).then_inc(mod_ready, 1)
            dve.wait_ge(mod_ready, 4)
            down(0, T2)

            norm("n1_1")
            low(B0["in1"] + 2)
            rest("in1")
            norm("cq")
            norm("ckv")
            rest("uq")
            norm("mem")
            rest("ukv_k")

            def rotate(tiles, r0, some):
                for i in some:
                    x, _, which = tiles[i]
                    cos, sin = ("cm", "sm") if which == "m" else ("c" + which, "s" + which)
                    dve.wait_ge(A["rp_m"], r0 + i + 1)
                    v.tensor_tensor(RT[:, i % 2, :], BK[2 + i % 2][:, 0:SEQ], ltab(sin), ALU.mult)
                    link(v.tensor_tensor(x, x, ltab(cos), ALU.mult))
                    v.tensor_tensor(x, x, RT[:, i % 2, :], ALU.add).then_inc(A["rp_d"], 1)

            dve.wait_ge(late_in, 16)
            dve.wait_ge(n_lo, NORM_S0["mem"] + KC)
            rotate(ROPE1, 0, range(len(ROPE1)))
            rest("ukv_v")

            def attend(ly, out_bank, out_chunks, mask=None):
                for a in range(ly.steps):
                    w = ly.kt * P
                    if a < ly.n:
                        r = a % 3
                        src = ly.banks[a % len(ly.banks)][:, 0:w]
                        dve.wait_ge(A["at_s"], ly.a0 + a + 1)
                        if ly.masked:
                            link(v.scalar_tensor_tensor(SX[:, a % 2, :], src, ly.scale, mask(a % 2), ALU.mult, ALU.add))
                            src = SX[:, a % 2, :]
                        link(v.tensor_reduce(SM[:, 16 + r:17 + r], src, AX.X, ALU.max))
                        v.tensor_scalar(SM[:, 20 + r:21 + r], SM[:, 16 + r:17 + r], -1.0 if ly.masked else -ly.scale, None, ALU.mult).then_inc(A["at_m"], 1)
                    if 1 <= a <= ly.n:
                        p = a - 1
                        r = p % 3
                        dve.wait_ge(A["at_p"], ly.a0 + p + 1)
                        if ly is DIL:
                            link(v.scalar_tensor_tensor(PB[:, r, 0:w], PB[:, r, 0:w], 1.0, ltab("dcnt", p % 2), ALU.mult, ALU.mult, accum_out=SM[:, 24 + r:25 + r]))
                        link(v.reciprocal(SM[:, 28 + r:29 + r], SM[:, 24 + r:25 + r]))
                        v.tensor_scalar(PB[:, r, 0:w], PB[:, r, 0:w], SM[:, 28 + r:29 + r], None, ALU.mult).then_inc(A["at_n"], 1)
                    if a >= ly.lag and (a - ly.lag) % ly.per == 0:
                        e = (a - ly.lag) // ly.per
                        dve.wait_ge(A["at_hi"], ly.e0 + e + 1)
                        v.tensor_tensor(out_chunks(HL, e), out_bank(e), out_chunks(HH, e), ALU.subtract).then_inc(A["at_y"], 1)

            attend(MLA, lambda e: BK[4 + e % 2][:, 0:SEQ], lambda h, e: h[:, e, LAT])
            project("out1", SEQ)
            norm("n2_1")
            up(1, AH1, AL1, SEQ)
            down(1, SEQ)
            norm("final1")

            norm("mix")
            project("in2", None, 5)
            low(B0["in2"] + 20 + lead("in2"))
            low(B0["in2"] + 21 + lead("in2"))
            rest("in2_v")
            norm("kv2")
            causal = LTAB[:, LATE_AT["causal"]:LATE_AT["causal"] + 2 * SEQ].rearrange("p (t k) -> p t k", t=2)
            for j in range(SIDE):
                low((B0["xk"] + j if j < 8 else B0["xv"] + j - 8) + lead("xk"))
                rotate(ROPE2, len(ROPE1), ROTATE_AT[j])
                if j == 2:
                    dve.wait_ge(A["we_t"], 1)
                    v.tensor_scalar(WE[:], BK[4][:, 0:16].rearrange("p (t h) -> p t h", t=2), 8 ** -0.5 * 64 ** -0.5, None, ALU.mult).then_inc(A["we_ready"], 1)
                    dve.wait_ge(A["we_ready"], 1)
                if j in INDEX_AT:
                    for c in range(4 * (j - INDEX_AT[0]), 4 * (j - INDEX_AT[0]) + 4):
                        qt, h = c // 8, c % 8
                        dve.wait_ge(A["ix_r"], c + 1)
                        if c:
                            dve.wait_ge(A["ix_a"], c)
                        if h == 0:
                            ins = v.tensor_scalar(IX[:, qt, :], RL[:, c % 2, :], WE[:, qt, h:h + 1], None, ALU.mult)
                        else:
                            ins = v.scalar_tensor_tensor(IX[:, qt, :], RL[:, c % 2, :], WE[:, qt, h:h + 1], IX[:, qt, :], ALU.mult, ALU.add)
                        ins.then_inc(A["ix_a"], 1)
                if j == TOP_AT[0]:
                    dve.wait_ge(A["ix_a"], 16)
                    link(v.tensor_tensor(IX[:], IX[:], causal, ALU.add))
                if j in TOP_AT:
                    v.max(M8[:, 0, :], IX[:, 0, :])
                    link(v.max(M8[:, 1, :], IX[:, 1, :]))
                    v.match_replace(IX[:, 0, :], M8[:, 0, :], IX[:, 0, :], TAKEN)
                    link(v.match_replace(IX[:, 1, :], M8[:, 1, :], IX[:, 1, :], TAKEN))
            link(v.tensor_scalar(AM[:], IX[:], -2e38, NEG, ALU.is_gt, ALU.mult))
            link(v.tensor_tensor(AM[:], AM[:], causal, ALU.add))
            attend(DSA, lambda e: PL[e % 2][:, 0:SEQ], lambda h, e: h[:, e, LAT], lambda qt: AM[:, qt, :])
            attend(DIL, lambda e: BK[4 + e % 2][:, 0:SEQ], lambda h, e: h[:, 4 + e, LAT], lambda qt: ltab("dneg", qt))
            project("out2", SEQ)
            norm("cross")
            project("xq")
            attend(CRS, lambda e: BK[4 + e % 2][:, 0:512].rearrange("p (c q) -> p c q", c=2), lambda h, e: h[:, 2 * e:2 * e + 2, LAT])
            project("xo", SEQ)
            norm("mlp")
            ahf, alf = AH2[:].rearrange("p a b -> p (a b)"), AL2[:].rearrange("p a b -> p (a b)")
            with dve.Fori(0, 8) as i:
                for s in range(4):
                    low(B0["up2"] + s + lead("up2"), 4 * i)
                    dve.wait_ge(tile_out, T0["up2"] + s + 3 + 4 * i)
                    half = slice(s % 2 * SEQ, (s % 2 + 1) * SEQ)
                    v.tensor_tensor(A32[:, half], C1[:, s % 2, 0:SEQ], C1[:, s % 2, 0:SEQ], ALU.mult).then_inc(act_done, 1)
                    dve.wait_ge(act_done, 2 * FC + s + 1 + 4 * i)
                    dve.wait_ge(act_hi, 2 * FC + s + 1 + 4 * i)
                    o = ds(s * SEQ + 4 * SEQ * i, SEQ)
                    v.tensor_tensor(alf[:, o], A32[:, half], ahf[:, o], ALU.subtract).then_inc(act_lo, 1)

            with dve.Fori(0, 3) as i:
                for m in range(2):
                    for k in range(4):
                        low(B0["dn2"] + 4 * m + k + lead("dn2"), 8 * i)
                    add("dn2", m, SEQ, i, 2)
            for m in (6, 7):
                for k in range(4):
                    low(B0["dn2"] + 4 * m + k + lead("dn2"))
                add("dn2", m, SEQ)
            norm("final2")


def kernel(**inputs):
    import numpy as np
    import concourse.bacc as bacc
    from concourse.bass_utils import run_bass_kernel_spmd

    arrays = {k: np.ascontiguousarray(v) for k, v in lay_out({k: np.asarray(v) for k, v in inputs.items()}).items()}
    nc = bacc.Bacc("TRN2", target_bir_lowering=False, num_devices=1)
    args = [nc.dram_tensor(k, v.shape, mybir.dt.float32, kind="ExternalInput").ap() for k, v in arrays.items()]
    out = nc.dram_tensor("out", (P, KC, SEQ), mybir.dt.float32, kind="ExternalOutput").ap()
    two_blocks_kernel(nc, *args, out)
    r = run_bass_kernel_spmd(nc, [arrays], core_ids=[0])
    y = r.results[0]["out"]
    return np.ascontiguousarray(y.transpose(2, 1, 0).reshape(1, SEQ, D))
```

```python
from contextlib import ExitStack

import concourse.bass as bass
from concourse import mybir

P = 128
D = 1024
KC = D // P
SEQ = 256
T2 = 2 * SEQ
D_FF = 2816
FC = D_FF // P
D_FF_2 = 4096
HEADS = 4
EPS = 1e-6
NEG = -1e30
TAKEN = -3e38
BLOCK_CHUNKS = 8
BLOCK = BLOCK_CHUNKS * P

COLS = [("cond", 2 * KC), ("ada_b", 96), ("norm1", 16), ("norm2", 16), ("bconv", 36), ("dt_bias", 1), ("a_log", 1),
        ("a_ln_g", 4), ("a_ln_b", 4), ("b_norm", 1), ("mla_q", 3), ("mla_kv", 2), ("fconv", 2 * 2 * FC * 3),
        ("final1", 8), ("mix", 8), ("kv2", 1), ("cross", 8), ("mem", 8), ("mlp", 8), ("final2", 8), ("eps", 1), ("one", 1)]
COL_AT = {}
_n = 0
for _name, _w in COLS:
    COL_AT[_name] = _n
    _n += _w
NCOLS = _n

GDN_TABLES = [("cum", 2 * P), ("blk", P), ("neg", 2 * P), ("lev", 12 * P)]
LATE_TABLES = [("perm64", P), ("perm32", P), ("cm", SEQ), ("sm", SEQ), ("c64", SEQ), ("s64", SEQ), ("c32", SEQ),
               ("s32", SEQ), ("causal", 2 * SEQ), ("dneg", 2 * SEQ), ("dcnt", 2 * SEQ)]
GDN_AT, LATE_AT = {}, {}
_n = 0
for _name, _w in GDN_TABLES:
    GDN_AT[_name] = _n
    _n += _w
NGDN = _n
_n = 0
for _name, _w in LATE_TABLES:
    LATE_AT[_name] = _n
    _n += _w
NLATE = _n

STAGES = [("in0", 25, 25), ("out0", 8, 8), ("up0", 44, 44), ("dn0", 24, 8), ("in1", 6, 6), ("uq", 5, 12), ("ukv_k", 2, 8),
          ("ukv_v", 2, 8), ("out1", 8, 8), ("up1", 44, 44), ("dn1", 24, 8), ("in2", 22, 22), ("in2_v", 4, 2), ("xk", 8, 8),
          ("xv", 8, 4), ("out2", 8, 8), ("xq", 8, 8), ("xo", 8, 8), ("up2", 32, 32), ("dn2", 32, 8)]
B0, T0 = {}, {}
_b = _t = 0
for _name, _nb, _nt in STAGES:
    B0[_name], T0[_name] = _b, _t
    _b += _nb
    _t += _nt
NBLK = _b

NORMS = [("n1_0", 8, T2), ("n2_0", 8, T2), ("n1_1", 8, T2), ("cq", 3, SEQ), ("ckv", 2, T2), ("mem", 8, SEQ), ("n2_1", 8, SEQ), ("mix", 8, SEQ),
         ("final1", 8, SEQ), ("kv2", 1, SEQ), ("cross", 8, SEQ), ("mlp", 8, SEQ), ("final2", 8, SEQ)]
NORM_I = {n: i for i, (n, _, _) in enumerate(NORMS)}
SPLIT = {"n1_0", "n2_0", "n1_1", "cq", "ckv", "n2_1", "mix", "cross", "mem", "mlp"}
MODULATED = {"n1_0": (0, 0), "n2_0": (0, 3), "n1_1": (1, 0), "n2_1": (1, 3)}
SUMMED = ("n1_0", "n2_0", "n1_1", "n2_1", "mix", "final1", "cross", "mlp", "final2")
EARLY = KC - 2
NORM_C0, NORM_S0 = {}, {}
_c = _s = 0
for _name, _nc, _ in NORMS:
    NORM_C0[_name], NORM_S0[_name] = _c, _s
    _c += _nc
    _s += _nc if _name in SPLIT else 0

A_FIRST = 16
A_ALL = 96
PAIRS_IN, PAIRS_UP = 12, FC - 1
PAIRS = (A_ALL - A_FIRST) // 2
PAIR_OPS = (7, KC)


def tables():
    import numpy as np
    f = np.float32
    j, i = np.arange(P)[:, None], np.arange(P)[None, :]
    same = (j // 64) == (i // 64)
    cum = [same & (j <= i), same & (j >= i)]
    lev = []
    for d in range(2):
        for s in (1, 2, 4, 8, 16, 32):
            pair = (j // (2 * s)) == (i // (2 * s))
            lo, hi = (j // s) % 2, (i // s) % 2
            lev.append(pair & ((lo == 0) & (hi == 1) if d == 0 else (lo == 1) & (hi == 0)))
    gdn = np.concatenate([c.astype(f) for c in cum] + [same.astype(f)] + [np.where(c, 0, NEG).astype(f) for c in cum]
                         + [m.astype(f) for m in lev], axis=1)

    def perm(w):
        m = np.zeros((P, P), f)
        p = np.arange(P)
        m[(p // w) * w + (p % w + w // 2) % w, p] = 1
        return m

    def rope(ang, w):
        p = np.arange(P) % w
        c, s = np.cos(ang).astype(f), np.sin(ang).astype(f)
        return c.T[p % (w // 2)], s.T[p % (w // 2)] * np.where(p < w // 2, -1, 1).astype(f)[:, None]

    t = np.arange(SEQ, dtype=f)
    inv = (f(10000.0) ** (-np.arange(16, dtype=f) / f(16))).astype(f)
    cm, sm = rope(np.concatenate([np.floor(t / 64)[:, None] * inv, (t % 64)[:, None] * inv], axis=1), 64)
    inv64 = (f(10000.0) ** (-np.arange(0, 64, 2, dtype=f) / f(64))).astype(f)
    inv32 = (f(10000.0) ** (-np.arange(0, 32, 2, dtype=f) / f(32))).astype(f)
    c64, s64 = rope(t[:, None] * inv64, 64)
    c32, s32 = rope(t[:, None] * inv32, 32)
    q, k = np.arange(SEQ)[:, None], np.arange(SEQ)[None, :]
    back = q - k
    count = sum(((back >= 0) & (back <= w) & (back % dil == 0)).astype(f) for w, dil in ((128, 1), (512, 4), (2048, 16)))

    def rows(m):
        return m.reshape(2, P, SEQ).transpose(1, 0, 2).reshape(P, 2 * SEQ).astype(f)

    late = np.concatenate([perm(64), perm(32), cm, sm, c64, s64, c32, s32, rows(np.where(back >= 0, 0, NEG)),
                           rows(np.where(count > 0, 0, NEG)), rows(count)], axis=1).astype(f)
    return gdn, late


def lay_out(a):
    import numpy as np
    f = np.float32
    z = lambda *s: np.zeros(s, f)
    tr = lambda m: np.ascontiguousarray(m.T.reshape(KC, P, -1).transpose(1, 0, 2))

    def tiles(w, pad=0):
        k, m = w.shape
        b = w.reshape(k // P, P, m // P, P).transpose(2, 1, 0, 3)
        if pad:
            b = np.concatenate([b, z(b.shape[0], P, pad, P)], axis=2)
        return b

    def blocks(w, pad=0):
        b = tiles(w, pad)
        m, _, k, _ = b.shape
        if k >= BLOCK_CHUNKS:
            n = k // BLOCK_CHUNKS
            return b.reshape(m, P, n, BLOCK).transpose(0, 2, 1, 3).reshape(m * n, P, BLOCK)
        b = b.transpose(1, 0, 2, 3).reshape(P, m * k, P)
        n = -(-m * k // BLOCK_CHUNKS)
        b = np.concatenate([b, z(P, n * BLOCK_CHUNKS - m * k, P)], axis=1)
        return b.reshape(P, n, BLOCK).transpose(1, 0, 2)

    def moving(w):
        k, m = w.shape
        b = w.reshape(k // 256, 2, P, m // 512, 512).transpose(3, 0, 2, 1, 4)
        return b.reshape(-1, P, BLOCK)

    def narrow(w):
        k, m = w.shape
        return w.reshape(k // 512, 4, P, m // 256, 256).transpose(3, 0, 2, 1, 4).reshape(-1, P, BLOCK)

    def wide(w):
        return np.concatenate([w, z(w.shape[0], -w.shape[1] % P)], axis=1)

    wi = a["ab_w_in"][0]
    ab = z(D, P)
    ab[:, 0:8], ab[:, 32:40] = wi[:, 3072:3080], wi[:, 3080:3088]
    pairs = np.array([[j, FC + j] for j in range(FC)]).ravel()
    ffn_cols = (pairs[:, None] * P + np.arange(P)).ravel()
    uq = a["mla_w_uq"][0].reshape(384, 8, 192)
    ukv = a["mla_w_ukv"][0].reshape(256, 8, 256)
    w2 = a["w_in_2"][0]
    mi = a["mla_w_in"][0]
    kvc = a["w_kv_cross_2"][0]
    w_in2 = np.concatenate([w2[:, 0:896], np.tile(w2[:, 896:928], (1, 4)), np.tile(w2[:, 1440:1504], (1, 2)),
                            wide(w2[:, 1504:1512]), w2[:, 928:1440], w2[:, 1512:2536]], axis=1)
    stream = [blocks(np.concatenate([wi[:, 0:2560], ab, wi[:, 2560:3072]], axis=1)), blocks(a["ab_w_out"][0]),
              blocks(a["ffn_w_up"][0][:, ffn_cols]), blocks(a["ffn_w_down"][0], 2),
              blocks(np.concatenate([mi, mi[:, 640:704]], axis=1)),
              blocks(np.concatenate([uq[:, :, :128].reshape(384, -1), uq[:, :, 128:].reshape(384, -1)], axis=1)),
              blocks(np.ascontiguousarray(ukv[:, :, :128]).reshape(256, -1)), moving(np.ascontiguousarray(ukv[:, :, 128:]).reshape(256, -1)),
              blocks(a["mla_w_out"][0]), blocks(a["ffn_w_up"][1][:, ffn_cols]), blocks(a["ffn_w_down"][1], 2),
              blocks(w_in2), moving(w2[:, 2536:3048]), blocks(kvc[:, :1024]), moving(kvc[:, 1024:]),
              blocks(a["w_out_2"][0]), blocks(a["w_q_cross_2"][0]), blocks(a["w_o_cross_2"][0]), blocks(a["w_up_2"][0]), blocks(a["w_down_2"][0])]
    assert [len(s) for s in stream] == [n for _, n, _ in STAGES]
    vec = lambda v: v.reshape(-1, P).T
    dt_bias, a_log = z(P, 1), z(P, 1)
    dt_bias[:8, 0], a_log[:8, 0] = a["b_dt_bias"][0].ravel(), a["b_a_log"][0].ravel()
    cols = [np.stack([vec(a["c_ctx"]), vec(a["c"][0])], axis=2).reshape(P, -1),
            np.concatenate([vec(a["ada_b"][i]) for i in range(2)], axis=1),
            np.concatenate([vec(a["norm1_g"][i]) for i in range(2)], axis=1),
            np.concatenate([vec(a["norm2_g"][i]) for i in range(2)], axis=1),
            a["b_conv_w"][0].reshape(3, 12, P).transpose(2, 1, 0).reshape(P, -1), dt_bias, a_log,
            vec(a["a_ln_g"][0]), vec(a["a_ln_b"][0]), vec(a["b_norm_g"][0]), vec(a["mla_q_norm_g"][0]), vec(a["mla_kv_norm_g"][0]),
            np.concatenate([a["ffn_conv_w"][i][:, ffn_cols].reshape(3, 2 * FC, P).transpose(2, 1, 0).reshape(P, -1) for i in range(2)], axis=1),
            vec(a["final_g"]), vec(a["norm_mix_g_2"][0]), vec(a["kv_norm_g_2"][0]), vec(a["norm_cross_g_2"][0]),
            vec(a["norm_mem_g_2"][0]), vec(a["norm_mlp_g_2"][0]), vec(a["norm_final_g_2"]), np.full((P, 1), EPS, f), np.ones((P, 1), f)]
    gdn, late = tables()
    return {
        "x_in": np.concatenate([tr(a["ctx"][0]), tr(a["x"][0])], axis=2),
        "mem_in": tr(a["mem_2"][0]),
        "a_head": moving(a["ada_w"][0][:, :A_FIRST * P]),
        "a_stream": np.concatenate([narrow(a["ada_w"][0][:, A_FIRST * P:]), narrow(a["ada_w"][1])]),
        "w_stream": np.concatenate(stream),
        "cols": np.ascontiguousarray(np.concatenate(cols, axis=1)),
        "gdn_tables": gdn, "late_tables": late, "ident": np.eye(P, dtype=f),
        "ws_t": np.ascontiguousarray(a["a_ws"][0].transpose(2, 0, 1)),
        "bs_row": a["a_bs"][0].reshape(1, 512),
        "ln_rows": np.tile(np.concatenate([a["a_ln_g"][0], a["a_ln_b"][0]]), (P, 1)),
        "w_uk": np.ascontiguousarray(a["w_uk_2"][0].reshape(4, P, P).transpose(1, 0, 2)),
        "w_uv": np.ascontiguousarray(a["w_uv_2"][0].transpose(1, 0, 2)),
    }


DONE_BLOCK, DONE_TILE = {}, {}


def count_signals():
    n = 0
    for name, nb, nt in STAGES:
        b, t = B0[name], T0[name]
        if name in ("uq", "ukv_k"):
            per = 3 if name == "uq" else 2
            for m in range(nt):
                n += 1
                DONE_TILE[t + m] = n
                for k in range(nb):
                    if min(8 * k + 7, per * nt - 1) // per == m:
                        DONE_BLOCK[b + k] = n
        elif name == "ukv_v":
            for m in range(nt):
                n += 1
                DONE_TILE[t + m] = n
                DONE_BLOCK[b + m // 4] = n
        elif name in ("in2_v", "xv"):
            for k in range(nb):
                for tok in range(2):
                    n += 1
                    DONE_TILE[t + 2 * (k // 4) + tok] = n
                DONE_BLOCK[b + k] = n
        else:
            for k in range(nb):
                n += 1
                DONE_BLOCK[b + k] = n
                DONE_TILE[t + k * nt // nb] = n


count_signals()


def two_blocks_kernel(nc, x_in, mem_in, a_head, a_stream, w_stream, cols, gdn_tables, late_tables, ident, ws_t, bs_row, ln_rows, w_uk, w_uv, out):
    F32, F32R = mybir.dt.float32, mybir.dt.float32r
    ALU, ACT, AX = mybir.AluOpType, mybir.ActivationFunctionType, mybir.AxisListType
    ds = bass.ds
    ctx = ExitStack()
    with ctx:
        base = -(-nc.sbuf_base // 64) * 64
        end = nc.sbuf_usable_end // 32 * 32
        cursor = [base]

        def place(name, shape, dt=F32):
            size = 4
            for s in shape[1:]:
                size *= s
            size = -(-size // 32) * 32
            t = nc.alloc_sbuf_tensor_at(name, shape, dt, offset=cursor[0])
            cursor[0] += size
            assert cursor[0] <= end, (name, cursor[0] - end)
            return t

        RAW = place("w_raw", [P, 4, BLOCK])
        WH = place("w_high", [P, 2, BLOCK], F32R)
        WL = place("w_low", [P, 2, BLOCK], F32R)
        a_ring_at = cursor[0]
        AR = place("a_ring", [P, 2, BLOCK])
        X = place("x", [P, KC, T2])
        C = place("cols_sb", [P, NCOLS])
        MOD = place("mod", [P, 2, 6, KC, 2])
        GM = place("gains", [P, 2, 2, KC, 2])
        ID = place("ident_sb", [P, P])
        ONES = place("ones", [P, P])
        STD = place("std", [P, T2])
        SM = place("small", [P, 72])
        XP = place("conv_in", [P, 2, 2, SEQ + 2])
        tmp_at = cursor[0]
        TMP = place("tmp", [P, KC, T2])
        after_tmp = cursor[0]
        HH = place("h_high", [P, KC, T2], F32R)
        HL = place("h_low", [P, KC, T2], F32R)
        zone = cursor[0]
        cursor[0] = after_tmp
        A16 = place("a_first", [P, A_FIRST, BLOCK])
        MR = place("mod_rows", [2, 4, 512])
        cursor[0] = tmp_at
        C1 = place("conv_mid", [P, 2, T2])
        SG = place("silu_g", [P, T2])
        A32 = place("act", [P, T2])
        cursor[0] = after_tmp
        SQN = place("squares_n1_1", [P, KC, T2])
        cursor[0] = tmp_at + 6 * T2 * 4
        ACC1 = place("mod_sums1", [P, 2, 2, 256])
        cursor[0] = tmp_at
        GA = place("gate_a", [40, T2])
        GB = place("gate_b", [40, T2])
        GT = place("gate_t", [40, T2])
        SQL = place("qk_squares", [P, 4, T2])
        L2 = place("qk_lengths", [P, 2, 32])
        cursor[0] = tmp_at
        CT = place("lev_ct", [P, 2, HEADS, P])
        M1 = place("lev_m1", [P, 2, HEADS, P])
        decay_at = cursor[0]
        DT = place("decay", [P, 2, HEADS, P])
        ER = place("exp_cum", [P, 2, HEADS, P])
        cursor[0] = decay_at
        VN = place("v_new", [P, 2, HEADS, P])
        cursor[0] = decay_at
        ONQ = place("out_squares", [P, HEADS, SEQ])
        cursor[0] = decay_at
        LNR = place("ln_rows_sb", [P, 2, 4, P])
        WS = place("ws_sb", [P, 4, P])
        BS = place("bs_sb", [1, 512])
        cursor[0] = zone
        QKV = place("qkv", [P, 12, T2])
        UV = place("uv", [P, 8, T2])
        GATE = place("gate", [P, 4, T2])
        GTAB = place("gdn_tab", [P, NGDN])
        GTOK = place("g_tok", [P, 4, 40])
        GC = place("g_cum", [P, 4, 2, 8])
        EG = place("e_cum", [P, 4, 2, HEADS])
        EK = place("e_rest", [P, 4, 2, HEADS])
        BE = place("beta_e", [P, 4, 2, HEADS])
        GEND = place("g_end", [P, 2, 4, HEADS])
        inverse_at = cursor[0]
        ACC0 = place("mod_sums0", [P, 2, 2, 256])
        PROD0 = place("mod_products0", [P, 4, 256])
        cursor[0] = inverse_at
        TT = place("inv_t", [P, 4, HEADS, P])
        TU = place("inv_u", [P, 4, HEADS, P])
        ATT = place("attn_t", [P, 4, HEADS, P])
        QG0 = place("qg0", [P, 2, HEADS, P])
        S = place("state", [P, 2, HEADS, P])
        cursor[0] = after_tmp
        VB = place("v_beta", [P, 4, HEADS, P])
        KBG = place("k_beta_g", [P, 4, HEADS, P])
        KD = place("k_decay", [P, 4, HEADS, P])
        AT = place("a_t", [P, 4, HEADS, P])
        UU, WT = AT, TT
        cursor[0] = zone
        AH0 = place("act_high0", [P, FC, T2], F32R)
        AL0 = place("act_low0", [P, FC, T2], F32R)
        PROD1 = place("mod_products1", [P, 4, 256])
        cursor[0] = zone
        LTAB = place("late_tab", [P, NLATE])
        late = cursor[0]
        CQ = place("cq", [P, 3, SEQ])
        CKV = place("ckv", [P, 2, T2])
        KR = place("kr", [P, T2])
        MQ = place("mla_q", [P, 12, SEQ])
        KN = place("mla_k", [P, 8, T2])
        VT = place("mla_v", [P, 4, 1024])
        CQH = place("cq_high", [P, 3, SEQ], F32R)
        CQL = place("cq_low", [P, 3, SEQ], F32R)
        CKH = place("ckv_high", [P, 2, T2], F32R)
        CKL = place("ckv_low", [P, 2, T2], F32R)
        cursor[0] = late
        AH1 = place("act_high1", [P, FC, SEQ], F32R)
        AL1 = place("act_low1", [P, FC, SEQ], F32R)
        cursor[0] = late
        PJ = place("proj", [P, 22, SEQ])
        VBK = place("dil_v", [P, 2, 512])
        CTK = place("c_tok", [P, 2, P])
        QL = place("q_lat", [P, 8, SEQ])
        OL = place("o_lat", [P, 2, SEQ])
        IX = place("index", [P, 2, SEQ])
        RL = place("relu", [P, 2, SEQ])
        AM = place("top_mask", [P, 2, SEQ])
        WE = place("w_eff", [P, 2, 8])
        M8 = place("max8", [P, 2, 8])
        WUK = place("w_uk_sb", [P, 4, P])
        WUV = place("w_uv_sb", [P, 8, 64])
        KCR = place("cross_k", [P, 8, SEQ])
        VC = place("cross_v", [P, 2, 1024])
        cursor[0] = late
        QC = place("cross_q", [P, 8, SEQ])
        cursor[0] = late
        AH2 = place("act_high2", [P, 32, SEQ], F32R)
        AL2 = place("act_low2", [P, 32, SEQ], F32R)
        late_end = end - 2 * BLOCK * 4
        cursor[0] = a_ring_at
        WH2 = place("w_high2", [P, 2, BLOCK], F32R)
        cursor[0] = late_end
        WL2 = place("w_low2", [P, 2, BLOCK], F32R)
        cursor[0] = tmp_at
        PB = place("probs", [P, 3, T2])
        PT = place("probs_t", [P, 2, 4, P])
        SX = place("scores", [P, 2, SEQ])
        RT = place("rot", [P, 2, SEQ])

        def slot(n):
            late_block = n - B0["in1"]
            return n % 2 if late_block < 0 else (B0["in1"] % 2, 1 - B0["in1"] % 2, 2, 3)[late_block % 4]

        def slot_before(n):
            late_block = n - B0["in1"]
            return n - 2 if late_block < 2 else B0["in1"] - 1 if late_block < 4 else n - 4

        def lead(name):
            return 2 if B0[name] < B0["in1"] else 3

        def wh(n):
            return WH[:, slot(n), :] if slot(n) < 2 else WH2[:, slot(n) - 2, :]

        def wl(n):
            return WL[:, slot(n), :] if slot(n) < 2 else WL2[:, slot(n) - 2, :]

        PL = [ctx.enter_context(nc.psum_tensor(f"proj{i}", [P, 512], F32)) for i in range(2)]
        BK = [ctx.enter_context(nc.psum_tensor(f"bank{i}", [P, 512], F32)) for i in range(6)]

        MROWS = [BK[1], BK[5], PL[0], PL[1]]
        ROWS = [(BK[0], BK[1]), (PL[0], PL[1])]
        SUMS = [BK[i] for i in (0, 2, 3, 4)]
        OUT_BANKS = (PL, BK[0:2])

        def bank(i, a, b):
            return BK[i][:, 0:a * b].rearrange("p (a b) -> p a b", a=a)

        def col(name, j=0):
            return C[:, COL_AT[name] + j:COL_AT[name] + j + 1]

        def gtab(name, j=0):
            return GTAB[:, GDN_AT[name] + j * P:GDN_AT[name] + (j + 1) * P]

        def ltab(name, j=0, w=SEQ):
            return LTAB[:, LATE_AT[name] + j * w:LATE_AT[name] + (j + 1) * w]

        def sem(name):
            return ctx.enter_context(nc.semaphore(name))

        cols_in, x_ready, gdn_in, ws_in, late_in, uk_in, mem_ready, out_done = map(
            sem, ("cols_in", "x_ready", "gdn_in", "ws_in", "late_in", "uk_in", "mem_ready", "out_done"))
        a_first = [sem(f"a_first{i}") for i in range(4)]
        w_landed = [sem(f"w_landed{i}") for i in range(4)]
        a_landed = [sem(f"a_landed{i}") for i in range(2)]
        w_high, w_low, pe_done, tile_out, a_used = map(sem, ("w_high_ready", "w_low_ready", "pe_done", "tile_out", "a_used"))
        cond_ready, mod_ready, init, m_sum, m_rows, m_done = map(
            sem, ("cond_ready", "mod_ready", "init", "m_sum", "m_rows", "m_done"))
        m_acc = [sem(f"m_acc_{engine}") for engine in ("gpsimd", "vector")]
        n_sq, n_early, n_ss, n_root, n_std, n_bc, n_xn, n_hi, n_lo = map(sem, ("n_sq", "n_early", "n_ss", "n_root", "n_std", "n_bc", "n_xn", "n_hi", "n_lo"))
        conv_mid, conv_done, silu_done, act_done, act_hi, act_lo = map(sem, ("conv_mid", "conv_done", "silu_done", "act_done", "act_hi", "act_lo"))
        dve_step, act_step = sem("dve_step"), sem("act_step")
        names = ("l2_sq l2_ss l2_root l2_std l2_bc l2_done g_rows g_in g_soft g_tr g_tok g_cs g_cum g_exp gb_r gb_d gb_e gb_at gb_q gb_k "
                 "gv_t gv_vb gv_k lv_ct lv_m lv_m1 lv_x lv_u lv_tu uw_ready u_out w_out s_init on_sq on_ss on_root on_std on_bc on_n on_y on_hi y_b "
                 "vt_t vt_out ln_mean ln_sq ln_std ln_r ln_n ln_g ln_v sp_s sp_y sp_hi y_a").split()
        G = {n: sem(n) for n in names}
        sc_w, sc_v, sc_s, sc_state = ([sem(f"{n}{d}") for d in range(2)] for n in ("scan_w", "scan_v", "scan_s", "scan_state"))
        names = ("rp_m rp_d at_s at_m at_p at_n at_t at_pt at_o at_hi at_y ol_out ol_o ix_l ix_r ix_a we_t we_ready ct_t ct_out "
                 "ql_m ql_out").split()
        A = {n: sem(n) for n in names}

        class Layer:
            def __init__(self, name, heads, key_tiles, per_group, a0, e0, masked, scale):
                self.name, self.heads, self.kt, self.per, self.a0, self.e0 = name, heads, key_tiles, per_group, a0, e0
                self.n, self.masked, self.scale = 2 * heads, masked, scale
                self.groups = self.n // per_group
                self.banks = BK[0:2] if masked else [BK[0], BK[1], PL[0]]
                self.lag = per_group + (5 if name == "dsa" else 3)
                self.steps = self.n - per_group + self.lag + 1

        MLA = Layer("mla", 8, 4, 2, 0, 0, False, 192 ** -0.5)
        DSA = Layer("dsa", 8, 2, 4, 16, 8, True, 96 ** -0.5)
        DIL = Layer("dil", 8, 2, 4, 32, 12, True, 64 ** -0.5)
        CRS = Layer("cross", 4, 2, 2, 48, 16, False, 256 ** -0.5)
        LAT = slice(SEQ, T2)
        CTX = slice(0, SEQ)
        ROPE1 = [(MQ[:, 8 + i, :], T0["uq"] + 8 + i, "m") for i in range(4)] + [(KR[:, LAT], T0["in1"] + 5, "m")]
        ROPE2 = [(PJ[:, i, :], T0["in2"] + i, "32" if i in (4, 5, 7) else "64") for i in (10, 11, 12, 13, 8, 4, 5, 7, *range(14, 22))]
        SIDE = 16
        ROTATE_AT = {j: [r for r in (2 * j, 2 * j + 1) if r < len(ROPE2)] for j in range(SIDE)}
        INDEX_AT, TOP_AT, LATENT_AT = range(4, 8), range(8, 16), range(10, 14)

        def chunk_place(st, k, d):
            c = k if d == 0 else 3 - k
            return c, (c // 2) * 2 + d, 64 * (c % 2)

        def q_decayed(st, q):
            tl, d = q // 2, q % 2
            at = st * SEQ + tl * P
            return QG0[:, tl, :, :] if d == 0 else QKV[:, 0:HEADS, at:at + P]

        def squares(name, k):
            width = NORMS[NORM_I[name]][2]
            if name == "n1_1":
                return SQN[:, k, :]
            if name == "mix":
                return TMP[:, k, CTX]
            return TMP[:, k, :] if width == T2 else TMP[:, k, LAT]

        def sq_count(name, k):
            if name in ("mix", "final1"):
                return NORM_C0["mix"] + 2 * k + (1 if name == "mix" else 2)
            return NORM_C0[name] + k + 1

        TURNS = [(3, 6), (12, 16)]
        LEVELS = [(lev, q) for lev in range(6) for q in range(4)]
        block = ctx.enter_context(nc.Block())

        @block.tensor
        def _(pe):
            mm = nc.tensor.matmul

            def mm3(out_, wh, wl, xh, xl, first, last):
                mm(out_, wh, xh, start=first, stop=False)
                mm(out_, wh, xl, start=False, stop=False)
                return mm(out_, wl, xh, start=False, stop=last)

            def weights(n, off=0):
                pe.wait_ge(w_low, n + 1 + off)

            def free_bank(t, off=0):
                pe.wait_ge(tile_out, t + 1 + off)

            def tile(n, t, x, width, off=0):
                weights(n, off)
                free_bank(t, off)
                for k in range(KC):
                    w = slice(k * P, (k + 1) * P)
                    last = mm3(PL[t % 2][:, 0:width], wh(n)[:, w], wl(n)[:, w], HH[:, k, x], HL[:, k, x], k == 0, k == KC - 1)
                last.then_inc(pe_done, 1)

            def first_tiles(name, x, width, ready, order=None):
                n, t = B0[name], T0[name]
                behind = 3 if lead(name) == 2 else 2
                order = order or [(j, k) for step in range(KC + behind) for j, k in ((0, step), (1, step - behind)) if 0 <= k < KC]
                for j, k in order:
                    if k == 0:
                        weights(n + j)
                        free_bank(t + j)
                    if j == 0:
                        pe.wait_ge(*ready(k))
                    w = slice(k * P, (k + 1) * P)
                    last = mm3(PL[(t + j) % 2][:, 0:width], wh(n + j)[:, w], wl(n + j)[:, w], HH[:, k, x], HL[:, k, x], k == 0, k == KC - 1)
                    if k == KC - 1:
                        last.then_inc(pe_done, 1)

            def h_ready(name):
                return lambda k: (n_lo, NORM_S0[name] + k + 1)

            def mod_pair(h, acc, b, at, off=0):
                for s in range(2):
                    pe.wait_ge(m_acc[s], 1 - s + PAIR_OPS[s] * (h + 1 + off))
                for j in range(2):
                    for s in range(2):
                        c = 2 * (2 * h + j - at) + s + 4 * off
                        last = mm(BK[b][:, ds(c, 1)], acc[:, h % 2, s, j * P:(j + 1) * P], ONES[:, 0:1], start=True, stop=True)
                last.then_inc(m_done, 1)

            def norm_sum(name, c=0, count=1):
                _, nch, width = NORMS[NORM_I[name]]
                chunks = [0, *range(EARLY, nch)] if name in SUMMED else range(nch)
                for k in chunks:
                    if name in SUMMED and k == 0:
                        pe.wait_ge(n_early, (EARLY - 1) * (SUMMED.index("final1" if name == "mix" else name) + 1))
                    else:
                        pe.wait_ge(n_sq, sq_count(name, k))
                    for t in range(width // P):
                        last = mm(SUMS[t][:, c:c + 1], squares(name, k)[:, t * P:(t + 1) * P], ONES[:, 0:1], start=(k == 0), stop=(k == nch - 1))
                if count:
                    last.then_inc(n_ss, count)

            def norm_spread(name):
                pe.wait_ge(n_std, NORM_I[name] + 1)
                for t in range(NORMS[NORM_I[name]][2] // P):
                    last = mm(BK[0][:, t * P:(t + 1) * P], STD[:, 8 + t:9 + t].to_broadcast([P, P]), ID[:], start=True, stop=True)
                last.then_inc(n_bc, 1)

            def norm(name):
                norm_sum(name)
                norm_spread(name)

            pe.wait_ge(init, 1)
            pe.wait_ge(cond_ready, 1)
            for g in range(4):
                pe.wait_ge(a_first[g], 16)
                for k in range(KC):
                    at = COL_AT["cond"] + 2 * k
                    last = mm(MROWS[g][0:2, :], C[:, at:at + 2], A16[:, 4 * g + k // 2, k % 2 * 512:(k % 2 + 1) * 512], start=(k == 0), stop=(k == KC - 1))
                last.then_inc(m_sum, 1)
                if g == 1:
                    norm_sum("n1_0")
            pe.wait_ge(cols_in, 32)
            for m in range(A_FIRST):
                pe.wait_ge(m_rows, m // 4 + 1)
                nc.tensor.transpose(BK[1][:, 2 * m:2 * m + 2], MR[0:2, m // 4, m % 4 * P:(m % 4 + 1) * P], ID[0:2, 0:2]).then_inc(a_used, 1)
            norm_spread("n1_0")

            first_tiles("in0", slice(0, T2), T2, h_ready("n1_0"))
            for s in (2, 3):
                tile(s, s, slice(0, T2), T2)
            mod_pair(0, ACC0, 5, 0)
            with pe.Fori(1, 5) as i:
                for s in range(4):
                    tile(s, s, slice(0, T2), T2, 4 * i)
                    if s % 2:
                        mod_pair((s - 3) // 2, ACC0, 5, 0, 2 * i)

            def lengths(j):
                pe.wait_ge(G["l2_sq"], j + 1)
                for t in range(4):
                    last = mm(BK[0][:, 8 * t + j:8 * t + j + 1], SQL[:, j % 4, t * P:(t + 1) * P], ONES[:, 0:1], start=True, stop=True)
                last.then_inc(G["l2_ss"], 1)

            def inverse_lengths(some):
                for j in some:
                    if j >= 4:
                        pe.wait_ge(G["l2_done"], j - 3)
                    for t in range(4):
                        last = mm(BK[1 + j % 4][:, t * P:(t + 1) * P], L2[:, 1, 8 * t + j:8 * t + j + 1].to_broadcast([P, P]), ID[:], start=True, stop=True)
                    last.then_inc(G["l2_bc"], 1)

            for t in range(20, 25):
                tile(t, t, slice(0, T2), T2)
                if t % 2:
                    mod_pair((t - 3) // 2, ACC0, 5, 0)
                if t in (20, 21):
                    for j in range(4 * (t - 20), 4 * (t - 20) + 4):
                        lengths(j)
                if t == 23:
                    pe.wait_ge(G["l2_std"], 1)
                    inverse_lengths(range(4))
                    pe.wait_ge(G["g_soft"], 1)
                    for x in range(4):
                        last = nc.tensor.transpose(BK[0][:, 40 * x:40 * x + 40], GT[0:40, x * P:(x + 1) * P], ID[0:40, 0:40])
                    last.then_inc(G["g_tr"], 1)
            mod_pair(PAIRS_IN - 1, ACC0, 5, 0)

            inverse_lengths(range(4, 8))
            pe.wait_ge(G["g_tok"], 1)
            pe.wait_ge(gdn_in, 16)
            pe.wait_ge(mod_ready, 2)
            for d in range(2):
                o = BK[5][:, 0:64].rearrange("p (t d r) -> p t d r", t=4, d=2)[:, :, d, :]
                g = GTOK[:, :, 4 * d:4 * d + 4]
                mm(o[:, :, 0:4], gtab("cum", d), g, start=True, stop=True)
                last = mm(o[:, :, 4:8], gtab("blk"), g, start=True, stop=True)
            last.then_inc(G["g_cs"], 1)
            pe.wait_ge(G["l2_done"], 8)
            pe.wait_ge(tile_out, 27)

            def values_keys(st, k):
                if k in TURNS[st]:
                    tl = TURNS[st].index(k)
                    tok = slice(st * SEQ + tl * P, st * SEQ + (tl + 1) * P)
                    if tl:
                        pe.wait_ge(G["gv_vb"], 2 * (2 * st + tl))
                        pe.wait_ge(G["gv_k"], 2 * (2 * st + tl))
                    elif st:
                        pe.wait_ge(G["on_n"], 2)
                    for h in range(HEADS):
                        nc.tensor.transpose(PL[0][:, h * P:(h + 1) * P], QKV[:, 8 + h, tok], ID[:])
                    for h in range(HEADS):
                        last = nc.tensor.transpose(PL[1][:, h * P:(h + 1) * P], QKV[:, 4 + h, tok], ID[:])
                    last.then_inc(G["gv_t"], 1)

            def spatial_gate(k):
                if k in (9, 11):
                    for t in (k - 9, k - 8):
                        if t >= 2:
                            pe.wait_ge(G["vt_out"], t - 1)
                        else:
                            pe.wait_ge(G["gv_vb"], 4)
                            pe.wait_ge(G["gv_k"], 4)
                        for g in range(4):
                            last = nc.tensor.transpose(PL[t % 2][:, g * P:(g + 1) * P], UV[:, 4 + g, t * P:(t + 1) * P], ID[:])
                        last.then_inc(G["vt_t"], 1)
                if k >= 24:
                    t = k - 24
                    pe.wait_ge(ws_in, 48)
                    pe.wait_ge(G["ln_v"], t + 1)
                    if t >= 2:
                        pe.wait_ge(G["sp_y"], t - 1)
                    for g in range(4):
                        o = PL[t % 2][:, g * P:(g + 1) * P]
                        mm(o, ONES[0:1, :], BS[0:1, g * P:(g + 1) * P], start=True, stop=False)
                        last = mm(o, UV[:, 4 + g, t * P:(t + 1) * P], WS[:, g, :], start=False, stop=True)
                    last.then_inc(G["sp_s"], 1)

            def out_sums(st):
                pe.wait_ge(G["on_sq"], st + 1)
                for h in range(HEADS):
                    for t in range(2):
                        last = mm(OUT_BANKS[st][0][:, 2 * h + t:2 * h + t + 1], ONQ[:, h, t * P:(t + 1) * P], ONES[:, 0:1], start=True, stop=True)
                last.then_inc(G["on_ss"], 1)

            def out_spread(st):
                pe.wait_ge(G["on_std"], st + 1)
                for h in range(HEADS):
                    for t in range(2):
                        last = mm(OUT_BANKS[st][h // 2][:, h % 2 * SEQ + t * P:h % 2 * SEQ + (t + 1) * P], SM[:, 64 + 2 * h + t:65 + 2 * h + t].to_broadcast([P, P]), ID[:], start=True, stop=True)
                last.then_inc(G["on_bc"], 1)

            def first_outputs(k):
                if k == 6:
                    out_sums(0)
                if k == 9:
                    out_spread(0)

            for st in range(2):
                if st:
                    for d in range(2):
                        pe.wait_ge(sc_state[d], 4)
                    pe.wait_ge(G["sp_y"], 4)
                for q in range(4):
                    tl, d, z = q // 2, q % 2, 4 * st + q
                    tt = 2 * st + tl
                    if q >= 2:
                        pe.wait_ge(G["gb_at"], z - 1)
                    elif z == 0:
                        pe.wait_ge(G["g_cum"], 1)
                    sums, betas = ROWS[q % 2]
                    for h in range(HEADS):
                        mm(sums[:, h * P:(h + 1) * P], GTOK[:, tt, 4 * d + h:4 * d + h + 1].to_broadcast([P, P]), gtab("cum", d), start=True, stop=True)
                        last = mm(betas[:, h * P:(h + 1) * P], GTOK[:, tt, 32 + 4 * d + h:33 + 4 * d + h].to_broadcast([P, P]), ID[:], start=True, stop=True)
                    last.then_inc(G["gb_r"], 1)
                    if q < 2:
                        tok = slice(st * SEQ + q * P, st * SEQ + (q + 1) * P)
                        for h in range(HEADS):
                            mm(bank(2 + 2 * q, 4, P)[:, h, :], QKV[:, 4 + h, tok], QKV[:, 4 + h, tok], start=True, stop=True)
                            last = mm(bank(3 + 2 * q, 4, P)[:, h, :], QKV[:, 4 + h, tok], QKV[:, h, tok], start=True, stop=True)
                        last.then_inc(G["gb_k"], 1)
                pe.wait_ge(G["gb_at"], 4 * st + 3)

                def first_product(k):
                    lev, q = LEVELS[k]
                    b, at = k % 2, 24 * st
                    pe.wait_ge(G["lv_ct"], at + k + 1)
                    if lev == 0:
                        if k >= 2:
                            pe.wait_ge(G["lv_tu"], at + k - 1)
                        for h in range(HEADS):
                            last = nc.tensor.transpose(bank(b, 4, P)[:, h, :], CT[:, b, h, :], ID[:])
                    else:
                        pe.wait_ge(G["lv_tu"], at + (k - 1 if k < 6 else k - 3))
                        for h in range(HEADS):
                            last = mm(bank(b, 4, P)[:, h, :], CT[:, b, h, :], TT[:, q, h, :], start=True, stop=True)
                    last.then_inc(G["lv_m"], 1)

                def second_product(k):
                    lev, q = LEVELS[k]
                    b, at = k % 2, 24 * st
                    pe.wait_ge(G["lv_m1"], 20 * st + k - 3)
                    if k >= 6:
                        pe.wait_ge(G["lv_tu"], at + k - 1)
                    if lev < 5:
                        for h in range(HEADS):
                            mm(bank(2 + 2 * b, 4, P)[:, h, :], TU[:, q, h, :], M1[:, b, h, :], start=True, stop=True)
                    for h in range(HEADS):
                        last = mm(bank(3 + 2 * b, 4, P)[:, h, :], M1[:, b, h, :], TU[:, q, h, :], start=True, stop=True)
                    last.then_inc(G["lv_x"], 1)

                for k in range(25):
                    if k < 24:
                        first_product(k)
                    if k >= 5:
                        second_product(k - 1)
                    if k < 24:
                        values_keys(st, k)
                        (first_outputs if st else spatial_gate)(k)
                pe.wait_ge(G["lv_tu"], 24 * st + 24)
                for q in range(4):
                    b = q % 2
                    if q >= 2:
                        pe.wait_ge(G["u_out"], 4 * st + q - 1)
                        pe.wait_ge(G["w_out"], 4 * st + q - 1)
                    for h in range(HEADS):
                        mm(bank(2 + 2 * b, 4, P)[:, h, :], TU[:, q, h, :], VB[:, q, h, :], start=True, stop=True)
                        last = mm(bank(3 + 2 * b, 4, P)[:, h, :], KBG[:, q, h, :], TU[:, q, h, :], start=True, stop=True)
                    last.then_inc(G["uw_ready"], 1)
                pe.wait_ge(G["u_out"], 4 * st + 4)
                pe.wait_ge(G["w_out"], 4 * st + 4)
                pe.wait_ge(G["s_init"], 1)
                pe.wait_ge(G["gb_q"], 4 * st + 4)
                for k in range(4):
                    n = 4 * st + k
                    for d in range(2):
                        _, q, _ = chunk_place(st, k, d)
                        if n:
                            pe.wait_ge(sc_state[d], n)
                        for h in range(HEADS):
                            last = mm(bank(d, 4, P)[:, h, :], WT[:, q, h, :], S[:, d, h, :], start=True, stop=True)
                        last.then_inc(sc_w[d], 1)
                    for d in range(2):
                        _, q, po = chunk_place(st, k, d)
                        half = slice(po, po + 64)
                        pe.wait_ge(sc_v[d], n + 1)
                        o = BK[4 + d][:, 0:256].rearrange("p (h t) -> p h t", h=HEADS)
                        for h in range(HEADS):
                            mm(o[:, h, :], S[:, d, h, :], q_decayed(st, q)[:, h, half], start=True, stop=False)
                            last = mm(o[:, h, :], VN[half, d, h, :], ATT[half, q, h, half], start=False, stop=True)
                        if n < 7:
                            for h in range(HEADS):
                                last = mm(bank(2 + d, 4, P)[:, h, :], KD[half, q, h, :], VN[half, d, h, :], start=True, stop=True)
                        last.then_inc(sc_s[d], 1)
                    if st == 0:
                        spatial_gate(24 + k)
            for d in range(2):
                pe.wait_ge(sc_state[d], 8)
            out_sums(1)
            out_spread(1)

            first_tiles("out0", slice(0, T2), T2, lambda k: (G["y_a"], 4) if k < 4 else (G["y_b"], 2),
                        [(j, k) for ks in (range(4), range(4, KC)) for j in range(2) for k in ks])
            for s in (2, 3):
                tile(B0["out0"] + s, T0["out0"] + s, slice(0, T2), T2)
            with pe.Fori(1, 2) as i:
                for s in range(4):
                    tile(B0["out0"] + s, T0["out0"] + s, slice(0, T2), T2, 4 * i)
            norm_sum("n2_0")

            def up(layer, x, width):
                name = f"up{layer}"
                first_tiles(name, x, width, h_ready(f"n2_{layer}"))
                for s in (2, 3):
                    tile(B0[name] + s, T0[name] + s, x, width)
                if layer == 0:
                    mod_pair(PAIRS_IN, ACC1, 5, 2 * PAIRS_IN)
                with pe.Fori(1, FC // 2) as i:
                    for s in range(4):
                        tile(B0[name] + s, T0[name] + s, x, width, 4 * i)
                        if layer == 0 and s % 2:
                            mod_pair(PAIRS_IN + s // 2 - 1, ACC1, 5, 2 * PAIRS_IN, 2 * i)

            def down(layer, ah, al, width):
                name = f"dn{layer}"

                def one(m, i, per, first):
                    t = T0[name] + m
                    free_bank(t, per * i)
                    for k in range(FC):
                        n, w = B0[name] + 3 * m + k // 8, slice(k % 8 * P, (k % 8 + 1) * P)
                        if k % 8 == 0:
                            weights(n, 3 * per * i)
                        if first:
                            pe.wait_ge(act_lo, FC * layer + k + 1)
                        last = mm3(PL[t % 2][:, 0:width], wh(n)[:, w], wl(n)[:, w], ah[:, k, :], al[:, k, :], k == 0, k == FC - 1)
                        if k % 8 == 7 or k == FC - 1:
                            last.then_inc(pe_done, 1)
                    if layer == 0 and PAIRS_IN + PAIRS_UP + m < PAIRS:
                        mod_pair(PAIRS_IN + PAIRS_UP + m, ACC1, 1, 2 * (PAIRS_IN + PAIRS_UP), per * i)

                if layer == 0:
                    with pe.Fori(0, 3) as i:
                        for m in range(2):
                            one(m, i, 2, m == 0)
                    for m in (6, 7):
                        one(m, 0, 2, False)
                    norm_sum("n1_1")
                else:
                    with pe.Fori(0, 2) as i:
                        for m in range(4):
                            one(m, i, 4, m == 0)

            def project(name, x, width, ready=None, loops=2):
                if ready:
                    first_tiles(name, x, width, ready)
                    for s in (2, 3):
                        tile(B0[name] + s, T0[name] + s, x, width)
                with pe.Fori(1 if ready else 0, loops) as i:
                    for s in range(4):
                        tile(B0[name] + s, T0[name] + s, x, width, 4 * i)

            norm_spread("n2_0")
            up(0, slice(0, T2), T2)
            down(0, AH0, AL0, T2)

            norm_spread("n1_1")
            first_tiles("in1", LAT, SEQ, h_ready("n1_1"))
            for m in range(2, 6):
                x = LAT if m < 3 else slice(0, T2)
                tile(B0["in1"] + m, T0["in1"] + m, x, SEQ if m < 3 else T2)
                if m == 3:
                    norm_sum("cq")
                if m == 4:
                    norm_spread("cq")
            norm_sum("ckv")

            def chunks(name, per, xh, xl, ready, beside=None):
                done = -1
                for m in range(dict((s, n) for s, _, n in STAGES)[name]):
                    t = T0[name] + m
                    free_bank(t)
                    for k in range(per):
                        n, w = B0[name] + (m * per + k) // 8, slice((m * per + k) % 8 * P, ((m * per + k) % 8 + 1) * P)
                        if n != done:
                            weights(n)
                            done = n
                        if m == 0:
                            pe.wait_ge(n_lo, NORM_S0[ready] + k + 1)
                        last = mm3(PL[t % 2][:, 0:xh.shape[2]], wh(n)[:, w], wl(n)[:, w], xh[:, k, :], xl[:, k, :], k == 0, k == per - 1)
                    last.then_inc(pe_done, 1)
                    if beside:
                        beside(m)

            def moving(name, xh, xl, x0, some, toks, per_tile):
                for b in some:
                    n = B0[name] + b
                    weights(n)
                    first, final = b % per_tile == 0, b % per_tile == per_tile - 1
                    for tok in range(toks):
                        t = T0[name] + (b // per_tile) * toks + tok
                        if first:
                            free_bank(t)
                        for kk in range(2):
                            k = 2 * (b % per_tile) + kk
                            x = slice(x0 + tok * P, x0 + (tok + 1) * P)
                            w = slice(kk * 512, (kk + 1) * 512)
                            o = PL[t % 2][:]
                            mm(o, xh[:, k, x], wh(n)[:, w], start=(first and kk == 0), stop=False)
                            mm(o, xh[:, k, x], wl(n)[:, w], start=False, stop=False)
                            last = mm(o, xl[:, k, x], wh(n)[:, w], start=False, stop=(final and kk == 1))
                        last.then_inc(pe_done, 1)

            chunks("uq", 3, CQH, CQL, "cq", lambda m: norm_spread("ckv") if m == 2 else None)
            norm("mem")
            chunks("ukv_k", 2, CKH, CKL, "ckv")

            def rotate(tiles, r0, some):
                for i in some:
                    x, t, which = tiles[i]
                    pe.wait_ge(tile_out, t + 3)
                    if i >= 2:
                        pe.wait_ge(A["rp_d"], r0 + i - 1)
                    mm(BK[2 + i % 2][:, 0:SEQ], ltab("perm32" if which == "32" else "perm64", 0, P), x, start=True, stop=True).then_inc(A["rp_m"], 1)

            pe.wait_ge(late_in, 16)
            for b in range(2):
                rotate(ROPE1, 0, (2 * b, 2 * b + 1))
                moving("ukv_v", CKH, CKL, 0, (b,), 4, 1)
            rotate(ROPE1, 0, (4,))

            pe.wait_ge(A["rp_d"], len(ROPE1))
            pe.wait_ge(tile_out, T0["out1"] + 2)

            def attend(ly, scores, values, extra=None):
                nb = len(ly.banks)
                for a in range(ly.n + 3):
                    if a < ly.n:
                        if ly.a0 or a >= nb:
                            pe.wait_ge(A["at_m" if ly.masked else "at_p"], ly.a0 + max(0, a - nb + 1))
                        scores(a // 2, a % 2, ly.banks[a % nb]).then_inc(A["at_s"], 1)
                    if 2 <= a < ly.n + 2:
                        p = a - 2
                        pe.wait_ge(A["at_n"], ly.a0 + p + 1)
                        for k in range(ly.kt):
                            last = nc.tensor.transpose(BK[2 + p % 2][:, k * P:(k + 1) * P], PB[:, p % 3, k * P:(k + 1) * P], ID[:])
                        last.then_inc(A["at_t"], 1)
                    if a >= 3:
                        p = a - 3
                        pe.wait_ge(A["at_pt"], ly.a0 + p + 1)
                        e = p // ly.per
                        if ly is not DSA and p % ly.per == 0 and ly.e0 + e >= 2:
                            pe.wait_ge(A["at_y"], ly.e0 + e - 1)
                        values(p // 2, p % 2, PT[:, p % 2, :, :]).then_inc(A["at_o"], 1)
                        if extra:
                            extra(p)

            def mla_scores(h, qt, o):
                q, po = slice(qt * P, (qt + 1) * P), 64 * (h % 2)
                mm(o[:], MQ[:, h, q], KN[:, h, :], start=True, stop=False)
                return mm(o[:], MQ[po:po + 64, 8 + h // 2, q], KR[po:po + 64, :], start=False, stop=True)

            def mla_values(h, qt, pt):
                for k in range(4):
                    last = mm(BK[4 + h % 2][:, qt * P:(qt + 1) * P], VT[:, k, h * P:(h + 1) * P], pt[:, k, :], start=(k == 0), stop=(k == 3))
                return last

            attend(MLA, mla_scores, mla_values)
            project("out1", LAT, SEQ, lambda k: (A["at_y"], k + 1))
            norm("n2_1")
            up(1, LAT, SEQ)
            down(1, AH1, AL1, SEQ)

            norm_sum("mix", 1, 0)
            norm_sum("final1", 0, 2)
            pe.wait_ge(n_std, NORM_I["mix"] + 2)
            for c, x in ((10, CTX), (8, LAT)):
                for t in range(2):
                    o = BK[0][:, x.start + t * P:x.start + (t + 1) * P]
                    last = mm(o, STD[:, c + t:c + t + 1].to_broadcast([P, P]), ID[:], start=True, stop=True)
            last.then_inc(n_bc, 2)

            project("in2", LAT, SEQ, h_ready("mix"), 5)
            for m in (20, 21):
                tile(B0["in2"] + m, T0["in2"] + m, LAT, SEQ)
            moving("in2_v", HH, HL, SEQ, range(4), 2, 4)
            norm("kv2")
            for j in range(SIDE):
                if j < 8:
                    if j == 0:
                        pe.wait_ge(n_lo, NORM_S0["mem"] + KC)
                    tile(B0["xk"] + j, T0["xk"] + j, CTX, SEQ)
                else:
                    moving("xv", HH, HL, 0, (j - 8,), 2, 4)
                rotate(ROPE2, len(ROPE1), ROTATE_AT[j])
                if j == 2:
                    for qt in range(2):
                        last = nc.tensor.transpose(BK[4][:, 8 * qt:8 * qt + 8], PJ[0:8, 9, qt * P:(qt + 1) * P], ID[0:8, 0:8])
                    last.then_inc(A["we_t"], 1)
                    pe.wait_ge(n_xn, NORM_C0["kv2"] + 1)
                    for qt in range(2):
                        last = nc.tensor.transpose(BK[5][:, qt * P:(qt + 1) * P], PJ[:, 6, qt * P:(qt + 1) * P], ID[:])
                    last.then_inc(A["ct_t"], 1)
                if j in INDEX_AT:
                    pe.wait_ge(A["rp_d"], len(ROPE1) + 5)
                    for c in range(4 * (j - INDEX_AT[0]), 4 * (j - INDEX_AT[0]) + 4):
                        qt, h = c // 8, c % 8
                        po = 64 * (h % 2)
                        if c >= 2:
                            pe.wait_ge(A["ix_r"], c - 1)
                        mm(BK[c % 2][:, 0:SEQ], PJ[po:po + 64, 10 + h // 2, qt * P:(qt + 1) * P], PJ[po:po + 64, 8, :], start=True, stop=True).then_inc(A["ix_l"], 1)
                if j in LATENT_AT:
                    pe.wait_ge(uk_in, 32)
                    pe.wait_ge(A["rp_d"], len(ROPE1) + len(ROPE2))
                    for h in (2 * (j - LATENT_AT[0]), 2 * (j - LATENT_AT[0]) + 1):
                        po = 64 * (h % 2)
                        if h >= 2:
                            pe.wait_ge(A["ql_out"], h - 1)
                        mm(BK[2 + h % 2][:, 0:SEQ], WUK[po:po + 64, h // 2, :], PJ[po:po + 64, h // 2, :], start=True, stop=True).then_inc(A["ql_m"], 1)
            pe.wait_ge(A["rp_d"], len(ROPE1) + len(ROPE2))
            pe.wait_ge(tile_out, T0["out2"] + 2)
            pe.wait_ge(A["ix_r"], 16)
            pe.wait_ge(A["ql_out"], 8)
            pe.wait_ge(A["ct_out"], 1)
            pe.wait_ge(A["we_ready"], 1)

            def dsa_scores(h, qt, o):
                q, po = slice(qt * P, (qt + 1) * P), 32 * (h % 4)
                mm(o[:, 0:SEQ], QL[:, h, q], PJ[:, 6, :], start=True, stop=False)
                return mm(o[:, 0:SEQ], PJ[po:po + 32, 4 + h // 4, q], PJ[po:po + 32, 7, :], start=False, stop=True)

            def dsa_values(h, qt, pt):
                if qt == 0 and h >= 2:
                    pe.wait_ge(A["ol_out"], h - 1)
                for k in range(2):
                    last = mm(BK[4 + h % 2][:, qt * P:(qt + 1) * P], CTK[:, k, :], pt[:, k, :], start=(k == 0), stop=(k == 1))
                return last

            def dsa_out(h):
                pair, po = h // 2, 64 * (h % 2)
                pe.wait_ge(A["ol_out"], h + 1)
                if h % 2 == 0 and pair >= 2:
                    pe.wait_ge(A["at_y"], DSA.e0 + pair - 1)
                mm(PL[pair % 2][po:po + 64, 0:SEQ], WUV[:, h, :], OL[:, h % 2, :], start=True, stop=True).then_inc(A["ol_o"], 1)

            attend(DSA, dsa_scores, dsa_values, lambda p: dsa_out((p - 3) // 2) if p % 2 and p >= 3 else None)
            dsa_out(7)

            def dil_scores(h, qt, o):
                q, po = slice(qt * P, (qt + 1) * P), 64 * (h % 2)
                return mm(o[:, 0:SEQ], PJ[po:po + 64, 14 + h // 2, q], PJ[po:po + 64, 18 + h // 2, :], start=True, stop=True)

            def dil_values(h, qt, pt):
                po = 64 * (h % 2)
                for k in range(2):
                    last = mm(BK[4 + h // 2 % 2][po:po + 64, qt * P:(qt + 1) * P], VBK[:, k, h * 64:(h + 1) * 64], pt[:, k, :], start=(k == 0), stop=(k == 1))
                return last

            attend(DIL, dil_scores, dil_values)
            project("out2", LAT, SEQ, lambda k: (A["at_y"], 8 + k + 1))

            norm("cross")
            project("xq", LAT, SEQ, h_ready("cross"))
            pe.wait_ge(tile_out, T0["xo"] + 2)

            def cross_scores(h, qt, o):
                q = slice(qt * P, (qt + 1) * P)
                mm(o[:, 0:SEQ], QC[:, 2 * h, q], KCR[:, 2 * h, :], start=True, stop=False)
                return mm(o[:, 0:SEQ], QC[:, 2 * h + 1, q], KCR[:, 2 * h + 1, :], start=False, stop=True)

            def cross_values(h, qt, pt):
                o = BK[4 + h % 2][:, 0:512].rearrange("p (c q) -> p c q", c=2)
                for c in range(2):
                    for k in range(2):
                        last = mm(o[:, c, qt * P:(qt + 1) * P], VC[:, k, h * 256 + c * P:h * 256 + (c + 1) * P], pt[:, k, :], start=(k == 0), stop=(k == 1))
                return last

            attend(CRS, cross_scores, cross_values)
            project("xo", LAT, SEQ, lambda k: (A["at_y"], 16 + k // 2 + 1))

            norm("mlp")
            project("up2", LAT, SEQ, h_ready("mlp"), 8)

            def down2(i):
                for m in range(2):
                    t = T0["dn2"] + m
                    free_bank(t, 2 * i)
                    for k in range(32):
                        n, w = B0["dn2"] + 4 * m + k // 8, slice(k % 8 * P, (k % 8 + 1) * P)
                        if k % 8 == 0:
                            weights(n, 8 * i)
                        if m == 0:
                            pe.wait_ge(act_lo, 2 * FC + k + 1)
                        last = mm3(PL[t % 2][:, 0:SEQ], wh(n)[:, w], wl(n)[:, w], AH2[:, k, :], AL2[:, k, :], k == 0, k == 31)
                        if k % 8 == 7:
                            last.then_inc(pe_done, 1)

            with pe.Fori(0, 4) as i:
                down2(i)
            norm("final2")

        @block.sync
        def _(sp):
            def load_w(n, off=0):
                sp.dma_start(RAW[:, n % 4, :], w_stream[n + off]).then_inc(w_landed[n % 4], 16)

            def next_w(s, off=0):
                sp.wait_ge(w_low, s + 1 + off)
                load_w(s + 4, off)

            def load_a(j, off=0):
                if j >= 2:
                    sp.wait_ge(m_acc[1], PAIR_OPS[1] // 2 * (j - 1) + PAIR_OPS[1] * off)
                sp.dma_start(AR[:, j % 2, :], a_stream[j + 2 * off]).then_inc(a_landed[j % 2], 16)

            for g in range(4):
                m = slice(4 * g, 4 * g + 4)
                sp.dma_start(A16[:, m, :], a_head[m].rearrange("m p n -> p m n")).then_inc(a_first[g], 16)
                if g == 0:
                    sp.dma_start(X[:], x_in).then_inc(x_ready, 16)
            for n in range(4):
                load_w(n)
            load_a(0)
            load_a(1)
            with sp.Fori(0, 5) as i:
                for s in range(4):
                    next_w(s, 4 * i)
                    load_a(s + 2, 2 * i)
            for s in range(20, 25):
                next_w(s)
                if s < 22:
                    load_a(s + 2)
            up_at = 2 * PAIRS_IN
            load_a(up_at)
            load_a(up_at + 1)
            with sp.Fori(0, 3) as i:
                for s in range(4):
                    next_w(B0["out0"] + s, 4 * i)
            load_a(up_at + 2)
            load_a(up_at + 3)
            with sp.Fori(0, FC // 2 - 1) as i:
                for s in range(4):
                    next_w(B0["up0"] + 4 + s, 4 * i)
                    load_a(up_at + 4 + s, 2 * i)
            dn_at = up_at + 2 * FC
            for b in range(B0["in1"] - B0["dn0"]):
                next_w(B0["dn0"] + b)
                if b % 3 == 1:
                    for j in range(dn_at + b // 3 * 2, dn_at + b // 3 * 2 + 2):
                        if j < 2 * PAIRS:
                            load_a(j)
            left = NBLK - 4 - B0["in1"]
            with sp.Fori(0, left // 4) as i:
                for s in range(4):
                    next_w(B0["in1"] + s, 4 * i)
            for s in range(left // 4 * 4, left):
                next_w(B0["in1"] + s)
            for k in range(0, KC, 4):
                sp.wait_ge(n_xn, NORM_C0["final2"] + k + 4)
                sp.dma_start(out[:, k:k + 4, :], X[:, k:k + 4, LAT]).then_inc(out_done, 16)
            sp.wait_ge(out_done, 32)

        @block.gpsimd
        def _(pool):
            nc.gpsimd.memset(ONES[:], 1.0).then_inc(init, 1)
            for k in range(2):
                nc.gpsimd.memset(XP[:, k, :, 0:1], 0.0).then_inc(m_done, 1)
                nc.gpsimd.memset(XP[:, k, :, SEQ + 1:SEQ + 2], 0.0).then_inc(conv_done, 1)
            nc.gpsimd.memset(S[:], 0.0).then_inc(G["s_init"], 1)
            nc.gpsimd.memset(PROD0[:, 0, 0:1], 0.0).then_inc(m_acc[0], 1)
            def sum_early(*names):
                for k in range(1, EARLY):
                    for j, name in enumerate(names):
                        before = (EARLY - 1) * SUMMED.index(names[0])
                        pool.wait_ge(n_sq, sq_count(name, k))
                        if k > 1:
                            pool.wait_ge(n_early, before + len(names) * (k - 2) + j + 1)
                        nc.gpsimd.tensor_tensor(squares(name, 0), squares(name, 0), squares(name, k), ALU.add).then_inc(n_early, 1)

            sum_early("n1_0")
            pool.wait_ge(mod_ready, 1)
            pool.dma_start(GTAB[:], gdn_tables).then_inc(gdn_in, 16)

            def mod_pair(h, acc, prod, off):
                n = 1 + PAIR_OPS[0] * h

                def summed(*operands):
                    nonlocal n
                    pool.wait_ge(m_acc[0], n + PAIR_OPS[0] * off)
                    nc.gpsimd.tensor_tensor(*operands, ALU.add).then_inc(m_acc[0], 1)
                    n += 1

                pool.wait_ge(m_done, h + 1 + off)
                o = acc[:, h % 2, 0, :]
                for half in range(2):
                    pool.wait_ge(a_landed[half], 16 * (h + 1) + 16 * off)
                    w = AR[:, half, :].rearrange("p (k n) -> p k n", k=4)
                    at = COL_AT["cond"] + KC * half
                    vector = C[:, at:at + KC].rearrange("p (k s) -> p k s", s=2)[:, :, 0]
                    pool.wait_ge(m_acc[0], n + PAIR_OPS[0] * off)
                    nc.gpsimd.tensor_tensor(prod[:], w, vector.unsqueeze(2).to_broadcast([P, 4, 256]), ALU.mult).then_inc(m_acc[0], 1)
                    n += 1
                    summed(prod[:, 0:2, :], prod[:, 0:2, :], prod[:, 2:4, :])
                    if half == 0:
                        summed(o, prod[:, 0, :], prod[:, 1, :])
                    else:
                        summed(prod[:, 0, :], prod[:, 0, :], prod[:, 1, :])
                        summed(o, o, prod[:, 0, :])

            pool.wait_ge(cond_ready, 1)
            with pool.Fori(0, PAIRS_IN // 2) as i:
                for h in range(2):
                    mod_pair(h, ACC0, PROD0, 2 * i)
            pool.wait_ge(gdn_in, 16)
            for st in range(2):
                def decayed(q):
                    tl, z = q // 2, 4 * st + q
                    tok = slice(st * SEQ + tl * P, st * SEQ + (tl + 1) * P)
                    pool.wait_ge(G["gb_e"], 2 * z + 1)
                    if q % 2:
                        pool.wait_ge(G["gb_q"], z)
                        pool.wait_ge(G["gb_k"], 2 * st + tl + 1)
                    nc.gpsimd.tensor_tensor(q_decayed(st, q), QKV[:, 0:HEADS, tok], ER[:, z % 2, :, :], ALU.mult).then_inc(G["gb_q"], 1)

                decayed(0)
                decayed(1)
                for k, (lev, q) in enumerate(LEVELS):
                    n, b = 24 * st + k, k % 2
                    if lev == 0:
                        pool.wait_ge(G["gb_at"], 4 * st + q + 1)
                    if n >= 2:
                        pool.wait_ge(G["lv_m"], n - 1)
                    if 2 <= k < 6:
                        pool.wait_ge(G["lv_u"], 4 * st + k - 1)
                    mask = gtab("lev", 6 * (q % 2) + lev).unsqueeze(1).to_broadcast([P, HEADS, P])
                    nc.gpsimd.tensor_tensor(CT[:, b, :, :], AT[:, q, :, :], mask, ALU.mult).then_inc(G["lv_ct"], 1)
                    if k in (4, 6):
                        decayed(k // 2)
                    if st == 0 and k == 8:
                        pool.wait_ge(G["gb_q"], 4)
                        pool.dma_start(LNR[:], ln_rows.rearrange("p (a b c) -> p a b c", a=2, b=4)).then_inc(ws_in, 16)
                    if st == 0 and k == 9:
                        pool.dma_start(WS[:], ws_t).then_inc(ws_in, 16)
                    if st == 0 and k == 10:
                        pool.dma_start(BS[:], bs_row).then_inc(ws_in, 16)
                if st == 0:
                    pool.wait_ge(ws_in, 48)
                    for t in range(4):
                        x = UV[:, 4:8, t * P:(t + 1) * P]
                        pool.wait_ge(G["ln_g"], t + 1)
                        nc.gpsimd.tensor_tensor(x, x, LNR[:, 1, :, :], ALU.add).then_inc(G["ln_v"], 1)
            sum_early("n2_0")
            pool.wait_ge(n_lo, NORM_S0["n2_0"] + KC)
            with pool.Fori(0, (PAIRS - PAIRS_IN) // 2) as i:
                for h in range(2):
                    mod_pair(PAIRS_IN + h, ACC1, PROD1, 2 * i)
            sum_early("n1_1")
            pool.wait_ge(tile_out, T0["dn0"] + KC + 2)
            pool.dma_start(LTAB[:], late_tables).then_inc(late_in, 16)
            pool.wait_ge(n_xn, NORM_C0["n1_1"] + 8)
            pool.dma_start(X[:, :, CTX], mem_in).then_inc(mem_ready, 16)
            sum_early("n2_1")
            sum_early("mix", "final1")
            pool.wait_ge(tile_out, T0["dn1"] + KC + 2)
            pool.dma_start(WUK[:], w_uk).then_inc(uk_in, 16)
            pool.dma_start(WUV[:], w_uv).then_inc(uk_in, 16)
            for name in ("cross", "mlp", "final2"):
                sum_early(name)

        UVF = UV[:].rearrange("p a b -> p (a b)")
        PJF = PJ[:].rearrange("p a b -> p (a b)")
        QCF = QC[:].rearrange("p a b -> p (a b)")
        QKVF = QKV[:].rearrange("p a b -> p (a b)")
        XF = X[:].rearrange("p a b -> p (a b)")
        MODF = MOD[:].rearrange("p a b c d -> p (a b c d)")
        NORM_OUT = {"cq": (CQH, CQL), "ckv": (CKH, CKL)}

        def norm_src(name, k):
            if name == "cq":
                return CQ[:, k, :]
            if name == "ckv":
                return CKV[:, k, :]
            if name == "kv2":
                return PJ[:, 6, :]
            if name == "mem":
                return X[:, k, CTX]
            return X[:, k, :] if NORMS[NORM_I[name]][2] == T2 else X[:, k, LAT]

        def norm_dst(name, k, low):
            if name in NORM_OUT:
                return NORM_OUT[name][low][:, k, :]
            x = CTX if name == "mem" else LAT if NORMS[NORM_I[name]][2] == SEQ else slice(0, T2)
            return (HL if low else HH)[:, k, x]

        def streams(name):
            return [(CTX, 0), (LAT, 1)] if NORMS[NORM_I[name]][2] == T2 else [(CTX, 1)]

        @block.scalar
        def _(act):
            f = nc.scalar.activation
            steps = [0]

            def link(ins):
                steps[0] += 1
                ins.then_inc(act_step, 1)
                act.wait_ge(act_step, steps[0])

            def split(n, off=0):
                if n >= NBLK:
                    return
                act.wait_ge(w_landed[n % 4], 16 * (n // 4 + 1) + 4 * off)
                if n >= 2:
                    act.wait_ge(pe_done, DONE_BLOCK[slot_before(n)] + off)
                f(wh(n), RAW[:, n % 4, :], ACT.Copy).then_inc(w_high, 1)

            def done(t, off=0):
                act.wait_ge(pe_done, DONE_TILE[t] + off)

            def norm_start(name):
                i = NORM_I[name]
                f(SM[:, 32 + i:33 + i], col("one"), ACT.Sqrt)
                if NORM_S0[name]:
                    act.wait_ge(n_lo, NORM_S0[name])
                if i:
                    act.wait_ge(n_xn, NORM_C0[name])

            def square(name, k, ready):
                act.wait_ge(*ready)
                f(squares(name, k), norm_src(name, k), ACT.Square).then_inc(n_sq, 1)

            def norm_root(name):
                i = NORM_I[name]
                width = NORMS[i][2]
                features = {"cq": 384, "ckv": 256, "kv2": 128}.get(name, D)
                act.wait_ge(n_ss, i + 1)
                for t in range(width // P):
                    last = f(STD[:, t:t + 1], SUMS[t][:, 0:1], ACT.Sqrt, scale=1.0 / features, bias=col("eps"))
                last.then_inc(n_root, 1)

            def norm_high(name, some=None):
                _, nch, width = NORMS[NORM_I[name]]
                if name not in SPLIT:
                    return
                for k in some or range(nch):
                    act.wait_ge(n_xn, NORM_C0[name] + k + 1)
                    if name in MODULATED:
                        layer, part = MODULATED[name]
                        act.wait_ge(mod_ready, {"n1_0": 1, "n2_0": 2}.get(name, 3))
                        for x, s in streams(name):
                            last = f(norm_dst(name, k, 0)[:, x], TMP[:, k, x], ACT.Identity, bias=MOD[:, layer, part, k, s:s + 1])
                        last.then_inc(n_hi, 1)
                    else:
                        f(norm_dst(name, k, 0), TMP[:, k, 0:width], ACT.Copy).then_inc(n_hi, 1)

            def norm_end(name):
                norm_root(name)
                norm_high(name)

            def norm(name, ready):
                norm_start(name)
                for k in range(NORMS[NORM_I[name]][1]):
                    square(name, k, ready(k))
                norm_end(name)

            def chunk_squares(name, k, ready):
                if name == "final1":
                    act.wait_ge(*ready)
                    f(squares("mix", k), norm_src("mix", k), ACT.Square, scale=col("final1", k)).then_inc(n_sq, 1)
                square(name, k, ready)

            def residuals(name, per, then):
                norm_start("mix" if then == "final1" else then)
                for m in range(KC):
                    if m:
                        chunk_squares(then, m - 1, (tile_out, T0[name] + m + 2))
                    for k in range(per):
                        split(B0[name] + per * m + k + lead(name))
                chunk_squares(then, KC - 1, (tile_out, T0[name] + KC + 2))
                if then != "final1":
                    norm_end(then)

            def conv_in(t, k, cv, taps, width, it=0, per=0):
                act.wait_ge(pe_done, DONE_TILE[t] + per * it)
                act.wait_ge(conv_done, cv + k + 1 + per * it)
                n = width // SEQ
                f(XP[:, k % 2, 0:n, 1:SEQ + 1], PL[t % 2][:, 0:width].rearrange("p (s t) -> p s t", s=n), ACT.Copy)
                f(C1[:, k % 2, 0:width], PL[t % 2][:, 0:width], ACT.Identity, scale=C[:, ds(taps + 3 * k + 1 + 3 * per * it, 1)]).then_inc(tile_out, 1)

            act.dma_start(C[:], cols).then_inc(cols_in, 16)
            act.dma_start(ID[:], ident).then_inc(cols_in, 16)
            act.wait_ge(cols_in, 32)
            cond = C[:, COL_AT["cond"]:COL_AT["cond"] + 16]
            f(cond, cond, ACT.Silu).then_inc(cond_ready, 1)
            norm_start("n1_0")
            for k in range(KC):
                square("n1_0", k, (x_ready, 16))
            norm_root("n1_0")
            for g in range(4):
                if g == 3:
                    split(0)
                    split(1)
                act.wait_ge(m_sum, g + 1)
                f(MR[0:2, g, :], MROWS[g][0:2, :], ACT.Copy).then_inc(m_rows, 1)
            for j in range(2):
                f(SM[:, j:j + 1], col("one"), ACT.Copy).then_inc(tile_out, 1)
            norm_high("n1_0")

            with act.Fori(0, 2) as i:
                for s in range(4):
                    split(s + 2, 4 * i)
                    done(s, 4 * i)
                    f(UVF[:, ds(s * T2 + 4 * T2 * i, T2)], PL[s % 2][:], ACT.Gelu).then_inc(tile_out, 1)
            with act.Fori(0, 3) as i:
                for s in range(4):
                    split(8 + s + 2, 4 * i)
                    conv_in(8 + s, s, 0, COL_AT["bconv"], T2, i, 4)
                    act.wait_ge(conv_done, s + 3 + 4 * i)
                    f(QKVF[:, ds(s * T2 + 4 * T2 * i, T2)], C1[:, s % 2, :], ACT.Silu).then_inc(silu_done, 1)
            act.wait_ge(silu_done, 12)
            def gate_rows():
                done(20)
                act.wait_ge(G["g_rows"], 1)
                f(GA[0:8, :], PL[0][0:8, :], ACT.Identity, bias=C[0:8, COL_AT["dt_bias"]:COL_AT["dt_bias"] + 1])
                link(f(GT[32:40, :], PL[0][32:40, :], ACT.Sigmoid))
                f(SM[:, 2:3], col("one"), ACT.Copy).then_inc(tile_out, 1)
                link(f(GB[0:8, :], GA[0:8, :], ACT.Abs))
                link(f(GB[0:8, :], GB[0:8, :], ACT.Exp, scale=-1.0))
                f(SM[0:8, 4:5], C[0:8, COL_AT["a_log"]:COL_AT["a_log"] + 1], ACT.Exp)
                f(GB[0:8, :], GB[0:8, :], ACT.Ln, bias=C[0:8, COL_AT["one"]:COL_AT["one"] + 1]).then_inc(G["g_in"], 1)

            for t in range(20, 25):
                if t < 24:
                    split(t + 2)
                if t in (20, 21):
                    for j in range(4 * (t - 20), 4 * (t - 20) + 4):
                        if j >= 4:
                            act.wait_ge(G["l2_ss"], j - 3)
                        f(SQL[:, j % 4, :], QKV[:, j, :], ACT.Square).then_inc(G["l2_sq"], 1)
                if t == 20:
                    gate_rows()
                else:
                    done(t)
                    f(GATE[:, t - 21, :], PL[t % 2][:], ACT.Silu).then_inc(tile_out, 1)
                if t == 22:
                    act.wait_ge(G["l2_ss"], 8)
                    f(L2[:, 0, :], BK[0][:, 0:32], ACT.Sqrt, bias=col("eps")).then_inc(G["l2_root"], 1)
            split(26)

            def values(st, k):
                for tl, at in enumerate(TURNS[st]):
                    if k - at in (1, 2):
                        y, d = 2 * st + tl, k - at - 1
                        act.wait_ge(G["gv_t"], y + 1)
                        for h in range(HEADS):
                            last = f(VB[:, 2 * tl + d, h, :], PL[0][:, h * P:(h + 1) * P], ACT.Identity, scale=GTOK[:, y, 32 + 4 * d + h:33 + 4 * d + h])
                        last.then_inc(G["gv_vb"], 1)

            def spatial_gate(k):
                if k in (10, 12):
                    for t in (k - 10, k - 9):
                        act.wait_ge(G["vt_t"], t + 1)
                        f(UV[:, 4:8, t * P:(t + 1) * P], PL[t % 2][:].rearrange("p (a b) -> p a b", a=4), ACT.Copy, accum_out=SM[:, 50 + t:51 + t]).then_inc(G["vt_out"], 1)
                if k in (14, 15):
                    act.wait_ge(G["ln_mean"], 1)
                    for t in (2 * k - 28, 2 * k - 27):
                        if t:
                            act.wait_ge(G["ln_sq"], t)
                        f(STD[:].rearrange("p (a b) -> p a b", a=4), UV[:, 4:8, t * P:(t + 1) * P], ACT.Square, bias=SM[:, 54 + t:55 + t], accum_out=SM[:, 58 + t:59 + t]).then_inc(G["ln_sq"], 1)
                if k == 16:
                    act.wait_ge(G["ln_sq"], 4)
                    f(SM[:, 58:62], SM[:, 58:62], ACT.Sqrt, scale=1.0 / 512, bias=col("eps")).then_inc(G["ln_std"], 1)

            def out_squares(st):
                f(ONQ[:], QKV[:, 8:12, st * SEQ:(st + 1) * SEQ], ACT.Square).then_inc(G["on_sq"], 1)

            def out_root(st):
                act.wait_ge(G["on_ss"], st + 1)
                f(SM[:, 64:72], OUT_BANKS[st][0][:, 0:8], ACT.Sqrt, scale=1.0 / P, bias=col("eps")).then_inc(G["on_root"], 1)

            def first_outputs(k):
                if k == 4:
                    out_squares(0)
                if k == 7:
                    out_root(0)

            act.wait_ge(G["g_cum"], 1)
            f(EG[:], GC[:, :, :, 0:4], ACT.Exp).then_inc(G["g_exp"], 1)
            act.wait_ge(G["g_cum"], 2)
            f(EK[:], EK[:], ACT.Exp).then_inc(G["g_exp"], 1)
            for st in range(2):
                for q in range(4):
                    z = 4 * st + q
                    act.wait_ge(G["gb_r"], z + 1)
                    if z >= 2:
                        act.wait_ge(G["gb_at"], z - 1)
                        act.wait_ge(G["gb_q"], z - 1)
                    f(ER[:, z % 2, :, :], ROWS[q % 2][0][:].rearrange("p (a b) -> p a b", a=HEADS), ACT.Exp).then_inc(G["gb_e"], 1)
                    act.wait_ge(G["gb_d"], z + 1)
                    f(DT[:, z % 2, :, :], DT[:, z % 2, :, :], ACT.Exp).then_inc(G["gb_e"], 1)
                for k in range(4, 24):
                    act.wait_ge(G["lv_m"], 24 * st + k + 1)
                    if k >= 6:
                        act.wait_ge(G["lv_x"], 20 * st + k - 5)
                    f(M1[:, k % 2, :, :], bank(k % 2, 4, P), ACT.Copy).then_inc(G["lv_m1"], 1)
                    values(st, k)
                    (first_outputs if st else spatial_gate)(k)
                for q in range(4):
                    act.wait_ge(G["uw_ready"], 4 * st + q + 1)
                    f(UU[:, q, :, :], bank(2 + 2 * (q % 2), 4, P), ACT.Copy).then_inc(G["u_out"], 1)
            for t in range(4):
                f(HH[:, 0:4, t * P:(t + 1) * P], UV[:, 0:4, t * P:(t + 1) * P], ACT.Copy).then_inc(G["sp_hi"], 1)
            act.wait_ge(G["on_y"], 1)
            f(HH[:, 4:8, CTX], QKV[:, 8:12, CTX], ACT.Copy).then_inc(G["on_hi"], 1)
            for d in range(2):
                act.wait_ge(sc_state[d], 8)
            out_squares(1)
            out_root(1)
            act.wait_ge(G["on_y"], 2)
            f(HH[:, 4:8, LAT], QKV[:, 8:12, LAT], ACT.Copy).then_inc(G["on_hi"], 1)

            residuals("out0", 1, "n2_0")

            def up(layer, ah, width):
                name = f"up{layer}"
                cv, taps = 12 + 2 * FC * layer, COL_AT["fconv"] + 2 * FC * 3 * layer
                ahf = ah[:].rearrange("p a b -> p (a b)")
                def more(s, i):
                    split(B0[name] + s + lead(name), 4 * i)

                def taps_of(s, i):
                    conv_in(T0[name] + s, s, cv, taps, width, i, 4)

                def silu(p, i):
                    act.wait_ge(conv_done, cv + 2 * p + 3 + 4 * i)
                    f(SG[:, 0:width], C1[:, 0, 0:width], ACT.Silu).then_inc(silu_done, 1)

                def high(p, i):
                    act.wait_ge(act_done, FC * layer + p + 1 + 2 * i)
                    f(ahf[:, ds(p * width + 2 * width * i, width)], A32[:, 0:width], ACT.Copy).then_inc(act_hi, 1)

                def step(i, first=False):
                    f(SM[:, 48:49], col("one"), ACT.Silu)
                    taps_of(0, i)
                    if not first:
                        high(-1, i)
                    more(0, i)
                    taps_of(1, i)
                    more(1, i)
                    silu(0, i)
                    act.wait_ge(silu_done, 12 + FC * layer + 1 + 2 * i)
                    taps_of(2, i)
                    high(0, i)
                    more(2, i)
                    more(3, i)
                    taps_of(3, i)
                    silu(1, i)
                    act.wait_ge(silu_done, 12 + FC * layer + 2 + 2 * i)

                step(0, True)
                with act.Fori(1, FC // 2) as i:
                    step(i)
                high(1, FC // 2 - 1)

            def project(name, evac, loops=2):
                with act.Fori(0, loops) as i:
                    for s in range(4):
                        split(B0[name] + s + lead(name), 4 * i)
                        evac(s, i)

            def copy_to(name, flat, width):
                def evac(s, i):
                    done(T0[name] + s, 4 * i)
                    f(flat[:, ds(s * width + 4 * width * i, width)], PL[(T0[name] + s) % 2][:, 0:width], ACT.Copy).then_inc(tile_out, 1)
                return evac

            up(0, AH0, T2)
            residuals("dn0", 3, "n1_1")

            split(B0["in1"] + 2)
            for m, o in enumerate([CQ[:, 0, :], CQ[:, 1, :], CQ[:, 2, :], CKV[:, 0, :], CKV[:, 1, :], KR[:]]):
                split(B0["in1"] + m + lead("in1"))
                done(T0["in1"] + m)
                f(o, PL[(T0["in1"] + m) % 2][:, 0:o.shape[1]], ACT.Copy).then_inc(tile_out, 1)
                if m == 2:
                    norm_start("cq")
                    for k in range(3):
                        square("cq", k, (tile_out, T0["in1"] + k + 3))
                if m == 3:
                    norm_root("cq")
                if m == 4:
                    norm_high("cq")
                    norm_start("ckv")
                    for k in range(2):
                        square("ckv", k, (tile_out, T0["in1"] + k + 6))
            norm_root("ckv")

            def walk(name, place_of, beside=None):
                nb, nt = next((b, t) for s, b, t in STAGES if s == name)
                events = [(DONE_BLOCK[B0[name] + b], 0, b) for b in range(nb)] + [(DONE_TILE[T0[name] + t], 1, t) for t in range(nt)]
                for _, is_tile, j in sorted(events):
                    if is_tile:
                        o = place_of(j)
                        done(T0[name] + j)
                        f(o, PL[(T0[name] + j) % 2][:, 0:o.shape[1]], ACT.Copy).then_inc(tile_out, 1)
                        if beside:
                            beside(j)
                    else:
                        split(B0[name] + j + lead(name))

            def beside_uq(j):
                if j == 4:
                    norm_high("ckv")
                if j == 6:
                    norm_start("mem")
                    for k in range(KC):
                        square("mem", k, (mem_ready, 16))

            walk("uq", lambda m: MQ[:, m, :], beside_uq)
            norm_root("mem")
            walk("ukv_k", lambda m: KN[:, m, :], lambda m: norm_high("mem", (m,)))
            walk("ukv_v", lambda m: VT[:, m % 4, m // 4 * 512:(m // 4 + 1) * 512])

            def attend(ly, out_bank, out_chunks):
                for a in range(ly.steps):
                    w = ly.kt * P
                    if a < ly.n:
                        r = a % 3
                        act.wait_ge(A["at_m"], ly.a0 + a + 1)
                        if ly.a0 + a >= 3:
                            act.wait_ge(A["at_t"], ly.a0 + max(0, a - 2))
                        src = SX[:, a % 2, :] if ly.masked else ly.banks[a % 3][:, 0:w]
                        scale = 1.0 if ly.masked else ly.scale
                        if ly is DIL:
                            f(PB[:, r, 0:w], src, ACT.Exp, scale=scale, bias=SM[:, 20 + r:21 + r]).then_inc(A["at_p"], 1)
                        else:
                            f(PB[:, r, 0:w], src, ACT.Exp, scale=scale, bias=SM[:, 20 + r:21 + r], accum_out=SM[:, 24 + r:25 + r]).then_inc(A["at_p"], 1)
                    if 2 <= a < ly.n + 2:
                        p = a - 2
                        act.wait_ge(A["at_t"], ly.a0 + p + 1)
                        if ly.a0 + p >= 2:
                            act.wait_ge(A["at_o"], ly.a0 + p - 1)
                        f(PT[:, p % 2, 0:ly.kt, :], BK[2 + p % 2][:, 0:w].rearrange("p (k q) -> p k q", k=ly.kt), ACT.Copy).then_inc(A["at_pt"], 1)
                    if ly is DSA and a >= 5 and a % 2 == 1 and (a - 5) // 2 < 8:
                        h = (a - 5) // 2
                        act.wait_ge(A["at_o"], ly.a0 + 2 * h + 2)
                        if h >= 2:
                            act.wait_ge(A["ol_o"], h - 1)
                        f(OL[:, h % 2, :], BK[4 + h % 2][:, 0:SEQ], ACT.Copy).then_inc(A["ol_out"], 1)
                    if a >= ly.lag and (a - ly.lag) % ly.per == 0:
                        e = (a - ly.lag) // ly.per
                        if ly is DSA:
                            act.wait_ge(A["ol_o"], 2 * e + 2)
                        else:
                            act.wait_ge(A["at_o"], ly.a0 + ly.per * (e + 1))
                        f(out_chunks(HH, e), out_bank(e), ACT.Copy).then_inc(A["at_hi"], 1)

            attend(MLA, lambda e: BK[4 + e % 2][:, 0:SEQ], lambda h, e: h[:, e, LAT])
            residuals("out1", 1, "n2_1")
            up(1, AH1, SEQ)
            residuals("dn1", 3, "final1")

            act.wait_ge(n_ss, NORM_I["mix"] + 2)
            for t in range(2):
                last = f(STD[:, t:t + 1], SUMS[t][:, 0:1], ACT.Sqrt, scale=1.0 / D, bias=col("eps"))
            last.then_inc(n_root, 1)
            act.wait_ge(n_std, NORM_I["mix"] + 1)
            f(STD[:, 2:4], STD[:, 16:18], ACT.Sqrt, scale=1.0 / D, bias=col("eps")).then_inc(n_root, 1)
            norm_high("mix")
            project("in2", copy_to("in2", PJF, SEQ), 5)
            for m in (20, 21):
                split(B0["in2"] + m + lead("in2"))
                done(T0["in2"] + m)
                f(PJ[:, m, :], PL[(T0["in2"] + m) % 2][:, 0:SEQ], ACT.Copy).then_inc(tile_out, 1)
            walk("in2_v", lambda m: VBK[:, m, :])
            norm("kv2", lambda k: (tile_out, T0["in2"] + 9))
            for j in range(SIDE):
                if j < 8:
                    split(B0["xk"] + j + lead("xk"))
                    done(T0["xk"] + j)
                    f(KCR[:, j, :], PL[(T0["xk"] + j) % 2][:, 0:SEQ], ACT.Copy).then_inc(tile_out, 1)
                else:
                    split(B0["xv"] + j - 8 + lead("xv"))
                    if j % 4 == 3:
                        for m in (2 * (j // 12), 2 * (j // 12) + 1):
                            t = T0["xv"] + m
                            done(t)
                            f(VC[:, m % 2, m // 2 * 512:(m // 2 + 1) * 512], PL[t % 2][:], ACT.Copy).then_inc(tile_out, 1)
                if j == 2:
                    act.wait_ge(A["ct_t"], 1)
                    f(CTK[:], BK[5][:, 0:SEQ].rearrange("p (k c) -> p k c", k=2), ACT.Copy).then_inc(A["ct_out"], 1)
                if j in INDEX_AT:
                    for c in range(4 * (j - INDEX_AT[0]), 4 * (j - INDEX_AT[0]) + 4):
                        act.wait_ge(A["ix_l"], c + 1)
                        if c >= 2:
                            act.wait_ge(A["ix_a"], c - 1)
                        f(RL[:, c % 2, :], BK[c % 2][:, 0:SEQ], ACT.Relu).then_inc(A["ix_r"], 1)
                if j in LATENT_AT:
                    for h in (2 * (j - LATENT_AT[0]), 2 * (j - LATENT_AT[0]) + 1):
                        act.wait_ge(A["ql_m"], h + 1)
                        f(QL[:, h, :], BK[2 + h % 2][:, 0:SEQ], ACT.Copy).then_inc(A["ql_out"], 1)
            attend(DSA, lambda e: PL[e % 2][:, 0:SEQ], lambda h, e: h[:, e, LAT])
            attend(DIL, lambda e: BK[4 + e % 2][:, 0:SEQ], lambda h, e: h[:, 4 + e, LAT])
            residuals("out2", 1, "cross")
            project("xq", copy_to("xq", QCF, SEQ))
            attend(CRS, lambda e: BK[4 + e % 2][:, 0:512].rearrange("p (c q) -> p c q", c=2), lambda h, e: h[:, 2 * e:2 * e + 2, LAT])
            residuals("xo", 1, "mlp")
            AHF2 = AH2[:].rearrange("p a b -> p (a b)")
            with act.Fori(0, 8) as i:
                for s in range(4):
                    split(B0["up2"] + s + lead("up2"), 4 * i)
                    t = T0["up2"] + s
                    done(t, 4 * i)
                    act.wait_ge(act_lo, 2 * FC + s - 1 + 4 * i)
                    f(C1[:, s % 2, 0:SEQ], PL[t % 2][:, 0:SEQ], ACT.Relu).then_inc(tile_out, 1)
                    act.wait_ge(tile_out, t + 3 + 4 * i)
                    f(AHF2[:, ds(s * SEQ + 4 * SEQ * i, SEQ)], C1[:, s % 2, 0:SEQ], ACT.Square).then_inc(act_hi, 1)

            residuals("dn2", 4, "final2")

        @block.vector
        def _(dve):
            v = nc.vector
            steps = [0]

            def link(ins):
                steps[0] += 1
                ins.then_inc(dve_step, 1)
                dve.wait_ge(dve_step, steps[0])

            def low(n, off=0):
                if n >= NBLK:
                    return
                dve.wait_ge(w_high, n + 1 + off)
                v.tensor_tensor(wl(n), RAW[:, n % 4, :], wh(n), ALU.subtract).then_inc(w_low, 1)

            def modulation(b, first, n, at=0):
                bias = C[:, COL_AT["ada_b"] + first:COL_AT["ada_b"] + first + n].unsqueeze(2).to_broadcast([P, n, 2])
                o = MODF[:, 2 * first:2 * (first + n)].rearrange("p (m s) -> p m s", s=2)
                return v.tensor_tensor(o, BK[b][:, 2 * at:2 * (at + n)].rearrange("p (m s) -> p m s", s=2), bias, ALU.add)

            def gains(layer, which):
                at = COL_AT["norm1" if which == 0 else "norm2"] + KC * layer
                g = C[:, at:at + KC].unsqueeze(2).to_broadcast([P, KC, 2])
                return v.scalar_tensor_tensor(GM[:, layer, which, :, :], MOD[:, layer, 3 * which + 1, :, :], 1.0, g, ALU.add, ALU.mult)

            def norm_factor(name):
                i = NORM_I[name]
                nt = NORMS[i][2] // P
                dve.wait_ge(n_root, i + 1)
                v.reciprocal(STD[:, 8:8 + nt], STD[:, 0:nt]).then_inc(n_std, 1)

            def norm(name):
                i = NORM_I[name]
                _, nch, width = NORMS[i]
                if name != "n1_0":
                    norm_factor(name)
                dve.wait_ge(n_bc, i + 1)
                layer, part = MODULATED.get(name, (0, 0))

                def low_part(k):
                    dve.wait_ge(n_hi, NORM_S0[name] + k + 1)
                    if name in MODULATED:
                        for x, s in streams(name):
                            last = v.scalar_tensor_tensor(norm_dst(name, k, 1)[:, x], TMP[:, k, x], MOD[:, layer, part, k, s:s + 1], norm_dst(name, k, 0)[:, x],
                                                          ALU.add, ALU.subtract)
                    else:
                        last = v.tensor_tensor(norm_dst(name, k, 1), TMP[:, k, 0:width], norm_dst(name, k, 0), ALU.subtract)
                    last.then_inc(n_lo, 1)

                for k in range(nch):
                    src = norm_src(name, k)
                    o = TMP[:, k, 0:width] if name in SPLIT else src
                    if name in MODULATED:
                        for x, s in streams(name):
                            ins = v.scalar_tensor_tensor(o[:, x], src[:, x], GM[:, layer, part // 3, k, s:s + 1], BK[0][:, x], ALU.mult, ALU.mult)
                    else:
                        gain = {"cq": "mla_q", "ckv": "mla_kv"}.get(name, name)
                        ins = v.scalar_tensor_tensor(o, src, col(gain, k), BK[0][:, 0:width], ALU.mult, ALU.mult)
                    ins.then_inc(n_xn, 1)
                    if name in SPLIT and k:
                        low_part(k - 1)
                if name in SPLIT:
                    low_part(nch - 1)

            def two_norms():
                i = NORM_I["mix"]
                gain = SM[:, 64:72]
                v.tensor_tensor(gain, C[:, COL_AT["final1"]:COL_AT["final1"] + KC], C[:, COL_AT["mix"]:COL_AT["mix"] + KC], ALU.mult)
                dve.wait_ge(n_root, i + 1)
                link(v.reciprocal(STD[:, 8:10], STD[:, 0:2]))
                for t in range(2):
                    last = v.scalar_tensor_tensor(STD[:, 16 + t:17 + t], SUMS[t][:, 1:2], STD[:, 8 + t:9 + t], STD[:, 8 + t:9 + t], ALU.mult, ALU.mult)
                last.then_inc(n_std, 1)
                dve.wait_ge(n_root, i + 2)
                link(v.reciprocal(STD[:, 18:20], STD[:, 2:4]))
                v.tensor_tensor(STD[:, 10:12], STD[:, 18:20], STD[:, 8:10], ALU.mult).then_inc(n_std, 1)
                dve.wait_ge(n_bc, i + 2)
                for k in range(KC + 1):
                    if k < KC:
                        v.scalar_tensor_tensor(TMP[:, k, CTX], X[:, k, LAT], gain[:, k:k + 1], BK[0][:, CTX], ALU.mult, ALU.mult).then_inc(n_xn, 1)
                    if k:
                        dve.wait_ge(n_hi, NORM_S0["mix"] + k)
                        v.tensor_tensor(norm_dst("mix", k - 1, 1), TMP[:, k - 1, CTX], norm_dst("mix", k - 1, 0), ALU.subtract).then_inc(n_lo, 1)

            def conv(t, k, cv, taps, width, it=0, per=0):
                n = width // SEQ
                o = C1[:, k % 2, 0:width].rearrange("p (s t) -> p s t", s=n)
                dve.wait_ge(tile_out, t + 3 + per * it)
                v.scalar_tensor_tensor(o, XP[:, k % 2, 0:n, 0:SEQ], C[:, ds(taps + 3 * k + 3 * per * it, 1)], o, ALU.mult, ALU.add).then_inc(conv_mid, 1)
                dve.wait_ge(conv_mid, cv + k + 1 + per * it)
                v.scalar_tensor_tensor(o, XP[:, k % 2, 0:n, 2:SEQ + 2], C[:, ds(taps + 3 * k + 2 + 3 * per * it, 1)], o, ALU.mult, ALU.add).then_inc(conv_done, 1)

            def add(name, m, gate, width, it=0, per=0):
                t = T0[name] + m
                blocks = DONE_TILE[T0[name] + 1] - DONE_TILE[T0[name]]
                dve.wait_ge(pe_done, DONE_TILE[t] + blocks * per * it)
                for x, s in ([(CTX, 0), (LAT, 1)] if width == T2 else [(LAT, 1)]):
                    o = XF[:, ds(m * T2 + x.start + per * T2 * it, SEQ)]
                    y = PL[t % 2][:, x if width == T2 else CTX]
                    if gate is None:
                        last = v.tensor_tensor(o, o, y, ALU.add)
                    else:
                        g = MODF[:, ds((gate * KC + m) * 2 + s + 2 * per * it, 1)]
                        last = v.scalar_tensor_tensor(o, y, g, o, ALU.mult, ALU.add)
                last.then_inc(tile_out, 1)

            norm_factor("n1_0")
            low(0)
            low(1)
            dve.wait_ge(cond_ready, 1)
            dve.wait_ge(a_used, A_FIRST)
            link(modulation(1, 0, A_FIRST))
            gains(0, 0).then_inc(mod_ready, 1)
            dve.wait_ge(mod_ready, 1)
            norm("n1_0")

            def mod_half(j, acc, off=0):
                h, half = j // 2, j % 2
                if half == 0:
                    dve.wait_ge(m_done, h + 1 + off)
                dve.wait_ge(a_landed[half], 16 * (h + 1) + 16 * off)
                o = acc[:, h % 2, 1, :]
                for k in range(4):
                    n = 4 * half + k
                    if k == 3:
                        dve.wait_ge(m_acc[0], PAIR_OPS[0] * h + (2, 5)[half] + PAIR_OPS[0] * off)
                    w, at = AR[:, half, k * 256:(k + 1) * 256], COL_AT["cond"] + 2 * n + 1
                    if n == 0:
                        ins = v.tensor_scalar(o, w, C[:, at:at + 1], None, ALU.mult)
                    else:
                        dve.wait_ge(m_acc[1], KC * h + n + KC * off)
                        ins = v.scalar_tensor_tensor(o, w, C[:, at:at + 1], o, ALU.mult, ALU.add)
                    ins.then_inc(m_acc[1], 1)

            with dve.Fori(0, 2) as i:
                for s in range(4):
                    low(s + 2, 4 * i)
                    mod_half(s, ACC0, 2 * i)
            with dve.Fori(0, 3) as i:
                for s in range(4):
                    low(8 + s + 2, 4 * i)
                    conv(8 + s, s, 0, COL_AT["bconv"], T2, i, 4)
                    mod_half(8 + s, ACC0, 2 * i)
            def over_lengths(some):
                for j in some:
                    dve.wait_ge(G["l2_bc"], j + 1)
                    factor = BK[1 + j % 4][:]
                    if j < 4:
                        ins = v.scalar_tensor_tensor(QKV[:, j, :], QKV[:, j, :], P ** -0.5, factor, ALU.mult, ALU.mult)
                    else:
                        ins = v.tensor_tensor(QKV[:, j, :], QKV[:, j, :], factor, ALU.mult)
                    ins.then_inc(G["l2_done"], 1)

            v.memset(GT[:], 0.0).then_inc(G["g_rows"], 1)
            for t in range(20, 24):
                low(t + 2)
                mod_half(t, ACC0)
                if t == 21:
                    dve.wait_ge(G["g_in"], 1)
                    link(v.scalar_tensor_tensor(GA[0:8, :], GA[0:8, :], 0.0, GB[0:8, :], ALU.max, ALU.add))
                    v.tensor_scalar(GT[0:8, :], GA[0:8, :], SM[0:8, 4:5], -1.0, ALU.mult, ALU.mult).then_inc(G["g_soft"], 1)
                if t == 22:
                    dve.wait_ge(G["l2_root"], 1)
                    v.reciprocal(L2[:, 1, :], L2[:, 0, :]).then_inc(G["l2_std"], 1)
            over_lengths(range(4))
            dve.wait_ge(G["g_tr"], 1)
            v.tensor_copy(GTOK[:], BK[0][:, 0:160].rearrange("p (t r) -> p t r", t=4)).then_inc(G["g_tok"], 1)
            dve.wait_ge(m_done, 2 + PAIRS_IN)
            link(modulation(5, A_FIRST, 2 * PAIRS_IN))
            gains(0, 1).then_inc(mod_ready, 1)
            over_lengths(range(4, 8))
            low(26)

            dve.wait_ge(G["g_cs"], 1)
            v.tensor_copy(GC[:], BK[5][:, 0:64].rearrange("p (t d r) -> p t d r", t=4, d=2)).then_inc(G["g_cum"], 1)
            dve.wait_ge(G["g_cum"], 1)
            v.tensor_tensor(EK[:], GC[:, :, :, 4:8], GC[:, :, :, 0:4], ALU.subtract).then_inc(G["g_cum"], 1)
            dve.wait_ge(G["g_exp"], 1)
            link(v.tensor_tensor(BE[:], EG[:], GTOK[:, :, 32:40].rearrange("p t (d h) -> p t d h", d=2), ALU.mult))
            dve.wait_ge(G["g_exp"], 2)
            dve.wait_ge(gdn_in, 16)

            def keys(st, k):
                for tl, at in enumerate(TURNS[st]):
                    if k - at in (1, 2):
                        y = 2 * st + tl
                        dve.wait_ge(G["gv_t"], y + 1)
                        for d in range(2):
                            o, factor = ((KBG, BE), (KD, EK))[k - at - 1]
                            last = v.tensor_tensor(o[:, 2 * tl + d, :, :], PL[1][:].rearrange("p (a b) -> p a b", a=HEADS),
                                                   factor[:, y, d, :].unsqueeze(2).to_broadcast([P, HEADS, P]), ALU.mult)
                        last.then_inc(G["gv_k"], 1)

            def spatial_gate(k):
                if k == 13:
                    dve.wait_ge(G["vt_out"], 4)
                    v.tensor_scalar(SM[:, 54:58], SM[:, 50:54], -1.0 / 512, None, ALU.mult).then_inc(G["ln_mean"], 1)
                if k == 17:
                    dve.wait_ge(G["ln_std"], 1)
                    v.reciprocal(SM[:, 58:62], SM[:, 58:62]).then_inc(G["ln_r"], 1)
                    dve.wait_ge(G["ln_r"], 1)
                    dve.wait_ge(ws_in, 48)
                if 18 <= k < 22:
                    t = k - 18
                    x = UV[:, 4:8, t * P:(t + 1) * P]
                    v.tensor_scalar(x, x, SM[:, 54 + t:55 + t], SM[:, 58 + t:59 + t], ALU.add, ALU.mult).then_inc(G["ln_n"], 1)
                    dve.wait_ge(G["ln_n"], t + 1)
                    v.tensor_tensor(x, x, LNR[:, 0, :, :], ALU.mult).then_inc(G["ln_g"], 1)
                if k >= 24:
                    t = k - 24
                    x = UV[:, 0:4, t * P:(t + 1) * P]
                    dve.wait_ge(G["sp_s"], t + 1)
                    v.tensor_tensor(x, x, PL[t % 2][:].rearrange("p (a b) -> p a b", a=4), ALU.mult).then_inc(G["sp_y"], 1)

            def out_factor(st):
                dve.wait_ge(G["on_root"], st + 1)
                v.reciprocal(SM[:, 64:72], SM[:, 64:72]).then_inc(G["on_std"], 1)

            def out_norm(st):
                x = slice(st * SEQ, (st + 1) * SEQ)
                dve.wait_ge(G["on_bc"], st + 1)
                for p in range(2):
                    o = QKV[:, 8 + 2 * p:10 + 2 * p, x]
                    v.scalar_tensor_tensor(o, o, col("b_norm"), OUT_BANKS[st][p][:].rearrange("p (a b) -> p a b", a=2), ALU.mult, ALU.mult).then_inc(G["on_n"], 1)
                dve.wait_ge(G["on_n"], 2 * st + 2)
                v.tensor_tensor(QKV[:, 8:12, x], QKV[:, 8:12, x], GATE[:, :, x], ALU.mult).then_inc(G["on_y"], 1)

            def first_outputs(k):
                if k == 8:
                    out_factor(0)
                if k == 10:
                    out_norm(0)

            for st in range(2):
                def decays(q):
                    tl, d, z = q // 2, q % 2, 4 * st + q
                    dve.wait_ge(G["gb_e"], 2 * z + 1)
                    if z >= 2:
                        dve.wait_ge(G["gb_at"], z - 1)
                    for h in range(HEADS):
                        last = v.scalar_tensor_tensor(DT[:, z % 2, h, :], ROWS[q % 2][0][:, h * P:(h + 1) * P], GC[:, 2 * st + tl, d, h:h + 1], gtab("neg", d), ALU.subtract, ALU.add)
                    last.then_inc(G["gb_d"], 1)

                def triangles(q):
                    tl, d, z = q // 2, q % 2, 4 * st + q
                    dt = DT[:, z % 2, :, :]
                    dve.wait_ge(G["gb_e"], 2 * z + 2)
                    dve.wait_ge(G["gb_k"], 2 * st + tl + 1)
                    v.tensor_tensor(ATT[:, q, :, :], bank(3 + 2 * tl, 4, P), dt, ALU.mult)
                    for c in range(2):
                        e = 64 * c + (63 if d == 0 else 0)
                        v.tensor_copy(GEND[:, d, 2 * tl + c, :], ER[:, z % 2, :, e])
                    link(v.tensor_tensor(dt, dt, ROWS[q % 2][1][:].rearrange("p (a b) -> p a b", a=HEADS), ALU.mult))
                    v.tensor_tensor(AT[:, q, :, :], bank(2 + 2 * tl, 4, P), dt, ALU.mult).then_inc(G["gb_at"], 1)

                eye = ID[:].unsqueeze(1).to_broadcast([P, HEADS, P])

                def first_u(q):
                    dve.wait_ge(G["lv_ct"], 24 * st + q + 1)
                    v.tensor_tensor(TU[:, q, :, :], eye, CT[:, q % 2, :, :], ALU.subtract).then_inc(G["lv_u"], 1)

                for q in (0, 2):
                    decays(q)
                    decays(q + 1)
                    triangles(q)
                    triangles(q + 1)
                    if q == 0:
                        first_u(0)
                        first_u(1)
                for k, (lev, q) in enumerate(LEVELS):
                    b = k % 2
                    if lev == 0:
                        if q >= 2:
                            first_u(q)
                        dve.wait_ge(G["lv_m"], 24 * st + k + 1)
                        v.tensor_tensor(TT[:, q, :, :], eye, bank(b, 4, P), ALU.subtract).then_inc(G["lv_tu"], 1)
                    else:
                        dve.wait_ge(G["lv_x"], 20 * st + k - 3)
                        if lev < 5:
                            v.tensor_tensor(TT[:, q, :, :], TT[:, q, :, :], bank(2 + 2 * b, 4, P), ALU.subtract)
                        v.tensor_tensor(TU[:, q, :, :], TU[:, q, :, :], bank(3 + 2 * b, 4, P), ALU.subtract).then_inc(G["lv_tu"], 1)
                    keys(st, k)
                    (first_outputs if st else spatial_gate)(k)
                for q in range(4):
                    dve.wait_ge(G["uw_ready"], 4 * st + q + 1)
                    v.tensor_copy(WT[:, q, :, :], bank(3 + 2 * (q % 2), 4, P)).then_inc(G["w_out"], 1)
                dve.wait_ge(G["u_out"], 4 * st + 4)
                dve.wait_ge(G["s_init"], 1)
                dve.wait_ge(G["ln_v"], 4)
                for k in range(4):
                    n = 4 * st + k
                    for d in range(2):
                        _, q, po = chunk_place(st, k, d)
                        half = slice(po, po + 64)
                        dve.wait_ge(sc_w[d], n + 1)
                        v.tensor_tensor(VN[half, d, :, :], UU[half, q, :, :], bank(d, 4, P)[half], ALU.subtract).then_inc(sc_v[d], 1)
                    for d in range(2):
                        c, _, _ = chunk_place(st, k, d)
                        dve.wait_ge(sc_s[d], n + 1)
                        o = QKV[:, 8:12, st * SEQ + c * 64:st * SEQ + (c + 1) * 64]
                        new = BK[4 + d][:, 0:256].rearrange("p (h t) -> p h t", h=HEADS)
                        if k < 2:
                            last = v.tensor_copy(o, new)
                        else:
                            last = v.tensor_tensor(o, o, new, ALU.add)
                        if st == 0 and d == 0 and k:
                            spatial_gate(24 + k - 1)
                        for h in range(HEADS if n < 7 else 0):
                            last = v.scalar_tensor_tensor(S[:, d, h, :], S[:, d, h, :], GEND[:, d, c, h:h + 1], bank(2 + d, 4, P)[:, h, :], ALU.mult, ALU.add)
                        last.then_inc(sc_state[d], 1)
                if st == 0:
                    spatial_gate(27)
            out_factor(1)
            for t in range(4):
                tok = slice(t * P, (t + 1) * P)
                dve.wait_ge(G["sp_hi"], t + 1)
                v.tensor_tensor(HL[:, 0:4, tok], UV[:, 0:4, tok], HH[:, 0:4, tok], ALU.subtract).then_inc(G["y_a"], 1)
            out_norm(1)
            for st, x in enumerate((CTX, LAT)):
                dve.wait_ge(G["on_hi"], st + 1)
                v.tensor_tensor(HL[:, 4:8, x], QKV[:, 8:12, x], HH[:, 4:8, x], ALU.subtract).then_inc(G["y_b"], 1)

            def project(name, width=None, gate=None, loops=2):
                with dve.Fori(0, loops) as i:
                    for s in range(4):
                        if width:
                            add(name, s, gate, width, i, 4)
                        low(B0[name] + s + lead(name), 4 * i)

            def up(layer, ah, al, width):
                name = f"up{layer}"
                cv, taps = 12 + 2 * FC * layer, COL_AT["fconv"] + 2 * FC * 3 * layer
                ahf, alf = ah[:].rearrange("p a b -> p (a b)"), al[:].rearrange("p a b -> p (a b)")
                def more(s, i):
                    low(B0[name] + s + lead(name), 4 * i)

                def outer_taps(s, i):
                    conv(T0[name] + s, s, cv, taps, width, i, 4)

                def gated(p, i):
                    dve.wait_ge(silu_done, 12 + FC * layer + p + 1 + 2 * i)
                    dve.wait_ge(conv_done, cv + 2 * p + 4 + 4 * i)
                    v.tensor_tensor(A32[:, 0:width], SG[:, 0:width], C1[:, 1, 0:width], ALU.mult).then_inc(act_done, 1)

                def low_part(p, i):
                    dve.wait_ge(act_hi, FC * layer + p + 1 + 2 * i)
                    o = ds(p * width + 2 * width * i, width)
                    v.tensor_tensor(alf[:, o], A32[:, 0:width], ahf[:, o], ALU.subtract).then_inc(act_lo, 1)

                def modulate(s, i):
                    if layer == 0:
                        mod_half(2 * PAIRS_IN + s, ACC1, 2 * i)

                def step(i, first=False):
                    outer_taps(0, i)
                    if not first:
                        low_part(-1, i)
                    more(0, i)
                    modulate(0, i)
                    outer_taps(1, i)
                    more(1, i)
                    gated(0, i)
                    modulate(1, i)
                    outer_taps(2, i)
                    more(2, i)
                    low_part(0, i)
                    modulate(2, i)
                    outer_taps(3, i)
                    gated(1, i)
                    more(3, i)
                    modulate(3, i)

                step(0, True)
                with dve.Fori(1, FC // 2) as i:
                    step(i)
                low_part(1, FC // 2 - 1)

            def down(layer, width):
                name = f"dn{layer}"
                if layer == 0:
                    for m in range(KC):
                        if m == KC - 1:
                            dve.wait_ge(m_done, 2 + PAIRS)
                            link(modulation(1, A_FIRST + 2 * (PAIRS_IN + PAIRS_UP), 2 * (PAIRS - PAIRS_IN - PAIRS_UP)))
                            gains(1, 0)
                            gains(1, 1).then_inc(mod_ready, 1)
                        low(B0[name] + 3 * m + lead(name))
                        low(B0[name] + 3 * m + 1 + lead(name))
                        add(name, m, 5, width)
                        low(B0[name] + 3 * m + 2 + lead(name))
                        for j in range(2 * (PAIRS_IN + FC + m), 2 * (PAIRS_IN + FC + m) + 2):
                            if j < 2 * PAIRS:
                                mod_half(j, ACC1)
                    return
                with dve.Fori(0, 2) as i:
                    for m in range(4):
                        for k in range(3):
                            low(B0[name] + 3 * m + k + lead(name), 12 * i)
                        add(name, m, 11, width, i, 4)

            def rest(name, first=0, last=None):
                for b in range(first, last or next(n for s, n, _ in STAGES if s == name)):
                    low(B0[name] + b + lead(name))

            project("out0", T2, 2)
            norm("n2_0")
            up(0, AH0, AL0, T2)
            dve.wait_ge(m_done, 2 + PAIRS_IN + PAIRS_UP)
            link(modulation(5, A_FIRST + 2 * PAIRS_IN, 2 * PAIRS_UP))
            down(0, T2)
            dve.wait_ge(mod_ready, 3)

            norm("n1_1")
            low(B0["in1"] + 2)
            rest("in1", 0, 4)
            norm("cq")
            rest("in1", 4)
            norm("ckv")
            rest("uq")
            norm("mem")
            rest("ukv_k")

            def rotate(tiles, r0, some):
                for i in some:
                    x, _, which = tiles[i]
                    cos, sin = ("cm", "sm") if which == "m" else ("c" + which, "s" + which)
                    dve.wait_ge(A["rp_m"], r0 + i + 1)
                    v.tensor_tensor(RT[:, i % 2, :], BK[2 + i % 2][:, 0:SEQ], ltab(sin), ALU.mult)
                    link(v.tensor_tensor(x, x, ltab(cos), ALU.mult))
                    v.tensor_tensor(x, x, RT[:, i % 2, :], ALU.add).then_inc(A["rp_d"], 1)

            dve.wait_ge(late_in, 16)
            dve.wait_ge(n_lo, NORM_S0["mem"] + KC)
            rotate(ROPE1, 0, range(len(ROPE1)))
            rest("ukv_v")

            def attend(ly, out_bank, out_chunks, mask=None):
                for a in range(ly.steps):
                    w = ly.kt * P
                    if a < ly.n:
                        r = a % 3
                        src = ly.banks[a % len(ly.banks)][:, 0:w]
                        dve.wait_ge(A["at_s"], ly.a0 + a + 1)
                        if ly.masked:
                            link(v.scalar_tensor_tensor(SX[:, a % 2, :], src, ly.scale, mask(a % 2), ALU.mult, ALU.add))
                            src = SX[:, a % 2, :]
                        link(v.tensor_reduce(SM[:, 16 + r:17 + r], src, AX.X, ALU.max))
                        v.tensor_scalar(SM[:, 20 + r:21 + r], SM[:, 16 + r:17 + r], -1.0 if ly.masked else -ly.scale, None, ALU.mult).then_inc(A["at_m"], 1)
                    if 1 <= a <= ly.n:
                        p = a - 1
                        r = p % 3
                        dve.wait_ge(A["at_p"], ly.a0 + p + 1)
                        if ly is DIL:
                            link(v.scalar_tensor_tensor(PB[:, r, 0:w], PB[:, r, 0:w], 1.0, ltab("dcnt", p % 2), ALU.mult, ALU.mult, accum_out=SM[:, 24 + r:25 + r]))
                        link(v.reciprocal(SM[:, 28 + r:29 + r], SM[:, 24 + r:25 + r]))
                        v.tensor_scalar(PB[:, r, 0:w], PB[:, r, 0:w], SM[:, 28 + r:29 + r], None, ALU.mult).then_inc(A["at_n"], 1)
                    if a >= ly.lag and (a - ly.lag) % ly.per == 0:
                        e = (a - ly.lag) // ly.per
                        dve.wait_ge(A["at_hi"], ly.e0 + e + 1)
                        v.tensor_tensor(out_chunks(HL, e), out_bank(e), out_chunks(HH, e), ALU.subtract).then_inc(A["at_y"], 1)

            attend(MLA, lambda e: BK[4 + e % 2][:, 0:SEQ], lambda h, e: h[:, e, LAT])
            project("out1", SEQ, 8)
            norm("n2_1")
            up(1, AH1, AL1, SEQ)
            down(1, SEQ)
            two_norms()

            project("in2", loops=5)
            for k in range(KC):
                x = X[:, k, LAT]
                v.scalar_tensor_tensor(x, x, col("final1", k), BK[0][:, LAT], ALU.mult, ALU.mult).then_inc(n_xn, 1)
            low(B0["in2"] + 20 + lead("in2"))
            low(B0["in2"] + 21 + lead("in2"))
            rest("in2_v")
            norm("kv2")
            causal = LTAB[:, LATE_AT["causal"]:LATE_AT["causal"] + 2 * SEQ].rearrange("p (t k) -> p t k", t=2)
            for j in range(SIDE):
                low((B0["xk"] + j if j < 8 else B0["xv"] + j - 8) + lead("xk"))
                rotate(ROPE2, len(ROPE1), ROTATE_AT[j])
                if j == 2:
                    dve.wait_ge(A["we_t"], 1)
                    v.tensor_scalar(WE[:], BK[4][:, 0:16].rearrange("p (t h) -> p t h", t=2), 8 ** -0.5 * 64 ** -0.5, None, ALU.mult).then_inc(A["we_ready"], 1)
                    dve.wait_ge(A["we_ready"], 1)
                if j in INDEX_AT:
                    for c in range(4 * (j - INDEX_AT[0]), 4 * (j - INDEX_AT[0]) + 4):
                        qt, h = c // 8, c % 8
                        dve.wait_ge(A["ix_r"], c + 1)
                        if c:
                            dve.wait_ge(A["ix_a"], c)
                        if h == 0:
                            ins = v.tensor_scalar(IX[:, qt, :], RL[:, c % 2, :], WE[:, qt, h:h + 1], None, ALU.mult)
                        else:
                            ins = v.scalar_tensor_tensor(IX[:, qt, :], RL[:, c % 2, :], WE[:, qt, h:h + 1], IX[:, qt, :], ALU.mult, ALU.add)
                        ins.then_inc(A["ix_a"], 1)
                if j == TOP_AT[0]:
                    dve.wait_ge(A["ix_a"], 16)
                    link(v.tensor_tensor(IX[:], IX[:], causal, ALU.add))
                if j in TOP_AT:
                    v.max(M8[:, 0, :], IX[:, 0, :])
                    link(v.max(M8[:, 1, :], IX[:, 1, :]))
                    v.match_replace(IX[:, 0, :], M8[:, 0, :], IX[:, 0, :], TAKEN)
                    link(v.match_replace(IX[:, 1, :], M8[:, 1, :], IX[:, 1, :], TAKEN))
            link(v.tensor_scalar(AM[:], IX[:], -2e38, NEG, ALU.is_gt, ALU.mult))
            link(v.tensor_tensor(AM[:], AM[:], causal, ALU.add))
            attend(DSA, lambda e: PL[e % 2][:, 0:SEQ], lambda h, e: h[:, e, LAT], lambda qt: AM[:, qt, :])
            attend(DIL, lambda e: BK[4 + e % 2][:, 0:SEQ], lambda h, e: h[:, 4 + e, LAT], lambda qt: ltab("dneg", qt))
            project("out2", SEQ)
            norm("cross")
            project("xq")
            attend(CRS, lambda e: BK[4 + e % 2][:, 0:512].rearrange("p (c q) -> p c q", c=2), lambda h, e: h[:, 2 * e:2 * e + 2, LAT])
            project("xo", SEQ)
            norm("mlp")
            ahf, alf = AH2[:].rearrange("p a b -> p (a b)"), AL2[:].rearrange("p a b -> p (a b)")
            with dve.Fori(0, 8) as i:
                for s in range(4):
                    low(B0["up2"] + s + lead("up2"), 4 * i)
                    dve.wait_ge(tile_out, T0["up2"] + s + 3 + 4 * i)
                    half = slice(s % 2 * SEQ, (s % 2 + 1) * SEQ)
                    v.tensor_tensor(A32[:, half], C1[:, s % 2, 0:SEQ], C1[:, s % 2, 0:SEQ], ALU.mult).then_inc(act_done, 1)
                    dve.wait_ge(act_done, 2 * FC + s + 1 + 4 * i)
                    dve.wait_ge(act_hi, 2 * FC + s + 1 + 4 * i)
                    o = ds(s * SEQ + 4 * SEQ * i, SEQ)
                    v.tensor_tensor(alf[:, o], A32[:, half], ahf[:, o], ALU.subtract).then_inc(act_lo, 1)

            with dve.Fori(0, 3) as i:
                for m in range(2):
                    for k in range(4):
                        low(B0["dn2"] + 4 * m + k + lead("dn2"), 8 * i)
                    add("dn2", m, None, SEQ, i, 2)
            for m in (6, 7):
                for k in range(4):
                    low(B0["dn2"] + 4 * m + k + lead("dn2"))
                add("dn2", m, None, SEQ)
            norm("final2")


def kernel(**inputs):
    import numpy as np
    import concourse.bacc as bacc
    from concourse.bass_utils import run_bass_kernel_spmd

    arrays = {k: np.ascontiguousarray(v) for k, v in lay_out({k: np.asarray(v) for k, v in inputs.items()}).items()}
    nc = bacc.Bacc("TRN2", target_bir_lowering=False, num_devices=1)
    args = [nc.dram_tensor(k, v.shape, mybir.dt.float32, kind="ExternalInput").ap() for k, v in arrays.items()]
    out = nc.dram_tensor("out", (P, KC, SEQ), mybir.dt.float32, kind="ExternalOutput").ap()
    two_blocks_kernel(nc, *args, out)
    r = run_bass_kernel_spmd(nc, [arrays], core_ids=[0])
    y = r.results[0]["out"]
    return np.ascontiguousarray(y.transpose(2, 1, 0).reshape(1, SEQ, D))
```
